# Optimizing a Trainium2 kernel written in Bass

```python
import jax, jax.numpy as jnp
from jax import lax
import numpy as np

D_MODEL = 1024
BATCH = 1
SEQ = 1024
DEPTH = 1

CHUNK = 64
N_MEM = 256
HEAD_DIM = D_MODEL // 16
A_HEADS = 8
B_HEADS = 4
C_HEADS = 4
A_WIDTH = A_HEADS * HEAD_DIM
B_WIDTH = B_HEADS * HEAD_DIM
C_WIDTH = C_HEADS * HEAD_DIM
MIX_WIDTH = A_WIDTH + B_WIDTH + C_WIDTH
IN_COLS = 3 * A_WIDTH + 4 * B_WIDTH + C_WIDTH
LEFT_CHUNKS = 8
BAND_CHUNKS = LEFT_CHUNKS + 1
MAX_REL_DIST = 128
REL_TABLE = MAX_REL_DIST + CHUNK
ROPE_BASE = 10000.0
N_GROUPS = 4
EXPERTS_PER_GROUP = 8
N_EXPERTS = N_GROUPS * EXPERTS_PER_GROUP
TOP_K = 2
D_EXPERT = D_MODEL // 2
ROW_BLOCK = 256
EPS = 1e-6
NEG_INF = -1e30

kernel_name = "hybrid_chunk_attn_retention_memxattn_hiermoe"

def rms_norm(x, g):
    xf = x.astype(jnp.float32)
    y = xf * lax.rsqrt(jnp.mean(xf * xf, axis=-1, keepdims=True) + EPS)
    return (y * g.astype(jnp.float32)).astype(x.dtype)

def split_heads(t, n_heads):
    b, s, _ = t.shape
    return t.reshape(b, s, n_heads, -1).transpose(0, 2, 1, 3)

def merge_heads(t):
    b, h, s, d = t.shape
    return t.transpose(0, 2, 1, 3).reshape(b, s, h * d)

def chunked_relpos_attention(q, k, v, rel_bias):
    b, h, s, dh = q.shape
    nc = s // CHUNK
    qc = q.reshape(b, h, nc, CHUNK, dh)
    pad = ((0, 0), (0, 0), (LEFT_CHUNKS * CHUNK, 0), (0, 0))
    kp = jnp.pad(k, pad).reshape(b, h, nc + LEFT_CHUNKS, CHUNK, dh)
    vp = jnp.pad(v, pad).reshape(b, h, nc + LEFT_CHUNKS, CHUNK, dh)
    band_idx = jnp.arange(nc)[:, None] + jnp.arange(BAND_CHUNKS)[None, :]
    kb = kp[:, :, band_idx].reshape(b, h, nc, BAND_CHUNKS * CHUNK, dh)
    vb = vp[:, :, band_idx].reshape(b, h, nc, BAND_CHUNKS * CHUNK, dh)
    scores = jnp.einsum('bhcqd,bhckd->bhcqk', qc, kb).astype(jnp.float32) * (dh ** -0.5)
    qpos = LEFT_CHUNKS * CHUNK + jnp.arange(CHUNK)
    kpos = jnp.arange(BAND_CHUNKS * CHUNK)
    rel = jnp.clip(qpos[:, None] - kpos[None, :], -(CHUNK - 1), MAX_REL_DIST) + (CHUNK - 1)
    bias = rel_bias[:, rel].astype(jnp.float32)
    valid = jnp.repeat(band_idx >= LEFT_CHUNKS, CHUNK, axis=1)
    scores = scores + bias[None, :, None]
    scores = jnp.where(valid[None, None, :, None, :], scores, NEG_INF)
    probs = jax.nn.softmax(scores, axis=-1).astype(v.dtype)
    out = jnp.einsum('bhcqk,bhckd->bhcqd', probs, vb)
    return out.reshape(b, h, s, dh)

def rotary(t, positions):
    half = t.shape[-1] // 2
    inv = ROPE_BASE ** (-jnp.arange(half, dtype=jnp.float32) / half)
    ang = positions.astype(jnp.float32)[:, None, :, None] * inv
    cos, sin = jnp.cos(ang), jnp.sin(ang)
    t1, t2 = t[..., :half], t[..., half:]
    return jnp.concatenate([t1 * cos - t2 * sin, t1 * sin + t2 * cos], axis=-1)

def chunkwise_retention(q, k, v):
    b, h, s, dh = q.shape
    nc = s // CHUNK
    log_g = jnp.log(1.0 - jnp.exp2(-5.0 - jnp.arange(h, dtype=jnp.float32)))
    idx = jnp.arange(CHUNK, dtype=jnp.float32)
    diff = idx[:, None] - idx[None, :]
    decay = jnp.where(diff >= 0, jnp.exp(log_g[:, None, None] * jnp.maximum(diff, 0.0)), 0.0)
    qc = q.reshape(b, h, nc, CHUNK, dh)
    kc = k.reshape(b, h, nc, CHUNK, dh)
    vc = v.reshape(b, h, nc, CHUNK, dh)
    inner = jnp.einsum('bhcqd,bhckd->bhcqk', qc, kc) * decay[None, :, None]
    inner_out = jnp.einsum('bhcqk,bhckd->bhcqd', inner, vc)
    zeta = jnp.exp(log_g[:, None] * (CHUNK - 1 - idx))
    kv = jnp.einsum('bhckd,hk,bhcke->bhcde', kc, zeta, vc)
    chunk_decay = jnp.exp(log_g * CHUNK)[None, :, None, None]

    def step(state, kv_c):
        return chunk_decay * state + kv_c, state

    _, states_prev = lax.scan(step, jnp.zeros((b, h, dh, dh), jnp.float32), jnp.moveaxis(kv, 2, 0))
    states_prev = jnp.moveaxis(states_prev, 0, 2)
    xi = jnp.exp(log_g[:, None] * (idx + 1.0))
    cross = jnp.einsum('bhcqd,bhcde->bhcqe', qc, states_prev) * xi[None, :, None, :, None]
    return (inner_out + cross).reshape(b, h, s, dh)

def head_group_norm(o, g):
    mu = jnp.mean(o, axis=-1, keepdims=True)
    var = jnp.mean(jnp.square(o - mu), axis=-1, keepdims=True)
    y = (o - mu) * lax.rsqrt(var + EPS)
    return merge_heads(y) * g.astype(jnp.float32)

def memory_cross_attention(q, mem_n, w_mem_kv, qn_c, kn_c):
    kv = mem_n @ w_mem_kv
    k, v = jnp.split(kv, 2, axis=-1)
    qh = rms_norm(split_heads(q, C_HEADS), qn_c)
    kh = rms_norm(split_heads(k, C_HEADS), kn_c)
    vh = split_heads(v, C_HEADS)
    scores = jnp.einsum('bhsd,bhmd->bhsm', qh, kh).astype(jnp.float32) * (HEAD_DIM ** -0.5)
    probs = jax.nn.softmax(scores, axis=-1).astype(vh.dtype)
    return merge_heads(jnp.einsum('bhsm,bhmd->bhsd', probs, vh))

def hierarchical_moe(hf, w_router_group, b_router_group, w_router_expert, b_router_expert,
                     w_gate, w_up, w_down):
    t, d = hf.shape
    g_prob = jax.nn.softmax((hf @ w_router_group + b_router_group).astype(jnp.float32), axis=-1)
    g_sel = jnp.argmax(g_prob, axis=-1)
    p_group = jnp.take_along_axis(g_prob, g_sel[:, None], axis=-1)[:, 0]
    e_logits = (hf @ w_router_expert + b_router_expert).astype(jnp.float32)
    e_logits = e_logits.reshape(t, N_GROUPS, EXPERTS_PER_GROUP)
    e_in_group = jnp.take_along_axis(e_logits, g_sel[:, None, None], axis=1)[:, 0]
    e_prob = jax.nn.softmax(e_in_group, axis=-1)
    top_p, top_i = lax.top_k(e_prob, TOP_K)
    top_p = top_p / jnp.sum(top_p, axis=-1, keepdims=True)
    weights = p_group[:, None] * top_p
    expert_id = g_sel[:, None] * EXPERTS_PER_GROUP + top_i

    n_assign = t * TOP_K
    flat_e = expert_id.reshape(-1).astype(jnp.int32)
    flat_t = jnp.repeat(jnp.arange(t, dtype=jnp.int32), TOP_K)
    flat_w = weights.reshape(-1)
    order = jnp.argsort(flat_e)
    e_s, t_s, w_s = flat_e[order], flat_t[order], flat_w[order]
    counts = jnp.bincount(flat_e, length=N_EXPERTS)
    starts = jnp.cumsum(counts) - counts
    padded = (counts + ROW_BLOCK - 1) // ROW_BLOCK * ROW_BLOCK
    pends = jnp.cumsum(padded)
    pstarts = pends - padded
    dest = pstarts[e_s] + (jnp.arange(n_assign) - starts[e_s])
    n_blocks = -(-n_assign // ROW_BLOCK) + N_EXPERTS
    n_rows = n_blocks * ROW_BLOCK
    row_tok = jnp.zeros((n_rows,), jnp.int32).at[dest].set(t_s)
    row_w = jnp.zeros((n_rows,), hf.dtype).at[dest].set(w_s.astype(hf.dtype))
    block_e = jnp.minimum(jnp.searchsorted(pends, jnp.arange(n_blocks) * ROW_BLOCK, side='right'),
                          N_EXPERTS - 1)
    xs = hf[row_tok].reshape(n_blocks, ROW_BLOCK, d)

    def expert_block(args):
        xb, e = args
        return (jax.nn.silu(xb @ w_gate[e]) * (xb @ w_up[e])) @ w_down[e]

    ys = lax.map(expert_block, (xs, block_e)).reshape(n_rows, d)
    return jnp.zeros((t, d), hf.dtype).at[row_tok].add(ys * row_w[:, None])

def setup_inputs(seed: int = 0) -> dict:
    key = jax.random.key(seed)
    ks = jax.random.split(key, 24)
    f32 = jnp.float32
    nrm = lambda k, shape, scale: jax.random.normal(k, shape, f32) * scale
    gain = lambda k, shape: 1.0 + 0.02 * jax.random.normal(k, shape, f32)
    return {
        "x": nrm(ks[0], (BATCH, SEQ, D_MODEL), 1.0),
        "mem": nrm(ks[1], (BATCH, N_MEM, D_MODEL), 1.0),
        "positions": jnp.broadcast_to(jnp.arange(SEQ, dtype=jnp.int32), (BATCH, SEQ)),
        "mix_norm_g": gain(ks[2], (D_MODEL,)),
        "w_in": nrm(ks[3], (D_MODEL, IN_COLS), D_MODEL ** -0.5),
        "qn_a": gain(ks[4], (HEAD_DIM,)),
        "kn_a": gain(ks[5], (HEAD_DIM,)),
        "rel_bias": nrm(ks[6], (A_HEADS, REL_TABLE), 0.2),
        "ret_gn_g": gain(ks[7], (B_WIDTH,)),
        "mem_norm_g": gain(ks[8], (D_MODEL,)),
        "w_mem_kv": nrm(ks[9], (D_MODEL, 2 * C_WIDTH), D_MODEL ** -0.5),
        "qn_c": gain(ks[10], (HEAD_DIM,)),
        "kn_c": gain(ks[11], (HEAD_DIM,)),
        "w_out": nrm(ks[12], (MIX_WIDTH, D_MODEL), MIX_WIDTH ** -0.5),
        "ffn_norm_g": gain(ks[13], (D_MODEL,)),
        "w_router_group": nrm(ks[14], (D_MODEL, N_GROUPS), D_MODEL ** -0.5),
        "b_router_group": nrm(ks[15], (N_GROUPS,), 0.01),
        "w_router_expert": nrm(ks[16], (D_MODEL, N_EXPERTS), D_MODEL ** -0.5),
        "b_router_expert": nrm(ks[17], (N_EXPERTS,), 0.01),
        "w_gate": nrm(ks[18], (N_EXPERTS, D_MODEL, D_EXPERT), D_MODEL ** -0.5),
        "w_up": nrm(ks[19], (N_EXPERTS, D_MODEL, D_EXPERT), D_MODEL ** -0.5),
        "w_down": nrm(ks[20], (N_EXPERTS, D_EXPERT, D_MODEL), D_EXPERT ** -0.5),
    }

def reference(x, mem, positions, mix_norm_g, w_in, qn_a, kn_a, rel_bias, ret_gn_g, mem_norm_g,
              w_mem_kv, qn_c, kn_c, w_out, ffn_norm_g, w_router_group, b_router_group,
              w_router_expert, b_router_expert, w_gate, w_up, w_down):
    b, s, d = x.shape
    splits = [int(v) for v in np.cumsum([A_WIDTH, A_WIDTH, A_WIDTH, B_WIDTH, B_WIDTH, B_WIDTH, B_WIDTH])]
    mem_n = rms_norm(mem, mem_norm_g)
    h = x
    for _ in range(DEPTH):
        xn = rms_norm(h, mix_norm_g)
        proj = xn @ w_in
        qa, ka, va, qb, kb, vb, gb, qc = jnp.split(proj, splits, axis=-1)
        qah = rms_norm(split_heads(qa, A_HEADS), qn_a)
        kah = rms_norm(split_heads(ka, A_HEADS), kn_a)
        out_a = merge_heads(chunked_relpos_attention(qah, kah, split_heads(va, A_HEADS), rel_bias))
        qbh = rotary(split_heads(qb, B_HEADS).astype(jnp.float32), positions)
        kbh = rotary(split_heads(kb, B_HEADS).astype(jnp.float32), positions) * (HEAD_DIM ** -0.5)
        vbh = split_heads(vb, B_HEADS).astype(jnp.float32)
        ret = head_group_norm(chunkwise_retention(qbh, kbh, vbh), ret_gn_g)
        out_b = (jax.nn.silu(gb.astype(jnp.float32)) * ret).astype(h.dtype)
        out_c = memory_cross_attention(qc, mem_n, w_mem_kv, qn_c, kn_c)
        h = h + jnp.concatenate([out_a, out_b, out_c], axis=-1) @ w_out
        hn = rms_norm(h, ffn_norm_g).reshape(b * s, d)
        h = h + hierarchical_moe(hn, w_router_group, b_router_group, w_router_expert,
                                 b_router_expert, w_gate, w_up, w_down).reshape(b, s, d)
    return h


_drawn_inputs = setup_inputs


def setup_inputs(seed=0):
    import zlib

    import numpy as np

    out = dict(_drawn_inputs(seed))
    spreads = {}
    factors = {'qn_a': 16.684,
     'kn_a': 16.821,
     'ret_gn_g': 22.168,
     'mem_norm_g': 8.0,
     'qn_c': 4.93,
     'kn_c': 8.0,
     'b_router_group': 64.0,
     'b_router_expert': 28.136,
     'rel_bias': 8.0,
     'ffn_norm_g': 7.167}
    for name, (base, spread) in spreads.items():
        noise = np.random.default_rng([zlib.crc32(name.encode()), seed]).standard_normal(out[name].shape)
        drawn = base * np.exp(spread * noise) if base else spread * noise
        out[name] = __import__('jax').numpy.asarray(drawn.astype(out[name].dtype))
    for name, factor in factors.items():
        out[name] = (out[name] * factor).astype(out[name].dtype)
    return out
```

```python
from contextlib import ExitStack

import numpy as np

import concourse.bass as bass
from concourse import mybir

F32 = mybir.dt.float32
F32R = mybir.dt.float32r
I32 = mybir.dt.int32
U32 = mybir.dt.uint32
BF16 = mybir.dt.bfloat16
ALU = mybir.AluOpType
ACT = mybir.ActivationFunctionType
AX = mybir.AxisListType

P = 128
D = 1024
SEQ = 1024
NT = SEQ // P
KD = D // P
HD = 64
AH, BH, CH = 8, 4, 4
AW, BW, CW = AH * HD, BH * HD, CH * HD
COLS = 3 * AW + 4 * BW + CW
BC0 = 3 * AW
BCW = COLS - BC0
N_MEM = 256
MT = N_MEM // P
CHUNK = 64
LEFT = 8
WIN = (LEFT * CHUNK) // P + 1
KEEP = WIN + 1
MAX_REL = 128
REL = MAX_REL + CHUNK
EXT = 2 * P + P - 1
NG, EG = 4, 8
NE = NG * EG
DE = D // 2
EPS = 1e-6
NEG = -1e30


class Steps:

    def __init__(self, eng, sem, base=0):
        self.eng, self.sem, self.base, self.n = eng, sem, base, 0

    def __call__(self, ins):
        self.n += 1
        ins.then_inc(self.sem, 1)
        self.eng.wait_ge(self.sem, self.base + self.n)


class Core:

    def __init__(self, nc, ctx):
        self.nc, self.ctx = nc, ctx

        self.sems = []

    def sem(self, name):
        self.sems.append(self.nc.alloc_semaphore(name=name))
        return self.sems[-1]

    def reuse_sems(self):
        self.nc.clear_and_free_semaphores(self.sems)
        self.nc.all_engine_barrier()
        self.sems = []

    def psum(self, name, banks=1):
        return self.ctx.enter_context(self.nc.psum_tensor(name, [P, 512 * banks], F32))


def sbuf(nc, stack, name, shape, dt=F32):
    return stack.enter_context(nc.sbuf_tensor(name, shape, dt))


def rows(ap, k):
    return ap.rearrange("(p k) n -> p k n", k=k)


def split_weights(c, name, src, gain, hi, lo, k_tiles, width):
    nc = c.nc
    with ExitStack() as st:
        SLOTS = 4
        raw = sbuf(nc, st, f"{name}_raw", [P, SLOTS, width])
        loaded = [c.sem(f"{name}_loaded{i}") for i in range(SLOTS)]
        gained = c.sem(f"{name}_gained")
        hi_done, lo_done = c.sem(f"{name}_hi"), c.sem(f"{name}_lo")
        g = None
        if gain is not None:
            g = sbuf(nc, st, f"{name}_g", [P, k_tiles])
        block = st.enter_context(nc.Block())

        @block.sync
        def _(sp):
            if g is not None:
                sp.dma_start(g[:], gain.rearrange("(p k) -> p k", k=k_tiles)).then_inc(gained, 16)
            for k in range(k_tiles):
                if k >= SLOTS:
                    sp.wait_ge(lo_done, k - SLOTS + 1)
                sp.dma_start(raw[:, k % SLOTS, :], src[:, k, :]).then_inc(loaded[k % SLOTS], 16)

        @block.scalar
        def _(act):
            if g is not None:
                act.wait_ge(gained, 16)
            for k in range(k_tiles):
                act.wait_ge(loaded[k % SLOTS], 16 * (k // SLOTS + 1))
                act.activation(hi[:, k, :], raw[:, k % SLOTS, :], ACT.Copy,
                               scale=1.0 if g is None else g[:, k:k + 1]).then_inc(hi_done, 1)

        @block.vector
        def _(dve):
            for k in range(k_tiles):
                dve.wait_ge(hi_done, k + 1)
                if g is None:
                    dve.tensor_tensor(lo[:, k, :], raw[:, k % SLOTS, :], hi[:, k, :].bitcast(F32),
                                      ALU.subtract).then_inc(lo_done, 1)
                else:
                    dve.scalar_tensor_tensor(lo[:, k, :], raw[:, k % SLOTS, :], g[:, k:k + 1],
                                             hi[:, k, :].bitcast(F32), ALU.mult,
                                             ALU.subtract).then_inc(lo_done, 1)


def product(pe, out, a, b, first=True, last=True):
    (ah, al), (bh, bl) = a, b
    pe.matmul(out, ah, bh, start=first, stop=False, skip_group_check=True)
    pe.matmul(out, ah, bl, start=False, stop=False, skip_group_check=True)
    return pe.matmul(out, al, bh, start=False, stop=last, skip_group_check=True)


def phase_a(c, d):
    nc = c.nc
    with ExitStack() as st:
        Wh = sbuf(nc, st, "a_wh", [P, KD, 3 * AW], F32R)
        Wl = sbuf(nc, st, "a_wl", [P, KD, 3 * AW], F32R)
        split_weights(c, "a_w", rows(d["w_in"], KD)[:, :, 0:3 * AW], d["mix_norm_g"], Wh, Wl, KD, 3 * AW)
        NP = AH // 2
        kTh = sbuf(nc, st, "a_kth", [P, NP, KEEP, P], F32R)
        kTl = sbuf(nc, st, "a_ktl", [P, NP, KEEP, P], F32R)
        Vh = sbuf(nc, st, "a_vh", [P, KEEP, AW], F32R)
        Vl = sbuf(nc, st, "a_vl", [P, KEEP, AW], F32R)
        bias = sbuf(nc, st, "a_bias", [P, AH, 2 * P])
        ext = sbuf(nc, st, "a_ext", [AH, EXT])
        rev = sbuf(nc, st, "a_rev", [AH, REL])
        xb = sbuf(nc, st, "a_x", [P, 2, D])
        xTh = sbuf(nc, st, "a_xth", [P, KD, P], F32R)
        xTl = sbuf(nc, st, "a_xtl", [P, KD, P], F32R)
        qTh = sbuf(nc, st, "a_qth", [P, 2, NP, P], F32R)
        qTl = sbuf(nc, st, "a_qtl", [P, 2, NP, P], F32R)
        qk = sbuf(nc, st, "a_qk", [P, 2, AW])
        qkn = sbuf(nc, st, "a_qkn", [P, 2, AW])
        sq = sbuf(nc, st, "a_sq", [P, AW])
        junk = sbuf(nc, st, "a_junk", [P, D], BF16)
        Pr = sbuf(nc, st, "a_p", [P, 2, WIN * P])
        PTh = sbuf(nc, st, "a_pth", [P, WIN * P], F32R)
        PTl = sbuf(nc, st, "a_ptl", [P, WIN * P], F32R)
        ident = sbuf(nc, st, "a_ident", [P, P])
        gq = sbuf(nc, st, "a_gq", [P, 1])
        gk = sbuf(nc, st, "a_gk", [P, 1])
        gq8 = sbuf(nc, st, "a_gq8", [P, 1])
        mhalf = sbuf(nc, st, "a_mhalf", [P, AH])
        ssx = sbuf(nc, st, "a_ssx", [P, NT])
        msx = sbuf(nc, st, "a_msx", [P, 2])
        rx = sbuf(nc, st, "a_rx", [P, NT])
        ssh = sbuf(nc, st, "a_ssh", [P, 2, AH])
        msh = sbuf(nc, st, "a_msh", [P, 2, AH])
        rh = sbuf(nc, st, "a_rh", [P, 2, AH])
        nmax = sbuf(nc, st, "a_nmax", [P, 2])
        rs = sbuf(nc, st, "a_rs", [P, 2, AH])
        rinv = sbuf(nc, st, "a_rinv", [P, AH])
        mixt = sbuf(nc, st, "a_mix", [P, 2, AW])

        S = [c.bank2[0], c.bank2[1]]
        PT = c.bank2[2]
        O, PJ = c.bank[0], c.bank[1]

        const_in, rev_in, ext_out, bias_in = (c.sem(f"a_{n}") for n in ("const_in", "rev_in", "ext_out", "bias_in"))
        x_in = [c.sem(f"a_x_in{i}") for i in range(2)]
        mix_out = [c.sem(f"a_mix_out{i}") for i in range(2)]
        pool_const, ext_set, bias_ready, gq8_set = (c.sem(f"a_{n}") for n in ("pool_const", "ext_set", "bias_ready", "gq8_set"))
        ssx_done, msx_done, rx_done = (c.sem(f"a_{n}") for n in ("ssx_done", "msx_done", "rx_done"))
        pj_done = c.sem("a_pj_done")
        pj_hi = c.sem("a_pj_hi")
        pj_free = c.sem("a_pj_free")
        sq_done, ssh_done, msh_done, rh_done, qkn_done = (
            c.sem(f"a_{n}") for n in ("sq_done", "ssh_done", "msh_done", "rh_done", "qkn_done"))
        s_done, biased, max_done, exp_done, pt_done, pth_done, ptl_done, pv_done = (
            c.sem(f"a_{n}") for n in ("s_done", "biased", "max_done", "exp_done", "pt_done", "pth_done", "ptl_done", "pv_done"))
        rinv_done, mix_done = c.sem("a_rinv_done"), c.sem("a_mix_done")
        block = st.enter_context(nc.Block())

        FILLS = 7
        XT0, XT1, Q, K, V, QT, KT = range(FILLS)

        def nblk(t):
            return min(t, WIN - 1) + 1

        def slot_fills(h):
            return [[XT0, XT1], [Q], [K], [V], [QT], [KT], [], []][h]

        def store(sp, t):
            sp.wait_ge(mix_done, t + 1)
            sp.dma_start(d["mix"][t * P:(t + 1) * P, 0:AW], mixt[:, t % 2, :]).then_inc(mix_out[t % 2], 16)

        @block.sync
        def _(sp):
            sp.dma_start(xb[:, 0, :], d["x"][0:P, :]).then_inc(x_in[0], 16)
            sp.dma_start(ident[:], d["ident"]).then_inc(const_in, 16)
            for half in range(2):
                sp.dma_start(gq[64 * half:64 * half + 64, :], d["qn_a"].rearrange("(p a) -> p a", a=1)).then_inc(const_in, 16)
                sp.dma_start(gk[64 * half:64 * half + 64, :], d["kn_a"].rearrange("(p a) -> p a", a=1)).then_inc(const_in, 16)
            sp.dma_start(rev[:], d["rel_bias"]).then_inc(rev_in, 16)
            sp.wait_ge(ext_set, 1)
            sp.dma_start(d["ext_dram"], ext[:]).then_inc(ext_out, 16)
            sp.wait_ge(ext_out, 16)
            toeplitz = bass.AP(d["ext_dram"].tensor, 0, [[1, P], [EXT, AH], [1, 2 * P]])
            sp.dma_start(bias[:], toeplitz).then_inc(bias_in, 16)
            for t in range(1, NT):
                if t >= 2:
                    sp.wait_ge(ssx_done, t - 1)
                    sp.wait_ge(pj_done, FILLS * (t - 2) + XT1 + 1)
                sp.dma_start(xb[:, t % 2, :], d["x"][t * P:(t + 1) * P, :]).then_inc(x_in[t % 2], 16)
                if t >= 2:
                    store(sp, t - 2)
            store(sp, NT - 2)
            store(sp, NT - 1)
            for i in range(2):
                sp.wait_ge(mix_out[i], 16 * (NT // 2))

        @block.gpsimd
        def _(pool):
            pool.memset(mhalf[:], -0.5).then_inc(pool_const, 1)
            pool.wait_ge(pool_const, 1)

            def x_scale(t):
                pool.wait_ge(ssx_done, t + 1)
                pool.tensor_scalar(msx[:, 0:1], ssx[:, t:t + 1], 1.0 / D, EPS, ALU.mult, ALU.add).then_inc(msx_done, 1)
                pool.wait_ge(msx_done, t + 1)
                pool.tensor_tensor(rx[:, t:t + 1], msx[:, 0:1], mhalf[:, 0:1], ALU.pow).then_inc(rx_done, 1)

            def head_scale(t, i):
                n = 2 * t + i + 1
                pool.wait_ge(pj_hi, FILLS * t + Q + i + 1)
                if n >= 2:
                    pool.wait_ge(ssh_done, n - 1)
                pool.tensor_tensor(sq[:], qk[:, i, :], qk[:, i, :], ALU.mult).then_inc(sq_done, 1)
                pool.wait_ge(ssh_done, n)
                pool.tensor_scalar(msh[:, i, :], ssh[:, i, :], 1.0 / HD, EPS, ALU.mult, ALU.add).then_inc(msh_done, 1)
                pool.wait_ge(msh_done, n)
                pool.tensor_tensor(rh[:, i, :], msh[:, i, :], mhalf[:], ALU.pow).then_inc(rh_done, 1)

            for t in range(NT):
                x_scale(t)
                head_scale(t, 0)
                head_scale(t, 1)

        @block.scalar
        def _(act):
            def sum_squares(t):
                act.wait_ge(x_in[t % 2], 16 * (t // 2 + 1))
                act.activation(junk[:], xb[:, t % 2, :], ACT.Square, accum_out=ssx[:, t:t + 1]).then_inc(ssx_done, 1)

            def take(t, f):
                act.wait_ge(pj_done, FILLS * t + f + 1)
                slot = t % KEEP
                if f in (XT0, XT1):
                    i = act.activation(xTh[:, 4 * f:4 * f + 4, :], PJ[:].rearrange("p (k n) -> p k n", n=P), ACT.Copy)
                elif f in (Q, K):
                    act.wait_ge(rx_done, t + 1)
                    i = act.activation(qk[:, f - Q, :], PJ[:], ACT.Copy, scale=rx[:, t:t + 1])
                elif f == V:
                    i = act.activation(Vh[:, slot, :], PJ[:], ACT.Copy, scale=rx[:, t:t + 1])
                elif f == QT:
                    i = act.activation(qTh[:, t % 2], PJ[:].rearrange("p (k n) -> p k n", n=P), ACT.Copy, scale=gq8[:])
                else:
                    i = act.activation(kTh[:, :, slot, :], PJ[:].rearrange("p (k n) -> p k n", n=P), ACT.Copy, scale=gk[:])
                i.then_inc(pj_hi, 1)

            def exps(n):
                t, h = divmod(n, AH)
                w = nblk(t) * P
                act.wait_ge(max_done, n + 1)
                if n >= 2:
                    act.wait_ge(pt_done, n - 1)
                act.activation(Pr[:, n % 2, 0:w], S[n % 2][:, 640 - w:640], ACT.Exp, bias=nmax[:, n % 2:n % 2 + 1],
                               accum_out=rs[:, t % 2, h:h + 1]).then_inc(exp_done, 1)

            def turn_hi(n):
                w = nblk(n // AH) * P
                act.wait_ge(pt_done, n + 1)
                act.activation(PTh[:, 0:w], PT[:, 0:w], ACT.Copy).then_inc(pth_done, 1)

            act.wait_ge(const_in, 80)
            act.wait_ge(gq8_set, 1)
            sum_squares(0)
            for f in range(FILLS):
                take(0, f)
            exps(0)
            for t in range(NT):
                for h in range(AH):
                    n = t * AH + h
                    if h == 0 and t + 1 < NT:
                        sum_squares(t + 1)
                    turn_hi(n)
                    for f in slot_fills(h):
                        if t + 1 < NT:
                            take(t + 1, f)
                    if n + 1 < NT * AH:
                        exps(n + 1)

        @block.tensor
        def _(pe):
            def fill(t, f):
                n = FILLS * t + f
                if n:
                    pe.wait_ge(pj_free, n)
                if f in (XT0, XT1):
                    pe.wait_ge(x_in[t % 2], 16 * (t // 2 + 1))
                    xs = xb[:, t % 2, :].rearrange("p (m k) -> p k m", k=KD)
                    for j in range(4):
                        mm = pe.transpose(PJ[:, j * P:(j + 1) * P], xs[:, 4 * f + j, :], ident[:])
                elif f in (Q, K, V):
                    cols = slice((f - Q) * AW, (f - Q + 1) * AW)
                    for k in range(KD):
                        mm = product(pe, PJ[:], (xTh[:, k, :], xTl[:, k, :]), (Wh[:, k, cols], Wl[:, k, cols]),
                                     k == 0, k == KD - 1)
                else:
                    pe.wait_ge(qkn_done, 2 * t + f - QT + 1)
                    for p in range(NP):
                        mm = pe.transpose(PJ[:, p * P:(p + 1) * P], qkn[:, f - QT, p * P:(p + 1) * P], ident[:])
                mm.then_inc(pj_done, 1)

            def blocks(t):
                first = t - nblk(t) + 1
                return [(kt, kt % KEEP, 640 - (t + 1 - kt) * P, (kt - first) * P) for kt in range(first, t + 1)]

            def scores(n):
                t, h = divmod(n, AH)
                p, r = h // 2, slice(64 * (h % 2), 64 * (h % 2) + 64)
                if h == 0:
                    pe.wait_ge(pj_free, FILLS * t + KT + 1)
                if n >= 2:
                    pe.wait_ge(exp_done, n - 1)
                bl = blocks(t)
                for i, (kt, slot, at, _) in enumerate(bl):
                    mm = product(pe, S[n % 2][:, at:at + P], (qTh[r, t % 2, p, :], qTl[r, t % 2, p, :]),
                                 (kTh[r, p, slot, :], kTl[r, p, slot, :]), i == 0 or kt == t)
                mm.then_inc(s_done, 1)

            def turn(n):
                t = n // AH
                pe.wait_ge(exp_done, n + 1)
                if n >= 1:
                    pe.wait_ge(ptl_done, n)
                for _, _, _, at in blocks(t):
                    mm = pe.transpose(PT[:, at:at + P], Pr[:, n % 2, at:at + P], ident[:])
                mm.then_inc(pt_done, 1)

            def values(n):
                t, h = divmod(n, AH)
                pe.wait_ge(ptl_done, n + 1)
                if h == 0 and t >= 1:
                    pe.wait_ge(mix_done, t)
                bl = blocks(t)
                cols = slice(h * HD, (h + 1) * HD)
                for i, (_, slot, _, at) in enumerate(bl):
                    mm = product(pe, O[:, cols], (PTh[:, at:at + P], PTl[:, at:at + P]),
                                 (Vh[:, slot, cols], Vl[:, slot, cols]), i == 0, i == len(bl) - 1)
                mm.then_inc(pv_done, 1)

            pe.wait_ge(const_in, 80)
            for f in range(FILLS):
                fill(0, f)
            scores(0)
            for t in range(NT):
                for h in range(AH):
                    n = t * AH + h
                    if n + 1 < NT * AH and h < AH - 1:
                        scores(n + 1)
                    turn(n)
                    for f in slot_fills(h):
                        if t + 1 < NT:
                            fill(t + 1, f)
                    values(n)
                    if n + 1 < NT * AH and h == AH - 1:
                        scores(n + 1)

        @block.vector
        def _(dve):
            own = Steps(dve, c.sem("a_dve"))

            def take(t, f):
                n = FILLS * t + f
                slot = t % KEEP
                dve.wait_ge(pj_hi, n + 1)
                PJ3 = PJ[:].rearrange("p (k n) -> p k n", n=P)
                if f in (XT0, XT1):
                    dve.tensor_tensor(xTl[:, 4 * f:4 * f + 4, :], PJ3, xTh[:, 4 * f:4 * f + 4, :].bitcast(F32),
                                      ALU.subtract).then_inc(pj_free, 1)
                elif f in (Q, K):
                    dve.sem_inc(pj_free, 1)
                    i, m = f - Q, 2 * t + f - Q
                    dve.wait_ge(sq_done, m + 1)
                    dve.tensor_reduce(ssh[:, i, :], sq[:].rearrange("p (h e) -> p h e", e=HD), AX.X, ALU.add).then_inc(ssh_done, 1)
                    dve.wait_ge(rh_done, m + 1)
                    dve.tensor_tensor(qkn[:, i, :].rearrange("p (h e) -> p h e", e=HD),
                                      qk[:, i, :].rearrange("p (h e) -> p h e", e=HD),
                                      rh[:, i, :].unsqueeze(2).to_broadcast([P, AH, HD]), ALU.mult).then_inc(qkn_done, 1)
                elif f == V:
                    dve.scalar_tensor_tensor(Vl[:, slot, :], PJ[:], rx[:, t:t + 1], Vh[:, slot, :].bitcast(F32),
                                             ALU.mult, ALU.subtract).then_inc(pj_free, 1)
                elif f == QT:
                    dve.scalar_tensor_tensor(qTl[:, t % 2], PJ3, gq8[:], qTh[:, t % 2].bitcast(F32),
                                             ALU.mult, ALU.subtract).then_inc(pj_free, 1)
                else:
                    dve.scalar_tensor_tensor(kTl[:, :, slot, :], PJ3, gk[:], kTh[:, :, slot, :].bitcast(F32),
                                             ALU.mult, ALU.subtract).then_inc(pj_free, 1)

            def maxes(n):
                t, h = divmod(n, AH)
                w = nblk(t) * P
                s = S[n % 2]
                dve.wait_ge(s_done, n + 1)
                if t == 0:
                    ins = dve.tensor_tensor(s[:, 512:640], s[:, 512:640], bias[:, h, P - 1::-1], ALU.add)
                else:
                    ins = dve.tensor_tensor(s[:, 384:640], s[:, 384:640], bias[:, h, ::-1], ALU.add)
                if nblk(t) == WIN:
                    ins = dve.tensor_scalar(s[64:128, 0:64], s[64:128, 0:64], NEG, None, ALU.add)
                ins.then_inc(biased, 1)
                dve.wait_ge(biased, n + 1)
                dve.tensor_reduce(nmax[:, n % 2:n % 2 + 1], s[:, 640 - w:640], AX.X, ALU.max, negate=True).then_inc(max_done, 1)

            def turn_lo(n):
                w = nblk(n // AH) * P
                dve.wait_ge(pth_done, n + 1)
                dve.tensor_tensor(PTl[:, 0:w], PT[:, 0:w], PTh[:, 0:w].bitcast(F32), ALU.subtract).then_inc(ptl_done, 1)

            def finish(t):
                dve.wait_ge(exp_done, AH * (t + 1))
                dve.reciprocal(rinv[:], rs[:, t % 2, :]).then_inc(rinv_done, 1)
                dve.wait_ge(rinv_done, t + 1)
                dve.wait_ge(pv_done, AH * (t + 1))
                if t >= 2:
                    dve.wait_ge(mix_out[t % 2], 16 * (t // 2))
                dve.tensor_tensor(mixt[:, t % 2, :].rearrange("p (h e) -> p h e", e=HD),
                                  O[:].rearrange("p (h e) -> p h e", e=HD),
                                  rinv[:].unsqueeze(2).to_broadcast([P, AH, HD]), ALU.mult).then_inc(mix_done, 1)

            dve.wait_ge(const_in, 80)
            dve.tensor_scalar(gq8[:], gq[:], HD ** -0.5, None, ALU.mult).then_inc(gq8_set, 1)
            dve.wait_ge(rev_in, 16)
            dve.memset(ext[:, 0:CHUNK], NEG)
            dve.memset(ext[:, CHUNK + REL:EXT], 0.0)
            dve.tensor_scalar(ext[:, CHUNK:CHUNK + REL], rev[:], rev[:, REL - 1:REL], None, ALU.subtract).then_inc(ext_set, 1)
            dve.wait_ge(bias_in, 16)
            own(dve.memset(bias[0:64, :, 0:64], NEG))
            dve.wait_ge(gq8_set, 1)
            for f in range(FILLS):
                take(0, f)
            maxes(0)
            for t in range(NT):
                for h in range(AH):
                    n = t * AH + h
                    if n + 1 < NT * AH and h < AH - 1:
                        maxes(n + 1)
                    turn_lo(n)
                    for f in slot_fills(h):
                        if t + 1 < NT:
                            take(t + 1, f)
                    if h == AH - 1:
                        finish(t)
                    if n + 1 < NT * AH and h == AH - 1:
                        maxes(n + 1)


class Filled:

    def __init__(self, c, name, fills, by_dve, by_act=None):
        self.fills, self.by_dve = fills, by_dve
        self.by_act = list(range(fills)) if by_act is None else by_act
        self.full, self.hi, self.lo = c.sem(f"{name}_full"), c.sem(f"{name}_hi"), c.sem(f"{name}_lo")

    def wait_full(self, eng, t, f):
        eng.wait_ge(self.full, self.fills * t + f + 1)

    def wait_hi(self, eng, t, f):
        eng.wait_ge(self.hi, len(self.by_act) * t + self.by_act.index(f) + 1)

    def wait_free(self, eng, t, f):
        if f in self.by_dve:
            eng.wait_ge(self.lo, len(self.by_dve) * t + self.by_dve.index(f) + 1)
        else:
            self.wait_hi(eng, t, f)

    def wait_before(self, eng, t, f, first):
        if f:
            self.wait_free(eng, t, f - 1)
        elif not first:
            self.wait_free(eng, t - 1, self.fills - 1)


def wait_apart(eng, sem, value, passed):
    eng.wait_ge(sem, value)
    eng.sem_inc(passed, 1)


def heads(ap):
    return ap.rearrange("p (h e) -> p h e", e=HD)


def tiles(ap):
    return ap.rearrange("p (k n) -> p k n", n=P)


def wide(ap, n):
    return ap.unsqueeze(2).to_broadcast([ap.shape[0], ap.shape[1], n])


TWO_PI = 2 * np.pi
TURN1 = 6.28125
TURN2 = float(np.float32(round((TWO_PI - TURN1) * 2 ** 21) / 2 ** 21))
TURN3 = float(np.float32(TWO_PI - TURN1 - TURN2))
ROUND = 1.5 * 2 ** 23
PI_BELOW = 3.1415925


def phase_m(c, d, kTh, kTl, Vh, Vl, cos, sin):
    nc = c.nc
    with ExitStack() as st:
        Wh = sbuf(nc, st, "m_wh", [P, KD, 2 * CW], F32R)
        Wl = sbuf(nc, st, "m_wl", [P, KD, 2 * CW], F32R)
        split_weights(c, "m_w", rows(d["w_mem_kv"], KD), d["mem_norm_g"], Wh, Wl, KD, 2 * CW)
        mb = sbuf(nc, st, "m_mem", [P, MT, D])
        mTh = sbuf(nc, st, "m_mth", [P, KD, P], F32R)
        mTl = sbuf(nc, st, "m_mtl", [P, KD, P], F32R)
        km = sbuf(nc, st, "m_k", [P, MT, CW])
        kn = sbuf(nc, st, "m_kn", [P, MT, CW])
        sq = sbuf(nc, st, "m_sq", [P, CW])
        junk = sbuf(nc, st, "m_junk", [P, D], BF16)
        ident = sbuf(nc, st, "m_ident", [P, P])
        gk = sbuf(nc, st, "m_gk", [P, 1])
        mhalf = sbuf(nc, st, "m_mhalf", [P, CH])
        ss = sbuf(nc, st, "m_ss", [P, MT])
        ms = sbuf(nc, st, "m_ms", [P, MT])
        r = sbuf(nc, st, "m_r", [P, MT])
        ssh = sbuf(nc, st, "m_ssh", [P, MT, CH])
        msh = sbuf(nc, st, "m_msh", [P, MT, CH])
        rh = sbuf(nc, st, "m_rh", [P, MT, CH])
        pos = sbuf(nc, st, "m_pos", [P, NT], I32)
        posf = sbuf(nc, st, "m_posf", [P, NT])
        inv = sbuf(nc, st, "m_inv", [P, HD // 2])
        ang = sbuf(nc, st, "m_ang", [P, NT, HD // 2])
        turns = sbuf(nc, st, "m_turns", [P, 2, NT, HD // 2])
        rest = sbuf(nc, st, "m_rest", [P, 2, NT, HD // 2])
        PJ = c.bank[1]
        XT0, XT1, KV, KT = range(4)
        pj = Filled(c, "m_pj", 4, [XT0, XT1, KV, KT])
        const_in, mem_in = c.sem("m_const_in"), [c.sem(f"m_mem_in{i}") for i in range(MT)]
        pool_own, ss_done, r_done, sq_done, ssh_done, rh_done, kn_done = (
            c.sem(f"m_{n}") for n in ("pool", "ss_done", "r_done", "sq_done", "ssh_done", "rh_done", "kn_done"))
        angles, sines = c.sem("m_angles"), c.sem("m_sines")
        CONSTS = 16 * 5
        block = st.enter_context(nc.Block())

        @block.sync
        def _(sp):
            for m in range(MT):
                sp.dma_start(mb[:, m, :], d["mem"][m * P:(m + 1) * P, :]).then_inc(mem_in[m], 16)
            sp.dma_start(ident[:], d["ident"]).then_inc(const_in, 16)
            for half in range(2):
                sp.dma_start(gk[64 * half:64 * half + 64, :], d["kn_c"].rearrange("(p a) -> p a", a=1)).then_inc(const_in, 16)
            sp.dma_start(pos[:], d["positions"]).then_inc(const_in, 16)
            sp.dma_start(inv[:], d["inv_freq"].partition_broadcast(P)).then_inc(const_in, 16)

        @block.gpsimd
        def _(pool):
            own = Steps(pool, pool_own)
            own(pool.memset(mhalf[:], -0.5))
            for m in range(MT):
                pool.wait_ge(ss_done, m + 1)
                own(pool.tensor_scalar(ms[:, m:m + 1], ss[:, m:m + 1], 1.0 / D, EPS, ALU.mult, ALU.add))
                pool.tensor_tensor(r[:, m:m + 1], ms[:, m:m + 1], mhalf[:, 0:1], ALU.pow).then_inc(r_done, 1)
            for m in range(MT):
                pj.wait_hi(pool, m, KV)
                pool.tensor_tensor(sq[:], km[:, m, :], km[:, m, :], ALU.mult).then_inc(sq_done, 1)
                pool.wait_ge(ssh_done, m + 1)
                own(pool.tensor_scalar(msh[:, m, :], ssh[:, m, :], 1.0 / HD, EPS, ALU.mult, ALU.add))
                pool.tensor_tensor(rh[:, m, :], msh[:, m, :], mhalf[:], ALU.pow).then_inc(rh_done, 1)

        @block.scalar
        def _(act):
            for m in range(MT):
                act.wait_ge(mem_in[m], 16)
                if m:
                    act.wait_ge(ss_done, m)
                act.activation(junk[:], mb[:, m, :], ACT.Square, accum_out=ss[:, m:m + 1]).then_inc(ss_done, 1)
            act.wait_ge(const_in, CONSTS)
            for m in range(MT):
                for f in (XT0, XT1):
                    pj.wait_full(act, m, f)
                    act.activation(mTh[:, 4 * f:4 * f + 4, :], tiles(PJ[:]), ACT.Copy).then_inc(pj.hi, 1)
                act.wait_ge(r_done, m + 1)
                pj.wait_full(act, m, KV)
                act.activation(km[:, m, :], PJ[:, 0:CW], ACT.Copy, scale=r[:, m:m + 1])
                act.activation(Vh[:, m, :], PJ[:, CW:2 * CW], ACT.Copy, scale=r[:, m:m + 1]).then_inc(pj.hi, 1)
                pj.wait_full(act, m, KT)
                act.activation(kTh[:, :, m * P:(m + 1) * P], tiles(PJ[:, 0:CW]), ACT.Copy, scale=gk[:]).then_inc(pj.hi, 1)
            act.wait_ge(angles, 1)
            act.activation(sin[:], rest[:, 0], ACT.Sin).then_inc(sines, 1)
            act.activation(cos[:], rest[:, 1], ACT.Sin).then_inc(sines, 1)

        @block.tensor
        def _(pe):
            pe.wait_ge(const_in, CONSTS)
            for m in range(MT):
                pe.wait_ge(mem_in[m], 16)
                xs = mb[:, m, :].rearrange("p (m k) -> p k m", k=KD)
                for f in (XT0, XT1):
                    pj.wait_before(pe, m, f, m == 0)
                    for j in range(4):
                        mm = pe.transpose(PJ[:, j * P:(j + 1) * P], xs[:, 4 * f + j, :], ident[:])
                    mm.then_inc(pj.full, 1)
                pj.wait_before(pe, m, KV, False)
                for k in range(KD):
                    mm = product(pe, PJ[:], (mTh[:, k, :], mTl[:, k, :]), (Wh[:, k, :], Wl[:, k, :]), k == 0, k == KD - 1)
                mm.then_inc(pj.full, 1)
                pj.wait_before(pe, m, KT, False)
                pe.wait_ge(kn_done, m + 1)
                for p in range(CH // 2):
                    mm = pe.transpose(PJ[:, p * P:(p + 1) * P], kn[:, m, p * P:(p + 1) * P], ident[:])
                mm.then_inc(pj.full, 1)

        @block.vector
        def _(dve):
            own = Steps(dve, c.sem("m_dve"))
            dve.wait_ge(const_in, CONSTS)
            own(dve.tensor_copy(posf[:], pos[:]))
            own(dve.tensor_tensor(ang[:], wide(posf[:], HD // 2), inv[:].unsqueeze(1).to_broadcast([P, NT, HD // 2]), ALU.mult))
            for i, quarter in enumerate((0.0, 0.25)):
                own(dve.tensor_scalar(turns[:, i], ang[:], 1 / TWO_PI, quarter, ALU.mult, ALU.add))
                own(dve.tensor_scalar(turns[:, i], turns[:, i], ROUND, None, ALU.add))
                own(dve.tensor_scalar(turns[:, i], turns[:, i], -ROUND, None, ALU.add))
                own(dve.scalar_tensor_tensor(rest[:, i], turns[:, i], -TURN1, ang[:], ALU.mult, ALU.add))
                own(dve.scalar_tensor_tensor(rest[:, i], turns[:, i], -TURN2, rest[:, i], ALU.mult, ALU.add))
                own(dve.scalar_tensor_tensor(rest[:, i], turns[:, i], -TURN3, rest[:, i], ALU.mult, ALU.add))
                own(dve.tensor_scalar(rest[:, i], rest[:, i], quarter * TWO_PI, PI_BELOW, ALU.add, ALU.min))
                own(dve.tensor_scalar(rest[:, i], rest[:, i], -PI_BELOW, None, ALU.max))
            dve.sem_inc(angles, 1)
            for m in range(MT):
                for f in (XT0, XT1):
                    pj.wait_hi(dve, m, f)
                    dve.tensor_tensor(mTl[:, 4 * f:4 * f + 4, :], tiles(PJ[:]), mTh[:, 4 * f:4 * f + 4, :].bitcast(F32),
                                      ALU.subtract).then_inc(pj.lo, 1)
                pj.wait_hi(dve, m, KV)
                dve.scalar_tensor_tensor(Vl[:, m, :], PJ[:, CW:2 * CW], r[:, m:m + 1], Vh[:, m, :].bitcast(F32),
                                         ALU.mult, ALU.subtract).then_inc(pj.lo, 1)
                dve.wait_ge(sq_done, m + 1)
                dve.tensor_reduce(ssh[:, m, :], heads(sq[:]), AX.X, ALU.add).then_inc(ssh_done, 1)
                dve.wait_ge(rh_done, m + 1)
                dve.tensor_tensor(heads(kn[:, m, :]), heads(km[:, m, :]), wide(rh[:, m, :], HD), ALU.mult).then_inc(kn_done, 1)
                pj.wait_hi(dve, m, KT)
                dve.scalar_tensor_tensor(kTl[:, :, m * P:(m + 1) * P], tiles(PJ[:, 0:CW]), gk[:],
                                         kTh[:, :, m * P:(m + 1) * P].bitcast(F32), ALU.mult, ALU.subtract).then_inc(pj.lo, 1)


def phase_bc(c, d):
    nc = c.nc
    with ExitStack() as st:
        kTCh = sbuf(nc, st, "c_kth", [P, CH // 2, N_MEM], F32R)
        kTCl = sbuf(nc, st, "c_ktl", [P, CH // 2, N_MEM], F32R)
        VCh = sbuf(nc, st, "c_vh", [P, MT, CW], F32R)
        VCl = sbuf(nc, st, "c_vl", [P, MT, CW], F32R)
        cos = sbuf(nc, st, "b_cos", [P, NT, HD // 2])
        sin = sbuf(nc, st, "b_sin", [P, NT, HD // 2])
        phase_m(c, d, kTCh, kTCl, VCh, VCl, cos, sin)
        Wh = sbuf(nc, st, "b_wh", [P, KD, BCW], F32R)
        Wl = sbuf(nc, st, "b_wl", [P, KD, BCW], F32R)
        split_weights(c, "b_w", rows(d["w_in"], KD)[:, :, BC0:COLS], d["mix_norm_g"], Wh, Wl, KD, BCW)
        t_ = lambda name, shape, dt=F32: sbuf(nc, st, "b_" + name, shape, dt)
        xb = t_("x", [P, D])
        xTh, xTl = t_("xth", [P, KD, P], F32R), t_("xtl", [P, KD, P], F32R)
        junk = t_("junk", [P, D], BF16)
        ident, tri = t_("ident", [P, P]), t_("tri", [P, P])
        dec, g128 = t_("dec", [P, 2 * BH]), t_("g128", [P, BH // 2])
        gng = t_("gng", [P, BW])
        gqc, gqc8 = t_("gqc", [P, 1]), t_("gqc8", [P, 1])
        mhalf = t_("mhalf", [P, CH])
        ssx, msx, rx = t_("ssx", [P, 1]), t_("msx", [P, 1]), t_("rx", [P, 1])
        qk = t_("qk", [P, 2 * BW])
        byc, bys = t_("byc", [P, 2 * BW]), t_("bys", [P, 2 * BW])
        rot, qkr = t_("rot", [P, 2 * BW]), t_("qkr", [P, 2 * BW])
        kh, kl = t_("kh", [P, BW], F32R), t_("kl", [P, BW], F32R)
        vh, vl = t_("vh", [P, BW], F32R), t_("vl", [P, BW], F32R)
        g, eg, sg = t_("g", [P, BW]), t_("eg", [P, BW]), t_("sg", [P, BW])
        qkTh, qkTl = t_("qkth", [P, BH, P], F32R), t_("qktl", [P, BH, P], F32R)
        Sm = t_("sm", [P, BH, P])
        Smh, Sml = t_("smh", [P, BH, P], F32R), t_("sml", [P, BH, P], F32R)
        R, Rt = t_("r", [P, BH // 2, HD]), t_("rt", [P, BH // 2, HD])
        Rh, Rl = t_("rh", [P, BH // 2, HD], F32R), t_("rl", [P, BH // 2, HD], F32R)
        qc, qcn, sqc = t_("qc", [P, CW]), t_("qcn", [P, CW]), t_("sqc", [P, CW])
        ssc, msc, rc = t_("ssc", [P, CH]), t_("msc", [P, CH]), t_("rc", [P, CH])
        qTCh, qTCl = t_("qtch", [P, CH // 2, P], F32R), t_("qtcl", [P, CH // 2, P], F32R)
        nmax, rs, rinv = t_("nmax", [P, CH]), t_("rs", [P, CH]), t_("rinv", [P, CH])
        Pr = t_("p", [P, CH, N_MEM])
        PTh, PTl = t_("pth", [P, CH * N_MEM], F32R), t_("ptl", [P, CH * N_MEM], F32R)
        sm4, mean, ss4, ms4, r4 = (t_(n, [P, BH]) for n in ("sm4", "mean", "ss4", "ms4", "r4"))
        cent, csq, y, yg = (t_(n, [P, BW]) for n in ("cent", "csq", "y", "yg"))
        mixt = t_("mix", [P, BW + CW])

        SC, PT, O = c.bank2[0], c.bank2[1], c.bank2[2]
        SB = PT
        TR, PJ = c.bank[0], c.bank[1]

        def place(h, width, base=0):
            at = (h % 2) * 512 + base + (h // 2) * width
            return slice(at, at + width)

        def by_head(ap, width, base=0):
            return ap.rearrange("p (s c) -> p s c", s=2)[:, :, base:base + 2 * width].rearrange("p s (a e) -> p s a e", a=2)

        def halves(ap):
            return ap.rearrange("p (a s e) -> p s a e", s=2, a=2)

        def halves1(ap):
            return ap.rearrange("p (a s) -> p s a", s=2)

        XT0, XT1, QK, VG, QC = range(5)
        pj = Filled(c, "b_pj", 5, [XT0, XT1, VG])
        QKT, QCT, U = range(3)
        tr = Filled(c, "b_tr", 3, [QKT, QCT, U], [QKT, QCT])
        s_ = lambda name: c.sem("b_" + name)
        const_in, x_in, mix_out, consts_set, state0 = map(s_, ("const_in", "x_in", "mix_out", "consts_set", "state0"))
        ssx_done, rx_done, pool_own, dve_own = map(s_, ("ssx_done", "rx_done", "pool", "dve"))
        rotated, qkr_done, kh_done, kl_done = map(s_, ("rotated", "qkr_done", "kh_done", "kl_done"))
        sb_done, sm_done, smh_done, sml_done = map(s_, ("sb_done", "sm_done", "smh_done", "sml_done"))
        sc_done, max_done, exp_done, pt_done, pth_done, ptl_done = map(
            s_, ("sc_done", "max_done", "exp_done", "pt_done", "pth_done", "ptl_done"))
        r_done, rh_done, rl_done = map(s_, ("r_done", "rh_done", "rl_done"))
        sqc_done, ssc_done, rc_done, qcn_done = map(s_, ("sqc_done", "ssc_done", "rc_done", "qcn_done"))
        o_done, cent_done, csq_done, ss4_done, r4_done, y_done, yg_done, eg_done, sig_done, sg_done, mix_done, o_free = map(
            s_, ("o_done", "cent_done", "csq_done", "ss4_done", "r4_done", "y_done", "yg_done", "eg_done", "sig_done", "sg_done",
                 "mix_done", "o_free"))
        CONSTS = 16 * 7
        block = st.enter_context(nc.Block())

        @block.sync
        def _(sp):
            for dst, src in ((ident, d["ident"]), (tri, d["tri"]), (dec, d["decay"]), (g128, d["decay_tile"])):
                sp.dma_start(dst[:], src).then_inc(const_in, 16)
            sp.dma_start(gng[:], d["ret_gn_g"].partition_broadcast(P)).then_inc(const_in, 16)
            for half in range(2):
                sp.dma_start(gqc[64 * half:64 * half + 64, :], d["qn_c"].rearrange("(p a) -> p a", a=1)).then_inc(const_in, 16)
            sp.dma_start(xb[:], d["x"][0:P, :]).then_inc(x_in, 16)

            def tile(t, more):
                if more:
                    sp.wait_ge(ssx_done, t + 1)
                    pj.wait_full(sp, t, XT1)
                    sp.dma_start(xb[:], d["x"][bass.ds((t + 1) * P, P), :]).then_inc(x_in, 16)
                sp.wait_ge(mix_done, 2 * t + 2)
                sp.dma_start(d["mix"][bass.ds(t * P, P), AW:D], mixt[:]).then_inc(mix_out, 16)

            for t in range(NT):
                tile(t, t + 1 < NT)
            sp.wait_ge(mix_out, 16 * NT)

        @block.gpsimd
        def _(pool):
            PER = 3
            setup = Steps(pool, consts_set)
            setup(pool.memset(mhalf[:], -0.5))
            pool.wait_ge(const_in, CONSTS)

            def scale_x(t, own):
                pool.wait_ge(ssx_done, t + 1)
                own(pool.tensor_scalar(msx[:], ssx[:], 1.0 / D, EPS, ALU.mult, ALU.add))
                pool.tensor_tensor(rx[:], msx[:], mhalf[:, 0:1], ALU.pow).then_inc(rx_done, 1)

            def rotate(t):
                pj.wait_hi(pool, t, QK)
                v = qk[:].rearrange("p (h s e) -> p h s e", s=2, e=HD // 2)
                for out, table in ((byc, cos), (bys, sin)):
                    i = pool.tensor_tensor(heads2(out[:]), heads2(qk[:]), across(table[:, bass.ds(t, 1), :]), ALU.mult)
                i.then_inc(rotated, 1)

            def heads2(ap):
                return ap.rearrange("p (h e) -> p h e", e=HD // 2)

            def across(ap):
                return ap.to_broadcast([P, 4 * BH, HD // 2])

            def scale_qc(t, own):
                pj.wait_hi(pool, t, QC)
                pool.tensor_tensor(sqc[:], qc[:], qc[:], ALU.mult).then_inc(sqc_done, 1)
                pool.wait_ge(ssc_done, t + 1)
                own(pool.tensor_scalar(msc[:], ssc[:], 1.0 / HD, EPS, ALU.mult, ALU.add))
                pool.tensor_tensor(rc[:], msc[:], mhalf[:], ALU.pow).then_inc(rc_done, 1)

            def norm(t, own):
                pool.wait_ge(sig_done, t + 1)
                pool.tensor_tensor(sg[:], g[:], eg[:], ALU.mult).then_inc(sg_done, 1)
                pool.wait_ge(cent_done, t + 1)
                pool.tensor_tensor(csq[:], cent[:], cent[:], ALU.mult).then_inc(csq_done, 1)
                pool.wait_ge(ss4_done, t + 1)
                own(pool.tensor_scalar(ms4[:], ss4[:], 1.0 / HD, EPS, ALU.mult, ALU.add))
                pool.tensor_tensor(r4[:], ms4[:], mhalf[:], ALU.pow).then_inc(r4_done, 1)
                pool.wait_ge(y_done, t + 1)
                pool.tensor_tensor(yg[:], y[:], gng[:], ALU.mult).then_inc(yg_done, 1)

            own = Steps(pool, pool_own)
            scale_x(0, own)
            rotate(0)
            scale_qc(0, own)

            def tile(t, more):
                own = Steps(pool, pool_own, PER * t + 2)
                if more:
                    scale_x(t + 1, own)
                    rotate(t + 1)
                norm(t, own)
                if more:
                    scale_qc(t + 1, own)
                    assert own.n == PER

            for t in range(NT):
                tile(t, t + 1 < NT)

        @block.scalar
        def _(act):
            def sum_squares(t):
                act.wait_ge(x_in, 16 * (t + 1))
                act.activation(junk[:], xb[:], ACT.Square, accum_out=ssx[:]).then_inc(ssx_done, 1)

            def take(t, f):
                pj.wait_full(act, t, f)
                if f in (XT0, XT1):
                    i = act.activation(xTh[:, 4 * f:4 * f + 4, :], tiles(PJ[:]), ACT.Copy)
                elif f == QK:
                    act.wait_ge(rx_done, t + 1)
                    i = act.activation(qk[:], PJ[:], ACT.Copy, scale=rx[:])
                elif f == VG:
                    act.activation(vh[:], PJ[:, 0:BW], ACT.Copy, scale=rx[:])
                    i = act.activation(g[:], PJ[:, BW:2 * BW], ACT.Copy, scale=rx[:])
                else:
                    i = act.activation(qc[:], PJ[:, 0:CW], ACT.Copy, scale=rx[:])
                i.then_inc(pj.hi, 1)

            def keys_hi(t):
                act.wait_ge(qkr_done, t + 1)
                act.activation(kh[:], qkr[:, BW:2 * BW], ACT.Copy).then_inc(kh_done, 1)

            act.wait_ge(consts_set, 2)
            sum_squares(0)
            for f in range(5):
                take(0, f)
            keys_hi(0)

            def tile(t, more):
                tr.wait_full(act, t, QKT)
                act.activation(qkTh[:], tiles(TR[:]), ACT.Copy).then_inc(tr.hi, 1)
                if more:
                    act.wait_ge(rx_done, t + 1)
                    sum_squares(t + 1)
                    take(t + 1, XT0)
                    take(t + 1, XT1)
                tr.wait_full(act, t, QCT)
                act.activation(qTCh[:], tiles(TR[:, 0:CW]), ACT.Copy, scale=gqc8[:]).then_inc(tr.hi, 1)
                act.wait_ge(sm_done, t + 1)
                act.activation(Smh[:], Sm[:], ACT.Copy).then_inc(smh_done, 1)
                act.wait_ge(max_done, t + 1)
                for h in range(CH):
                    act.activation(Pr[:, h, :], SC[:, place(h, N_MEM)], ACT.Exp, bias=nmax[:, h:h + 1],
                                   accum_out=rs[:, h:h + 1]).then_inc(exp_done, 1)
                if more:
                    take(t + 1, QK)
                act.activation(eg[:], g[:], ACT.Exp, scale=-1.0).then_inc(eg_done, 1)
                act.wait_ge(pt_done, t + 1)
                act.activation(PTh[:], PT[:], ACT.Copy).then_inc(pth_done, 1)
                act.wait_ge(r_done, t + 1)
                act.activation(Rh[:], R[:], ACT.Copy).then_inc(rh_done, 1)
                if more:
                    act.wait_ge(sg_done, t + 1)
                    take(t + 1, VG)
                    take(t + 1, QC)
                    keys_hi(t + 1)

            for t in range(NT):
                tile(t, t + 1 < NT)

        @block.tensor
        def _(pe):
            def fill(t, f, first=False):
                pj.wait_before(pe, t, f, first)
                if f in (XT0, XT1):
                    pe.wait_ge(x_in, 16 * (t + 1))
                    xs = xb[:].rearrange("p (m k) -> p k m", k=KD)
                    for j in range(4):
                        mm = pe.transpose(PJ[:, j * P:(j + 1) * P], xs[:, 4 * f + j, :], ident[:])
                else:
                    at, n = (f - QK) * 2 * BW, CW if f == QC else 2 * BW
                    for k in range(KD):
                        mm = product(pe, PJ[:, 0:n], (xTh[:, k, :], xTl[:, k, :]),
                                     (Wh[:, k, at:at + n], Wl[:, k, at:at + n]), k == 0, k == KD - 1)
                mm.then_inc(pj.full, 1)

            def half(h):
                return slice(64 * (h % 2), 64 * (h % 2) + 64)

            def tile(t, more, first):
                tr.wait_before(pe, t, QKT, first)
                pe.wait_ge(qkr_done, t + 1)
                for j in range(4):
                    mm = pe.transpose(TR[:, j * P:(j + 1) * P], qkr[:, j * P:(j + 1) * P], ident[:])
                mm.then_inc(tr.full, 1)
                if more:
                    fill(t + 1, XT0)
                    fill(t + 1, XT1)
                pe.wait_ge(qcn_done, t + 1)
                tr.wait_before(pe, t, QCT, False)
                for p in range(CH // 2):
                    mm = pe.transpose(TR[:, p * P:(p + 1) * P], qcn[:, p * P:(p + 1) * P], ident[:])
                mm.then_inc(tr.full, 1)
                if not first:
                    pe.wait_ge(ptl_done, t)
                for h in range(BH):
                    p, r = h // 2, half(h)
                    mm = product(pe, SB[:, place(h, P)], (qkTh[r, 2 + p, :], qkTl[r, 2 + p, :]),
                                 (qkTh[r, p, :], qkTl[r, p, :]))
                mm.then_inc(sb_done, 1)
                tr.wait_free(pe, t, QCT)
                for h in range(CH):
                    p, r = h // 2, half(h)
                    mm = product(pe, SC[:, place(h, N_MEM)], (qTCh[r, p, :], qTCl[r, p, :]),
                                 (kTCh[r, p, :], kTCl[r, p, :]))
                mm.then_inc(sc_done, 1)
                if more:
                    fill(t + 1, QK)
                pe.wait_ge(exp_done, CH * (t + 1))
                pe.wait_ge(sm_done, t + 1)
                for h in range(CH):
                    for b in range(MT):
                        j = h * MT + b
                        mm = pe.transpose(PT[:, j * P:(j + 1) * P], Pr[:, h, b * P:(b + 1) * P], ident[:])
                mm.then_inc(pt_done, 1)
                pe.wait_ge(sml_done, t + 1)
                if first:
                    pe.wait_ge(state0, 2)
                else:
                    pe.wait_ge(o_free, 2 * t)
                    pe.wait_ge(rl_done, t)
                for h in range(BH):
                    p, r, cols = h // 2, half(h), slice(h * HD, (h + 1) * HD)
                    product(pe, O[:, place(h, HD)], (Smh[:, h, :], Sml[:, h, :]), (vh[:, cols], vl[:, cols]), True, False)
                    product(pe, O[:, place(h, HD)], (qkTh[r, p, :], qkTl[r, p, :]), (Rh[r, p, :], Rl[r, p, :]), False, True)
                pe.wait_ge(kl_done, t + 1)
                tr.wait_before(pe, t, U, False)
                for p in range(BH // 2):
                    cols = slice(p * P, (p + 1) * P)
                    mm = product(pe, TR[:, cols], (kh[:, cols], kl[:, cols]), (vh[:, cols], vl[:, cols]))
                mm.then_inc(tr.full, 1)
                if more:
                    fill(t + 1, VG)
                pe.wait_ge(ptl_done, t + 1)
                for h in range(CH):
                    cols = slice(h * HD, (h + 1) * HD)
                    for b in range(MT):
                        j = slice((h * MT + b) * P, (h * MT + b + 1) * P)
                        mm = product(pe, O[:, place(h, HD, 2 * HD)], (PTh[:, j], PTl[:, j]),
                                     (VCh[:, b, cols], VCl[:, b, cols]), b == 0, b == MT - 1)
                mm.then_inc(o_done, 1)
                if more:
                    fill(t + 1, QC)

            pe.wait_ge(const_in, CONSTS)
            for f in range(5):
                fill(0, f, f == 0)
            for t in range(NT):
                tile(t, t + 1 < NT, t == 0)

        @block.vector
        def _(dve):
            PER = 2
            dve.wait_ge(const_in, CONSTS)
            dve.tensor_scalar(gqc8[:], gqc[:], HD ** -0.5, None, ALU.mult).then_inc(consts_set, 1)
            dve.memset(R[:], 0.0).then_inc(state0, 1)
            dve.wait_ge(state0, 1)
            dve.tensor_copy(Rh[:], R[:])
            dve.tensor_copy(Rl[:], R[:]).then_inc(state0, 1)
            dve.wait_ge(consts_set, 2)

            def take(t, f):
                pj.wait_hi(dve, t, f)
                if f in (XT0, XT1):
                    dve.tensor_tensor(xTl[:, 4 * f:4 * f + 4, :], tiles(PJ[:]), xTh[:, 4 * f:4 * f + 4, :].bitcast(F32),
                                      ALU.subtract).then_inc(pj.lo, 1)
                else:
                    dve.scalar_tensor_tensor(vl[:], PJ[:, 0:BW], rx[:], vh[:].bitcast(F32), ALU.mult,
                                             ALU.subtract).then_inc(pj.lo, 1)

            def rotate(t):
                dve.wait_ge(rotated, t + 1)
                v = lambda ap: ap.rearrange("p (h s e) -> p h s e", s=2, e=HD // 2)
                i = dve.tensor_tensor(v(rot[:])[:, :, 0, :], v(byc[:])[:, :, 0, :], v(bys[:])[:, :, 1, :], ALU.subtract)
                i.then_inc(dve_rot, 1)
                i = dve.tensor_tensor(v(rot[:])[:, :, 1, :], v(bys[:])[:, :, 0, :], v(byc[:])[:, :, 1, :], ALU.add)
                i.then_inc(dve_rot, 1)
                dve.wait_ge(dve_rot, 2 * t + 2)
                dve.tensor_tensor(heads(qkr[:]), heads(rot[:]), wide(dec[:], HD), ALU.mult).then_inc(qkr_done, 1)

            def keys_lo(t):
                dve.wait_ge(kh_done, t + 1)
                dve.tensor_tensor(kl[:], qkr[:, BW:2 * BW], kh[:].bitcast(F32), ALU.subtract).then_inc(kl_done, 1)

            def scale_qc(t):
                dve.wait_ge(sqc_done, t + 1)
                dve.tensor_reduce(ssc[:], heads(sqc[:]), AX.X, ALU.add).then_inc(ssc_done, 1)
                dve.wait_ge(rc_done, t + 1)
                dve.tensor_tensor(heads(qcn[:]), heads(qc[:]), wide(rc[:], HD), ALU.mult).then_inc(qcn_done, 1)

            dve_rot = s_("dve_rot")
            take(0, XT0)
            take(0, XT1)
            rotate(0)
            take(0, VG)
            scale_qc(0)
            keys_lo(0)

            def tile(t, more, first):
                own = Steps(dve, dve_own, OWN * t)
                tr.wait_hi(dve, t, QKT)
                dve.tensor_tensor(qkTl[:], tiles(TR[:]), qkTh[:].bitcast(F32), ALU.subtract).then_inc(tr.lo, 1)
                if more:
                    take(t + 1, XT0)
                    take(t + 1, XT1)
                tr.wait_hi(dve, t, QCT)
                dve.scalar_tensor_tensor(qTCl[:], tiles(TR[:, 0:CW]), gqc8[:], qTCh[:].bitcast(F32), ALU.mult,
                                         ALU.subtract).then_inc(tr.lo, 1)
                dve.wait_ge(sb_done, t + 1)
                for s in range(2):
                    i = dve.tensor_tensor(Sm[:].rearrange("p (a s) n -> p s a n", s=2)[:, s], by_head(SB[:], P)[:, s],
                                          tri[:].unsqueeze(1).to_broadcast([P, 2, P]), ALU.mult)
                i.then_inc(sm_done, 1)
                dve.wait_ge(sc_done, t + 1)
                dve.tensor_reduce(halves1(nmax[:]), by_head(SC[:], N_MEM), AX.X, ALU.max,
                                  negate=True).then_inc(max_done, 1)
                dve.wait_ge(smh_done, t + 1)
                dve.tensor_tensor(Sml[:], Sm[:], Smh[:].bitcast(F32), ALU.subtract).then_inc(sml_done, 1)
                dve.wait_ge(eg_done, t + 1)
                own(dve.tensor_scalar(eg[:], eg[:], 1.0, None, ALU.add))
                dve.reciprocal(eg[:], eg[:]).then_inc(sig_done, 1)
                if more:
                    rotate(t + 1)
                dve.wait_ge(pth_done, t + 1)
                dve.tensor_tensor(PTl[:], PT[:], PTh[:].bitcast(F32), ALU.subtract).then_inc(ptl_done, 1)
                tr.wait_full(dve, t, U)
                u = TR[:, 0:BW].rearrange("p (a b e) -> p a b e", b=2, e=HD)
                dve.tensor_tensor(Rt[0:64], R[0:64], u[0:64, :, 0, :], ALU.add)
                own(dve.tensor_tensor(Rt[64:128], R[64:128], u[64:128, :, 1, :], ALU.add))
                own(dve.tensor_tensor(R[:], Rt[:], wide(g128[:], HD), ALU.mult))
                dve.sem_inc(tr.lo, 1)
                dve.sem_inc(r_done, 1)
                dve.wait_ge(rh_done, t + 1)
                dve.tensor_tensor(Rl[:], R[:], Rh[:].bitcast(F32), ALU.subtract).then_inc(rl_done, 1)
                if more:
                    take(t + 1, VG)
                dve.wait_ge(o_done, t + 1)
                own(dve.tensor_reduce(halves1(sm4[:]), by_head(O[:], HD), AX.X, ALU.add))
                own(dve.tensor_scalar(mean[:], sm4[:], 1.0 / HD, None, ALU.mult))
                dve.tensor_tensor(halves(cent[:]), by_head(O[:], HD),
                                  halves1(mean[:]).unsqueeze(3).to_broadcast([P, 2, 2, HD]), ALU.subtract).then_inc(cent_done, 1)
                own(dve.reciprocal(rinv[:], rs[:]))
                if not first:
                    dve.wait_ge(mix_out, 16 * t)
                dve.tensor_tensor(halves(mixt[:, BW:BW + CW]), by_head(O[:], HD, 2 * HD),
                                  halves1(rinv[:]).unsqueeze(3).to_broadcast([P, 2, 2, HD]), ALU.mult).then_inc(mix_done, 1)
                dve.wait_ge(mix_done, 2 * t + 1)
                dve.sem_inc(o_free, 2)
                dve.wait_ge(csq_done, t + 1)
                dve.tensor_reduce(ss4[:], heads(csq[:]), AX.X, ALU.add).then_inc(ss4_done, 1)
                dve.wait_ge(r4_done, t + 1)
                dve.tensor_tensor(heads(y[:]), heads(cent[:]), wide(r4[:], HD), ALU.mult).then_inc(y_done, 1)
                if more:
                    scale_qc(t + 1)
                    keys_lo(t + 1)
                dve.wait_ge(yg_done, t + 1)
                dve.wait_ge(sg_done, t + 1)
                dve.tensor_tensor(mixt[:, 0:BW], yg[:], sg[:], ALU.mult).then_inc(mix_done, 1)
                assert own.n == OWN

            OWN = 6
            for t in range(NT):
                tile(t, t + 1 < NT, t == 0)



NLG = NG + NE
CAP = P
FULL = SEQ * 2 // CAP
BLOCKS = NE + FULL
KF = DE // P
SKIP = 1 << 20


def phase_o(c, d, lg):
    nc = c.nc
    with ExitStack() as st:
        Wh = sbuf(nc, st, "o_wh", [P, KD, D], F32R)
        Wl = sbuf(nc, st, "o_wl", [P, KD, D], F32R)
        Rh = sbuf(nc, st, "o_rh", [P, KD, NLG], F32R)
        Rl = sbuf(nc, st, "o_rl", [P, KD, NLG], F32R)
        split_weights(c, "o_w", rows(d["w_out"], KD), None, Wh, Wl, KD, D)
        t_ = lambda name, shape, dt=F32: sbuf(nc, st, "o_" + name, shape, dt)
        wr = t_("wr", [P, KD, NLG])
        mx, xb, h, hn = t_("m", [P, D]), t_("x", [P, D]), t_("h", [P, D]), t_("hn", [P, D])
        mTh, mTl = t_("mth", [P, KD, P], F32R), t_("mtl", [P, KD, P], F32R)
        nTh, nTl = t_("nth", [P, KD, P], F32R), t_("ntl", [P, KD, P], F32R)
        junk = t_("junk", [P, D], BF16)
        zero = t_("zero", [P, D])
        zero_out = c.sem("o_zero_out")
        ident = t_("ident", [P, P])
        gf, br = t_("gf", [P, D]), t_("br", [P, NLG])
        mhalf, ss, ms, r = t_("mhalf", [P, 1]), t_("ss", [P, 1]), t_("ms", [P, 1]), t_("r", [P, 1])
        Y, LG, PJ = c.bank2[0], c.bank[0], c.bank[1]
        XT0, XT1, HT0, HT1 = range(4)
        s_ = lambda name: c.sem("o_" + name)
        const_in, m_in, x_in, wr_in, wr_hi, wr_lo, pool_set = map(s_, ("const_in", "m_in", "x_in", "wr_in", "wr_hi", "wr_lo", "pool_set"))
        x_full, x_hi, x_lo, n_full, n_hi, n_lo = map(s_, ("x_full", "x_hi", "x_lo", "n_full", "n_hi", "n_lo"))
        y_done, h_done, ss_done, ms_done, r_done, hn_done, lg_full, lg_done, h_out, hn_out = map(
            s_, ("y_done", "h_done", "ss_done", "ms_done", "r_done", "hn_done", "lg_full", "lg_done", "h_out", "hn_out"))
        CONSTS = 16 * 4
        block = st.enter_context(nc.Block())

        @block.sync
        def _(sp):
            sp.dma_start(wr[:, :, 0:NG], rows(d["w_router_group"], KD)).then_inc(wr_in, 16)
            sp.dma_start(wr[:, :, NG:NLG], rows(d["w_router_expert"], KD)).then_inc(wr_in, 16)
            sp.dma_start(ident[:], d["ident"]).then_inc(const_in, 16)
            sp.dma_start(gf[:], d["ffn_norm_g"].partition_broadcast(P)).then_inc(const_in, 16)
            sp.dma_start(br[:, 0:NG], d["b_router_group"].partition_broadcast(P)).then_inc(const_in, 16)
            sp.dma_start(br[:, NG:NLG], d["b_router_expert"].partition_broadcast(P)).then_inc(const_in, 16)
            sp.dma_start(mx[:], d["mix"][0:P, :]).then_inc(m_in, 16)
            sp.dma_start(xb[:], d["x"][0:P, :]).then_inc(x_in, 16)

            def tile(t, more):
                if more:
                    sp.wait_ge(x_full, 2 * t + 2)
                    sp.dma_start(mx[:], d["mix"][bass.ds((t + 1) * P, P), :]).then_inc(m_in, 16)
                sp.wait_ge(h_done, t + 1)
                if more:
                    sp.dma_start(xb[:], d["x"][bass.ds((t + 1) * P, P), :]).then_inc(x_in, 16)
                sp.dma_start(d["h"][bass.ds(t * P, P), :], h[:]).then_inc(h_out, 16)
                sp.wait_ge(hn_done, t + 1)
                sp.dma_start(d["hn"][bass.ds(t * P, P), :], hn[:]).then_inc(hn_out, 16)

            for t in range(NT):
                tile(t, t + 1 < NT)
            sp.wait_ge(h_out, 16 * NT)
            sp.wait_ge(hn_out, 16 * NT)

        @block.gpsimd
        def _(pool):
            pool.memset(mhalf[:], -0.5).then_inc(pool_set, 1)
            pool.memset(zero[:], 0.0).then_inc(pool_set, 1)
            pool.wait_ge(pool_set, 2)
            pool.dma_start(d["y"][NE * P:, :].rearrange("(b p) n -> p b n", p=P),
                           zero[:].unsqueeze(1).to_broadcast([P, FULL, D])).then_inc(zero_out, 16)

            def tile(t):
                pool.wait_ge(ss_done, t + 1)
                pool.tensor_scalar(ms[:], ss[:], 1.0 / D, EPS, ALU.mult, ALU.add).then_inc(ms_done, 1)
                pool.wait_ge(ms_done, t + 1)
                pool.tensor_tensor(r[:], ms[:], mhalf[:], ALU.pow).then_inc(r_done, 1)

            for t in range(NT):
                tile(t)
            pool.wait_ge(zero_out, 16)

        @block.scalar
        def _(act):
            act.wait_ge(wr_in, 32)
            act.activation(Rh[:], wr[:], ACT.Copy).then_inc(wr_hi, 1)

            def mixed(t):
                for f in range(2):
                    act.wait_ge(x_full, 2 * t + f + 1)
                    act.activation(mTh[:, 4 * f:4 * f + 4, :], tiles(PJ[:]), ACT.Copy).then_inc(x_hi, 1)

            def tile(t, more, first):
                act.wait_ge(h_done, t + 1)
                if not first:
                    act.wait_ge(ms_done, t)
                    act.wait_ge(ss_done, t)
                act.activation(junk[:], h[:], ACT.Square, accum_out=ss[:]).then_inc(ss_done, 1)
                if more:
                    mixed(t + 1)
                for f in range(2):
                    act.wait_ge(n_full, 2 * t + f + 1)
                    act.activation(nTh[:, 4 * f:4 * f + 4, :], tiles(PJ[:]), ACT.Copy).then_inc(n_hi, 1)

            mixed(0)
            for t in range(NT):
                tile(t, t + 1 < NT, t == 0)

        @block.tensor
        def _(pe):
            def turn(t, src, k0, full):
                xs = src[:].rearrange("p (m k) -> p k m", k=KD)
                for j in range(4):
                    mm = pe.transpose(PJ[:, j * P:(j + 1) * P], xs[:, k0 + j, :], ident[:])
                mm.then_inc(full, 1)

            def mixed(t, first):
                pe.wait_ge(m_in, 16 * (t + 1))
                if not first:
                    pe.wait_ge(n_lo, 2 * (t - 1))
                turn(t, mx, 0, x_full)
                pe.wait_ge(x_lo, 2 * t + 1)
                turn(t, mx, 4, x_full)
                pe.wait_ge(x_lo, 2 * t + 2)
                if not first:
                    pe.wait_ge(h_done, t)
                for half in range(2):
                    cols = slice(512 * half, 512 * half + 512)
                    for k in range(KD):
                        mm = product(pe, Y[:, cols], (mTh[:, k, :], mTl[:, k, :]), (Wh[:, k, cols], Wl[:, k, cols]),
                                     k == 0, k == KD - 1)
                mm.then_inc(y_done, 1)

            def tile(t, more, first):
                if more:
                    mixed(t + 1, False)
                pe.wait_ge(hn_done, t + 1)
                if not more:
                    pe.wait_ge(x_lo, 2 * t + 2)
                turn(t, hn, 0, n_full)
                pe.wait_ge(n_lo, 2 * t + 1)
                turn(t, hn, 4, n_full)
                pe.wait_ge(n_lo, 2 * t + 2)
                if not first:
                    pe.wait_ge(lg_done, t)
                for k in range(KD):
                    mm = product(pe, LG[:, 0:NLG], (nTh[:, k, :], nTl[:, k, :]), (Rh[:, k, :], Rl[:, k, :]), k == 0, k == KD - 1)
                mm.then_inc(lg_full, 1)

            pe.wait_ge(const_in, CONSTS)
            pe.wait_ge(wr_lo, 1)
            mixed(0, True)
            for t in range(NT):
                tile(t, t + 1 < NT, t == 0)

        @block.vector
        def _(dve):
            dve.wait_ge(const_in, CONSTS)
            dve.wait_ge(wr_hi, 1)
            dve.tensor_tensor(Rl[:], wr[:], Rh[:].bitcast(F32), ALU.subtract).then_inc(wr_lo, 1)

            def mixed(t):
                for f in range(2):
                    dve.wait_ge(x_hi, 2 * t + f + 1)
                    dve.tensor_tensor(mTl[:, 4 * f:4 * f + 4, :], tiles(PJ[:]), mTh[:, 4 * f:4 * f + 4, :].bitcast(F32),
                                      ALU.subtract).then_inc(x_lo, 1)

            def tile(t, more, first):
                dve.wait_ge(y_done, t + 1)
                dve.wait_ge(x_in, 16 * (t + 1))
                if not first:
                    dve.wait_ge(h_out, 16 * t)
                    dve.wait_ge(ss_done, t)
                    dve.wait_ge(hn_done, t)
                dve.tensor_tensor(h[:], Y[:], xb[:], ALU.add).then_inc(h_done, 1)
                dve.wait_ge(r_done, t + 1)
                if not first:
                    dve.wait_ge(hn_out, 16 * t)
                dve.scalar_tensor_tensor(hn[:], h[:], r[:], gf[:], ALU.mult, ALU.mult).then_inc(hn_done, 1)
                if more:
                    mixed(t + 1)
                for f in range(2):
                    dve.wait_ge(n_hi, 2 * t + f + 1)
                    dve.tensor_tensor(nTl[:, 4 * f:4 * f + 4, :], tiles(PJ[:]), nTh[:, 4 * f:4 * f + 4, :].bitcast(F32),
                                      ALU.subtract).then_inc(n_lo, 1)
                dve.wait_ge(lg_full, t + 1)
                dve.tensor_tensor(lg[:, bass.ds(t, 1), :].rearrange("p a n -> p (a n)"), LG[:, 0:NLG], br[:], ALU.add).then_inc(lg_done, 1)

            mixed(0)
            for t in range(NT):
                tile(t, t + 1 < NT, t == 0)


def phase_r(c, d, lg, dest, wt, btab, ids):
    nc = c.nc
    with ExitStack() as st:
        t_ = lambda name, shape, dt=F32: sbuf(nc, st, "r_" + name, shape, dt)
        g8, gtop, gix = t_("g8", [P, NT, 8]), t_("gtop", [P, NT, 8]), t_("gix", [P, NT, 8], U32)
        gf, gsum, pg = t_("gf", [P, NT]), t_("gsum", [P, NT]), t_("pg", [P, NT])
        ge = t_("ge", [P, NT, NG])
        tab = t_("tab", [P, 2 * NE + 8 + FULL])
        ones, before = t_("ones", [P, P]), t_("before", [P, P])
        mask, pen, em = t_("mask", [P, NT, NE]), t_("pen", [P, NT, NE]), t_("em", [P, NT, NE])
        top, ix, ixf = t_("top", [P, NT, 8]), t_("ix", [P, NT, 8], U32), t_("ixf", [P, NT, 2])
        dv, ev = t_("dv", [P, NT]), t_("ev", [P, NT])
        A1, A2, A = t_("a1", [P, NT, NE]), t_("a2", [P, NT, NE]), t_("a", [P, NT, NE])
        rank, prior, cnt = t_("rank", [P, NT, NE]), t_("prior", [P, NT, NE]), t_("cnt", [P, NE])
        over, extra, upto, one = t_("over", [P, NE, 8]), t_("extra", [P, NE]), t_("upto", [P, NE]), t_("one", [P, NE])
        shift, late, row, pick = t_("shift", [P, NE]), t_("late", [P, NT, NE]), t_("row", [P, NT, NE]), t_("pick", [P, NT, NE])
        destf = t_("destf", [P, 2, NT])
        bm, bsum = t_("bm", [P, FULL, NE]), t_("bsum", [P, FULL + 1])
        tok = t_("tok", [P, NT], I32)
        blank = t_("blank", [P, BLOCKS], I32)
        C0, C1 = c.bank[0], c.bank[1]
        s_ = lambda name: c.sem("r_" + name)
        const_in, own_s, ge_in, ge_out, ev_in, ev_out, a_done, sums, dest_done, blank_set, blank_out, tok_out, ids_in = map(
            s_, ("const_in", "own", "ge_in", "ge_out", "ev_in", "ev_out", "a_done", "sums", "dest_done", "blank_set",
                 "blank_out", "tok_out", "ids_in"))
        GOF, EOF, BND, LATER = tab[:, 0:NE], tab[:, NE:2 * NE], tab[:, 2 * NE:2 * NE + 7], tab[:, 2 * NE + 8:]
        block = st.enter_context(nc.Block())

        def over_tiles(ap):
            return ap.unsqueeze(1).to_broadcast([P, NT, ap.shape[1]])

        @block.sync
        def _(sp):
            sp.dma_start(tab[:], d["route_tab"].partition_broadcast(P)).then_inc(const_in, 16)
            sp.dma_start(before[:], d["before"]).then_inc(const_in, 16)
            sp.dma_start(tok[:], d["token"]).then_inc(const_in, 16)
            sp.wait_ge(blank_set, 1)
            sp.dma_start(d["row_token"].rearrange("(i p) a -> p (i a)", p=P), blank[:], allow_slow_non_contiguous=True).then_inc(blank_out, 16)
            sp.wait_ge(tok_out, 16 * 2 * NT)
            sp.dma_start(ids[:], d["row_token"].rearrange("(i p) a -> p (i a)", p=P), allow_slow_non_contiguous=True).then_inc(ids_in, 16)
            sp.wait_ge(ids_in, 16)

        @block.gpsimd
        def _(pool):
            pool.memset(blank[:], SKIP).then_inc(blank_set, 1)
            pool.wait_ge(const_in, 48)
            pool.wait_ge(blank_out, 16)
            pool.wait_ge(dest_done, 1)
            for j in range(2):
                for t in range(NT):
                    pool.indirect_dma_start(out=d["row_token"], out_offset=bass.IndirectOffsetOnAxis(ap=dest[:, j, t:t + 1], axis=0),
                                            in_=tok[:, t:t + 1], in_offset=None).then_inc(tok_out, 16)

        @block.scalar
        def _(act):
            act.wait_ge(ge_in, 1)
            act.activation(ge[:], ge[:], ACT.Exp).then_inc(ge_out, 1)
            act.wait_ge(ev_in, 1)
            act.activation(ev[:], dv[:], ACT.Exp).then_inc(ev_out, 1)

        @block.tensor
        def _(pe):
            pe.wait_ge(const_in, 48)
            pe.wait_ge(a_done, 1)
            flat = A[:].rearrange("p t e -> p (t e)")
            pe.matmul(C0[:, 0:NT * NE], before[:], flat, start=True, stop=True)
            pe.matmul(C1[:, 0:NT * NE], ones[:], flat, start=True, stop=True).then_inc(sums, 1)

        @block.vector
        def _(dve):
            own = Steps(dve, own_s)
            own(dve.memset(ones[:], 1.0))
            own(dve.memset(one[:], 1.0))
            own(dve.memset(g8[:], NEG))
            own(dve.tensor_copy(g8[:, :, 0:NG], lg[:, :, 0:NG]))
            for t in range(NT):
                last = dve.max(gtop[:, t, :], g8[:, t, :])
            own(last)
            for t in range(NT):
                last = dve.max_index(gix[:, t, :], gtop[:, t, :], g8[:, t, :])
            own(last)
            dve.tensor_tensor(ge[:], lg[:, :, 0:NG], gtop[:, :, 0:1].to_broadcast([P, NT, NG]), ALU.subtract).then_inc(ge_in, 1)
            own(dve.tensor_copy(gf[:], gix[:, :, 0]))
            dve.wait_ge(const_in, 48)
            own(dve.tensor_tensor(mask[:], over_tiles(GOF), wide(gf[:], NE), ALU.is_equal))
            own(dve.tensor_scalar(pen[:], mask[:], -NEG, NEG, ALU.mult, ALU.add))
            own(dve.tensor_tensor(em[:], lg[:, :, NG:NLG], mask[:], ALU.mult))
            own(dve.tensor_tensor(em[:], em[:], pen[:], ALU.add))
            for t in range(NT):
                last = dve.max(top[:, t, :], em[:, t, :])
            own(last)
            for t in range(NT):
                last = dve.max_index(ix[:, t, :], top[:, t, :], em[:, t, :])
            own(last)
            dve.tensor_tensor(dv[:], top[:, :, 1], top[:, :, 0], ALU.subtract).then_inc(ev_in, 1)
            own(dve.tensor_copy(ixf[:], ix[:, :, 0:2]))
            own(dve.tensor_tensor(A1[:], over_tiles(EOF), ixf[:, :, 0:1].to_broadcast([P, NT, NE]), ALU.is_equal))
            own(dve.tensor_tensor(A2[:], over_tiles(EOF), ixf[:, :, 1:2].to_broadcast([P, NT, NE]), ALU.is_equal))
            dve.tensor_tensor(A[:], A1[:], A2[:], ALU.add).then_inc(a_done, 1)
            dve.wait_ge(ge_out, 1)
            own(dve.tensor_reduce(gsum[:], ge[:], AX.X, ALU.add))
            own(dve.reciprocal(pg[:], gsum[:]))
            dve.wait_ge(ev_out, 1)
            own(dve.tensor_scalar(dv[:], ev[:], 1.0, None, ALU.add))
            own(dve.reciprocal(dv[:], dv[:]))
            own(dve.tensor_tensor(wt[:, 0, :], pg[:], dv[:], ALU.mult))
            own(dve.tensor_tensor(wt[:, 1, :], wt[:, 0, :], ev[:], ALU.mult))
            dve.wait_ge(sums, 1)
            own(dve.memset(prior[:, 0, :], 0.0))
            for t in range(NT - 1):
                own(dve.tensor_tensor(prior[:, t + 1, :], prior[:, t, :], C1[:, t * NE:(t + 1) * NE], ALU.add))
            own(dve.tensor_tensor(cnt[:], prior[:, NT - 1, :], C1[:, (NT - 1) * NE:NT * NE], ALU.add))
            own(dve.tensor_tensor(rank[:].rearrange("p t e -> p (t e)"), C0[:, 0:NT * NE], prior[:].rearrange("p t e -> p (t e)"), ALU.add))
            own(dve.tensor_tensor(over[:, :, 0:7], wide(cnt[:], 7), BND.unsqueeze(1).to_broadcast([P, NE, 7]), ALU.is_gt))
            own(dve.tensor_reduce(extra[:], over[:, :, 0:7], AX.X, ALU.add))
            own(dve.tensor_tensor_scan(upto[:], one[:], extra[:], 0.0, ALU.mult, ALU.add))
            own(dve.tensor_tensor(shift[:], upto[:], extra[:], ALU.subtract))
            own(dve.tensor_tensor(shift[:], shift[:], EOF, ALU.subtract))
            own(dve.tensor_scalar(shift[:], shift[:], NE - 1.0, float(CAP), ALU.add, ALU.mult))
            own(dve.tensor_scalar(late[:], rank[:], float(CAP), None, ALU.is_ge))
            own(dve.tensor_tensor(late[:], late[:], over_tiles(shift[:]), ALU.mult))
            own(dve.tensor_tensor(row[:], rank[:], late[:], ALU.add))
            own(dve.scalar_tensor_tensor(row[:], over_tiles(EOF), float(CAP), row[:], ALU.mult, ALU.add))
            for j, a in enumerate((A1, A2)):
                own(dve.tensor_tensor(pick[:], row[:], a[:], ALU.mult))
                own(dve.tensor_reduce(destf[:, j, :], pick[:], AX.X, ALU.add))
            dve.tensor_copy(dest[:], destf[:]).then_inc(dest_done, 1)
            own(dve.tensor_tensor(bm[:], upto[:].unsqueeze(1).to_broadcast([P, FULL, NE]), wide(LATER, NE), ALU.is_le))
            own(dve.tensor_reduce(bsum[:, 0:FULL], bm[:], AX.X, ALU.add))
            own(dve.tensor_scalar(bsum[:, 0:FULL], bsum[:, 0:FULL], NE - 1.0, None, ALU.min))
            own(dve.tensor_scalar(bsum[:, FULL:FULL + 1], upto[:, NE - 1:NE], NE - 3.0, None, ALU.add))
            own(dve.tensor_copy(btab[:, 0:NE], EOF))
            own(dve.tensor_copy(btab[:, NE:], bsum[:]))


def phase_e(c, d, btab, ids):
    nc = c.nc
    with ExitStack() as st:
        t_ = lambda name, shape, dt=F32: sbuf(nc, st, "e_" + name, shape, dt)
        raw = t_("raw", [P, 3, KD * DE])
        Wh, Wl = t_("wh", [P, 3, KD * DE], F32R), t_("wl", [P, 3, KD * DE], F32R)
        ident = t_("ident", [P, P])
        ix = t_("ix", [P, 1], U32)
        xg = t_("xg", [P, D])
        xTh, xTl = t_("xth", [P, KD, P], F32R), t_("xtl", [P, KD, P], F32R)
        sg, hs = t_("sg", [P, DE]), t_("hs", [P, DE])
        hTh, hTl = t_("hth", [P, KF, P], F32R), t_("htl", [P, KF, P], F32R)
        y = t_("y", [P, D])
        XT, Y = c.bank2[0], c.bank2[1]
        G, U = c.bank2[2][:, 0:512], c.bank2[2][:, 512:1024]
        HT = c.bank[0]
        s_ = lambda name: c.sem("e_" + name)
        const_in, ix_set, xg_set, xg_in, y_out, sp_passed, pool_passed = map(
            s_, ("const_in", "ix_set", "xg_set", "xg_in", "y_out", "sp_passed", "pool_passed"))
        GU, DN = range(KD // 2), range(KD // 2, KD // 2 + KF // 2)
        CH_ = [*GU, *DN]
        loaded, hi, lo, used = ([s_(f"{n}{j}") for j in CH_] for n in ("loaded", "hi", "lo", "used"))
        xt_done, xt_hi, xt_lo, ht_done, ht_hi, ht_lo = map(s_, ("xt_done", "xt_hi", "xt_lo", "ht_done", "ht_hi", "ht_lo"))
        sg_done, hs_done, y_done = map(s_, ("sg_done", "hs_done", "y_done"))
        BY_POOL = (GU[1],)
        block = st.enter_context(nc.Block())
        GATE, UP, DOWN = range(3)

        def part(buf, j):
            if j in GU:
                return buf[:, 0:2, 2 * j * DE:2 * (j + 1) * DE]
            return buf[:, DOWN, 2 * (j - DN[0]) * D:2 * (j - DN[0] + 1) * D]

        def is_first(i):
            return isinstance(i, int) and i == 0

        def turns(eng, body, after=1):
            n = eng.value_load(btab[0:1, BLOCKS:BLOCKS + 1], min_val=NE - 3, max_val=BLOCKS - 4)
            body(0, None, after)
            body(1, 0, after)
            with eng.Fori(1, n + (2 - after)) as p:
                body(p + 1, p, after)
            for more in reversed(range(after)):
                body(n + (3 - more) - 1, n + (3 - more) - 2, more)
            return n + 2

        def split_lo(eng, i, j):
            eng.wait_ge(hi[j], i + 1)
            eng.tensor_tensor(part(Wl, j), part(raw, j), part(Wh, j).bitcast(F32), ALU.subtract).then_inc(lo[j], 1)

        @block.sync
        def _(sp):
            sp.dma_start(ident[:], d["ident"]).then_inc(const_in, 16)

            def load(e, j):
                if j in GU:
                    for m, w in ((GATE, d["w_gate"]), (UP, d["w_up"])):
                        src = w.rearrange("e (p k) n -> e p (k n)", p=P)[bass.ds(e, 1), :, 2 * j * DE:2 * (j + 1) * DE]
                        sp.dma_start(raw[:, m, 2 * j * DE:2 * (j + 1) * DE], src.rearrange("a p n -> p (a n)")).then_inc(loaded[j], 16)
                else:
                    k = j - DN[0]
                    src = d["w_down"].rearrange("e (p k) n -> e p (k n)", p=P)[bass.ds(e, 1), :, 2 * k * D:2 * (k + 1) * D]
                    sp.dma_start(part(raw, j), src.rearrange("a p n -> p (a n)")).then_inc(loaded[j], 16)

            def expert(i):
                return i if isinstance(i, int) else sp.value_load(btab[0:1, bass.ds(i, 1)], min_val=0, max_val=NE - 1)

            def load_next(i, chunks):
                e = expert(i)
                for j in chunks:
                    wait_apart(sp, lo[j], i, sp_passed)
                    load(e, j)

            def turn(i, p, more):
                if p is not None:
                    load_next(i, DN)
                if more == 2:
                    load_next(i + 2, GU)
                if p is not None:
                    wait_apart(sp, y_done, i, sp_passed)
                    sp.dma_start(d["y"][bass.ds(p * P, P), :], y[:]).then_inc(y_out, 16)

            for j in CH_:
                load(0, j)
            load_next(1, GU)
            last = turns(sp, turn, 2)
            wait_apart(sp, y_done, last + 1, sp_passed)
            sp.dma_start(d["y"][bass.ds(last * P, P), :], y[:]).then_inc(y_out, 16)
            wait_apart(sp, y_out, 16 * (last + 1), sp_passed)

        @block.gpsimd
        def _(pool):
            pool.memset(xg[:], 0.0).then_inc(xg_set, 1)
            pool.wait_ge(xg_set, 1)

            def gather(i):
                if not is_first(i):
                    wait_apart(pool, xt_done, i, pool_passed)
                pool.tensor_copy(ix[:], ids[:, bass.ds(i, 1)]).then_inc(ix_set, 1)
                wait_apart(pool, ix_set, i + 1, pool_passed)
                pool.indirect_dma_start(out=xg[:], out_offset=None, in_=d["hn"],
                                        in_offset=bass.IndirectOffsetOnAxis(ap=ix[:], axis=0),
                                        bounds_check=SEQ - 1, oob_is_err=False).then_inc(xg_in, 16)

            def turn(i, p, more):
                if more:
                    gather(i + 1)
                    for j in BY_POOL:
                        split_lo(pool, i + 1, j)

            gather(0)
            for j in BY_POOL:
                split_lo(pool, 0, j)
            turns(pool, turn)

        @block.scalar
        def _(act):
            def split(i, j):
                act.wait_ge(loaded[j], (32 if j in GU else 16) * (i + 1))
                if not is_first(i):
                    act.wait_ge(used[j], i)
                act.activation(part(Wh, j), part(raw, j), ACT.Copy).then_inc(hi[j], 1)

            def turn_x(i):
                act.wait_ge(xt_done, i + 1)
                act.activation(xTh[:], tiles(XT[:]), ACT.Copy).then_inc(xt_hi, 1)

            def turn_h(i):
                act.wait_ge(ht_done, i + 1)
                act.activation(hTh[:], tiles(HT[:]), ACT.Copy).then_inc(ht_hi, 1)

            def turn(i, p, more):
                if p is not None:
                    for j in DN:
                        split(p, j)
                if more:
                    split(i + 1, GU[0])
                    split(i + 1, GU[1])
                if p is not None:
                    turn_h(p)
                if more:
                    split(i + 1, GU[2])
                act.wait_ge(used[GU[-1]], i + 1)
                if p is not None:
                    act.wait_ge(hs_done, i)
                act.activation(sg[:], G, ACT.Silu).then_inc(sg_done, 1)
                if more:
                    split(i + 1, GU[3])
                    turn_x(i + 1)

            turn_x(0)
            for j in GU:
                split(0, j)
            last = turns(act, turn)
            for j in DN:
                split(last, j)
            turn_h(last)

        @block.tensor
        def _(pe):
            def turn_x(i):
                pe.wait_ge(xg_in, 16 * (i + 1))
                xs = xg[:].rearrange("p (m k) -> p k m", k=KD)
                for k in range(KD):
                    mm = pe.transpose(XT[:, k * P:(k + 1) * P], xs[:, k, :], ident[:])
                mm.then_inc(xt_done, 1)

            def turn_h(i):
                pe.wait_ge(hs_done, i + 1)
                hk = hs[:].rearrange("p (m k) -> p k m", k=KF)
                for k in range(KF):
                    mm = pe.transpose(HT[:, k * P:(k + 1) * P], hk[:, k, :], ident[:])
                mm.then_inc(ht_done, 1)

            def down(i, more=0):
                pe.wait_ge(ht_lo, i + 1)
                if not is_first(i):
                    pe.wait_ge(y_done, i)
                for j in DN:
                    if j == DN[-1] and more:
                        turn_x(i + 2)
                    pe.wait_ge(lo[j], i + 1)
                    for k in (2 * (j - DN[0]), 2 * (j - DN[0]) + 1):
                        for half in range(2):
                            w = slice(k * D + 512 * half, k * D + 512 * half + 512)
                            mm = product(pe, Y[:, 512 * half:512 * half + 512], (hTh[:, k, :], hTl[:, k, :]),
                                         (Wh[:, DOWN, w], Wl[:, DOWN, w]), k == 0, k == KF - 1)
                    mm.then_inc(used[j], 1)

            def turn(i, p, more):
                pe.wait_ge(xt_lo, i + 1)
                if p is not None:
                    pe.wait_ge(hs_done, i)
                for j in GU:
                    pe.wait_ge(lo[j], i + 1)
                    for k in (2 * j, 2 * j + 1):
                        x = (xTh[:, k, :], xTl[:, k, :])
                        for out, m in ((G, GATE), (U, UP)):
                            cols = slice(k * DE, (k + 1) * DE)
                            mm = product(pe, out, x, (Wh[:, m, cols], Wl[:, m, cols]), k == 0, k == KD - 1)
                    mm.then_inc(used[j], 1)
                    if j == GU[1] and p is not None:
                        turn_h(p)
                if p is None:
                    turn_x(i + 1)
                else:
                    down(p, more)

            pe.wait_ge(const_in, 16)
            turn_x(0)
            last = turns(pe, turn)
            turn_h(last)
            down(last)

        @block.vector
        def _(dve):
            def split(i, j):
                if j not in BY_POOL:
                    split_lo(dve, i, j)

            def turn_x(i):
                dve.wait_ge(xt_hi, i + 1)
                dve.tensor_tensor(xTl[:], tiles(XT[:]), xTh[:].bitcast(F32), ALU.subtract).then_inc(xt_lo, 1)

            def turn_h(i):
                dve.wait_ge(ht_hi, i + 1)
                dve.tensor_tensor(hTl[:], tiles(HT[:]), hTh[:].bitcast(F32), ALU.subtract).then_inc(ht_lo, 1)

            def store(i):
                dve.wait_ge(used[DN[-1]], i + 1)
                if not is_first(i):
                    dve.wait_ge(y_out, 16 * i)
                dve.tensor_copy(y[:], Y[:]).then_inc(y_done, 1)

            def turn(i, p, more):
                if p is not None:
                    for j in DN:
                        split(p, j)
                if more:
                    split(i + 1, GU[0])
                    split(i + 1, GU[1])
                if p is not None:
                    turn_h(p)
                if more:
                    split(i + 1, GU[2])
                if p is not None:
                    dve.wait_ge(ht_done, i)
                dve.wait_ge(sg_done, i + 1)
                dve.tensor_tensor(hs[:], U, sg[:], ALU.mult).then_inc(hs_done, 1)
                if more:
                    split(i + 1, GU[3])
                    turn_x(i + 1)
                if p is not None:
                    store(p)

            turn_x(0)
            for j in GU:
                split(0, j)
            last = turns(dve, turn)
            for j in DN:
                split(last, j)
            turn_h(last)
            store(last)


def phase_f(c, d, dest, wt):
    nc = c.nc
    with ExitStack() as st:
        B = 2
        hb = sbuf(nc, st, "f_h", [P, B, D])
        y1 = sbuf(nc, st, "f_y1", [P, B, D])
        y2 = sbuf(nc, st, "f_y2", [P, B, D])
        h_in = [c.sem(f"f_h_in{i}") for i in range(B)]
        y_in = [c.sem(f"f_y_in{i}") for i in range(2 * B)]
        out = [c.sem(f"f_out{i}") for i in range(B)]
        half, done = c.sem("f_half"), c.sem("f_done")
        block = st.enter_context(nc.Block())

        @block.sync
        def _(sp):
            def load(t):
                if t >= B:
                    sp.wait_ge(out[t % B], 16 * (t // B))
                sp.dma_start(hb[:, t % B, :], d["h"][t * P:(t + 1) * P, :]).then_inc(h_in[t % B], 16)

            load(0)
            for t in range(NT):
                if t + 1 < NT:
                    load(t + 1)
                sp.wait_ge(done, t + 1)
                sp.dma_start(d["out"][t * P:(t + 1) * P, :], hb[:, t % B, :]).then_inc(out[t % B], 16)
            for i in range(B):
                sp.wait_ge(out[i], 16 * (NT // B))

        @block.gpsimd
        def _(pool):
            for t in range(NT):
                if t >= B:
                    pool.wait_ge(done, t - B + 1)
                for j, y in enumerate((y1, y2)):
                    pool.indirect_dma_start(out=y[:, t % B, :], out_offset=None, in_=d["y"],
                                            in_offset=bass.IndirectOffsetOnAxis(ap=dest[:, j, t:t + 1], axis=0)
                                            ).then_inc(y_in[B * j + t % B], 16)

        @block.vector
        def _(dve):
            for t in range(NT):
                b = t % B
                dve.wait_ge(h_in[b], 16 * (t // B + 1))
                dve.wait_ge(y_in[b], 16 * (t // B + 1))
                dve.scalar_tensor_tensor(hb[:, b, :], y1[:, b, :], wt[:, 0, t:t + 1], hb[:, b, :], ALU.mult, ALU.add).then_inc(half, 1)
                dve.wait_ge(half, t + 1)
                dve.wait_ge(y_in[B + b], 16 * (t // B + 1))
                dve.scalar_tensor_tensor(hb[:, b, :], y2[:, b, :], wt[:, 1, t:t + 1], hb[:, b, :], ALU.mult, ALU.add).then_inc(done, 1)



def constants():
    n = np.arange(P, dtype=np.float64)[:, None]
    gamma = 1.0 - np.exp2(-5.0 - np.arange(BH, dtype=np.float64))
    half = HD // 2
    return {
        "ident": np.eye(P, dtype=np.float32),
        "tri": (np.arange(P)[:, None] <= np.arange(P)[None, :]).astype(np.float32),
        "decay": np.concatenate([gamma ** n, gamma ** -n * HD ** -0.5], axis=1).astype(np.float32),
        "decay_tile": np.repeat((gamma ** P).reshape(BH // 2, 2).T, HD, axis=0).astype(np.float32),
        "before": (np.arange(P)[:, None] < np.arange(P)[None, :]).astype(np.float32),
        "token": np.arange(SEQ, dtype=np.int32).reshape(NT, P).T,
        "route_tab": np.concatenate([np.arange(NE) // EG, np.arange(NE), CAP * np.arange(1, 9), np.arange(FULL)]).astype(np.float32),
        "inv_freq": (np.float32(10000.0) ** (-np.arange(half, dtype=np.float32) / np.float32(half))).astype(np.float32),
    }




SCRATCH = {
    "ext_dram": ((AH, EXT), F32),
    "mix": ((SEQ, D), F32),
    "h": ((SEQ, D), F32),
    "hn": ((SEQ, D), F32),
    "row_token": ((BLOCKS * P, 1), I32),
    "y": ((BLOCKS * P, D), F32),
}


def build(nc, d):
    with ExitStack() as ctx:
        c = Core(nc, ctx)
        c.bank2 = [c.psum(f"pair{i}", 2) for i in range(3)]
        c.bank = [c.psum(f"bank{i}") for i in range(2)]
        phase_a(c, d)
        c.reuse_sems()
        phase_bc(c, d)
        c.reuse_sems()
        lg = sbuf(nc, ctx, "logits", [P, NT, NLG])
        dest = sbuf(nc, ctx, "dest", [P, 2, NT], U32)
        wt = sbuf(nc, ctx, "weight", [P, 2, NT])
        btab = sbuf(nc, ctx, "block_expert", [P, BLOCKS + 1], I32)
        ids = sbuf(nc, ctx, "row_ids", [P, BLOCKS], I32)
        phase_o(c, d, lg)
        phase_r(c, d, lg, dest, wt, btab, ids)
        c.reuse_sems()
        phase_e(c, d, btab, ids)
        phase_f(c, d, dest, wt)


def kernel(**inputs):
    import numpy as _np
    import concourse.bacc as _bacc
    from concourse.bass_utils import run_bass_kernel_spmd as _run

    arrays = {name: _np.asarray(a) for name, a in inputs.items()}
    arrays["x"], arrays["mem"] = arrays["x"][0], arrays["mem"][0]
    arrays["positions"] = arrays["positions"][0].reshape(NT, P).T
    arrays.update(constants())
    arrays = {name + "_dram": _np.ascontiguousarray(a) for name, a in arrays.items()}
    nc = _bacc.Bacc("TRN2", target_bir_lowering=False, num_devices=1)
    args = {name[:-5]: nc.dram_tensor(name, a.shape, mybir.dt.from_np(a.dtype), kind="ExternalInput").ap()
            for name, a in arrays.items()}
    args["out"] = nc.dram_tensor("out_dram", (SEQ, D), F32, kind="ExternalOutput").ap()
    for name, (shape, dt) in SCRATCH.items():
        args[name] = nc.dram_tensor(name + "_dram", shape, dt, kind="Internal").ap()
    build(nc, args)
    return _run(nc, [arrays], core_ids=[0]).results[0]["out_dram"][None]
```

```python
from contextlib import ExitStack

import numpy as np

import concourse.bass as bass
from concourse import mybir

F32 = mybir.dt.float32
F32R = mybir.dt.float32r
I32 = mybir.dt.int32
U32 = mybir.dt.uint32
BF16 = mybir.dt.bfloat16
ALU = mybir.AluOpType
ACT = mybir.ActivationFunctionType
AX = mybir.AxisListType

P = 128
D = 1024
SEQ = 1024
NT = SEQ // P
KD = D // P
HD = 64
AH, BH, CH = 8, 4, 4
AW, BW, CW = AH * HD, BH * HD, CH * HD
COLS = 3 * AW + 4 * BW + CW
BC0 = 3 * AW
BCW = COLS - BC0
N_MEM = 256
MT = N_MEM // P
CHUNK = 64
LEFT = 8
WIN = (LEFT * CHUNK) // P + 1
KEEP = WIN + 1
MAX_REL = 128
REL = MAX_REL + CHUNK
EXT = 2 * P + P - 1
NG, EG = 4, 8
NE = NG * EG
DE = D // 2
EPS = 1e-6
NEG = -1e30


class Steps:

    def __init__(self, eng, sem, base=0):
        self.eng, self.sem, self.base, self.n = eng, sem, base, 0

    def __call__(self, ins):
        self.n += 1
        ins.then_inc(self.sem, 1)
        self.eng.wait_ge(self.sem, self.base + self.n)


class Core:

    def __init__(self, nc, ctx):
        self.nc, self.ctx = nc, ctx

        self.sems = []

    def sem(self, name):
        self.sems.append(self.nc.alloc_semaphore(name=name))
        return self.sems[-1]

    def reuse_sems(self):
        self.nc.clear_and_free_semaphores(self.sems)
        self.nc.all_engine_barrier()
        self.sems = []

    def psum(self, name, banks=1):
        return self.ctx.enter_context(self.nc.psum_tensor(name, [P, 512 * banks], F32))


def sbuf(nc, stack, name, shape, dt=F32):
    return stack.enter_context(nc.sbuf_tensor(name, shape, dt))


def rows(ap, k):
    return ap.rearrange("(p k) n -> p k n", k=k)


def split_weights(c, name, src, gain, hi, lo, k_tiles, width):
    nc = c.nc
    with ExitStack() as st:
        SLOTS = 4
        raw = sbuf(nc, st, f"{name}_raw", [P, SLOTS, width])
        loaded = [c.sem(f"{name}_loaded{i}") for i in range(SLOTS)]
        gained = c.sem(f"{name}_gained")
        hi_done, lo_done = c.sem(f"{name}_hi"), c.sem(f"{name}_lo")
        g = None
        if gain is not None:
            g = sbuf(nc, st, f"{name}_g", [P, k_tiles])
        block = st.enter_context(nc.Block())

        @block.sync
        def _(sp):
            if g is not None:
                sp.dma_start(g[:], gain.rearrange("(p k) -> p k", k=k_tiles)).then_inc(gained, 16)
            for k in range(k_tiles):
                if k >= SLOTS:
                    sp.wait_ge(lo_done, k - SLOTS + 1)
                sp.dma_start(raw[:, k % SLOTS, :], src[:, k, :]).then_inc(loaded[k % SLOTS], 16)

        @block.scalar
        def _(act):
            if g is not None:
                act.wait_ge(gained, 16)
            for k in range(k_tiles):
                act.wait_ge(loaded[k % SLOTS], 16 * (k // SLOTS + 1))
                act.activation(hi[:, k, :], raw[:, k % SLOTS, :], ACT.Copy,
                               scale=1.0 if g is None else g[:, k:k + 1]).then_inc(hi_done, 1)

        @block.vector
        def _(dve):
            for k in range(k_tiles):
                dve.wait_ge(hi_done, k + 1)
                if g is None:
                    dve.tensor_tensor(lo[:, k, :], raw[:, k % SLOTS, :], hi[:, k, :].bitcast(F32),
                                      ALU.subtract).then_inc(lo_done, 1)
                else:
                    dve.scalar_tensor_tensor(lo[:, k, :], raw[:, k % SLOTS, :], g[:, k:k + 1],
                                             hi[:, k, :].bitcast(F32), ALU.mult,
                                             ALU.subtract).then_inc(lo_done, 1)


def product(pe, out, a, b, first=True, last=True):
    (ah, al), (bh, bl) = a, b
    pe.matmul(out, ah, bh, start=first, stop=False, skip_group_check=True)
    pe.matmul(out, ah, bl, start=False, stop=False, skip_group_check=True)
    return pe.matmul(out, al, bh, start=False, stop=last, skip_group_check=True)


class Filled:

    def __init__(self, c, name, fills, by_dve, by_act=None):
        self.fills, self.by_dve = fills, by_dve
        self.by_act = list(range(fills)) if by_act is None else by_act
        self.full, self.hi, self.lo = c.sem(f"{name}_full"), c.sem(f"{name}_hi"), c.sem(f"{name}_lo")

    def wait_full(self, eng, t, f):
        eng.wait_ge(self.full, self.fills * t + f + 1)

    def wait_hi(self, eng, t, f):
        eng.wait_ge(self.hi, len(self.by_act) * t + self.by_act.index(f) + 1)

    def wait_free(self, eng, t, f):
        if f in self.by_dve:
            eng.wait_ge(self.lo, len(self.by_dve) * t + self.by_dve.index(f) + 1)
        else:
            self.wait_hi(eng, t, f)

    def wait_before(self, eng, t, f, first):
        if f:
            self.wait_free(eng, t, f - 1)
        elif not first:
            self.wait_free(eng, t - 1, self.fills - 1)


def wait_apart(eng, sem, value, passed):
    eng.wait_ge(sem, value)
    eng.sem_inc(passed, 1)


def heads(ap):
    return ap.rearrange("p (h e) -> p h e", e=HD)


def tiles(ap):
    return ap.rearrange("p (k n) -> p k n", n=P)


def wide(ap, n):
    return ap.unsqueeze(2).to_broadcast([ap.shape[0], ap.shape[1], n])


class Weights:

    def __init__(self, c, st, name, src, gain, width, slots):
        self.src, self.gain, self.slots = src, gain, slots
        self.raw = sbuf(c.nc, st, f"{name}_raw", [P, slots, width])
        self.h = sbuf(c.nc, st, f"{name}_wh", [P, KD, width], F32R)
        self.l = sbuf(c.nc, st, f"{name}_wl", [P, KD, width], F32R)
        self.loaded = [c.sem(f"{name}_w_loaded{i}") for i in range(slots)]
        self.hi, self.lo = c.sem(f"{name}_w_hi"), c.sem(f"{name}_w_lo")
        self.g, self.gained = sbuf(c.nc, st, f"{name}_w_g", [P, KD]), c.sem(f"{name}_w_gained")

    def load(self, sp, ks):
        for k in ks:
            if k == 0:
                sp.dma_start(self.g[:], self.gain.rearrange("(p k) -> p k", k=KD)).then_inc(self.gained, 16)
            if k >= self.slots:
                sp.wait_ge(self.lo, k - self.slots + 1)
            sp.dma_start(self.raw[:, k % self.slots, :], self.src[:, k, :]).then_inc(self.loaded[k % self.slots], 16)

    def split_hi(self, act, k):
        if k == 0:
            act.wait_ge(self.gained, 16)
        act.wait_ge(self.loaded[k % self.slots], 16 * (k // self.slots + 1))
        act.activation(self.h[:, k, :], self.raw[:, k % self.slots, :], ACT.Copy, scale=self.g[:, k:k + 1]).then_inc(self.hi, 1)

    def split_lo(self, dve, k):
        dve.wait_ge(self.hi, k + 1)
        dve.scalar_tensor_tensor(self.l[:, k, :], self.raw[:, k % self.slots, :], self.g[:, k:k + 1],
                                 self.h[:, k, :].bitcast(F32), ALU.mult, ALU.subtract).then_inc(self.lo, 1)


def phase_a(c, d):
    nc = c.nc
    with ExitStack() as st:
        W = Weights(c, st, "a", rows(d["w_in"], KD)[:, :, 0:3 * AW], d["mix_norm_g"], 3 * AW, 4)
        NP = AH // 2
        t_ = lambda name, shape, dt=F32: sbuf(nc, st, "a_" + name, shape, dt)
        kT, V = t_("kt", [P, NP, KEEP * P]), t_("v", [P, KEEP, AW])
        bias, ext, rev = t_("bias", [P, AH, 2 * P]), t_("ext", [AH, EXT]), t_("rev", [AH, REL])
        xb = t_("x", [P, 2, D])
        xTh, xTl = t_("xth", [P, KD, P], F32R), t_("xtl", [P, KD, P], F32R)
        qT = t_("qt", [P, 2, NP, P])
        qk, qkn, sq = t_("qk", [P, 2, AW]), t_("qkn", [P, 2, AW]), t_("sq", [P, AW])
        junk = t_("junk", [P, D], BF16)
        Pr, PTs = t_("p", [P, 2, WIN * P]), t_("pt", [P, 2, WIN * P])
        ident = t_("ident", [P, P])
        gq, gk, gq8, mhalf = t_("gq", [P, 1]), t_("gk", [P, 1]), t_("gq8", [P, 1]), t_("mhalf", [P, AH])
        ssx, msx, rx = t_("ssx", [P, NT]), t_("msx", [P, 1]), t_("rx", [P, NT])
        ssh, msh, rh = t_("ssh", [P, 2, AH]), t_("msh", [P, 2, AH]), t_("rh", [P, 2, AH])
        nmax, rs, rinv = t_("nmax", [P, 2]), t_("rs", [P, 2, AH]), t_("rinv", [P, AH])
        mixt = t_("mix", [P, 2, AW])

        S = [c.bank2[0], c.bank2[1]]
        PT = c.bank2[2]
        O, PJ = c.bank[0], c.bank[1]

        XT0, XT1, Q, K, V_, QT, KT = range(7)
        pj = Filled(c, "a_pj", 7, [XT0, XT1, KT], [XT0, XT1, Q, K, V_, QT])
        s_ = lambda name: c.sem("a_" + name)
        const_in, rev_in, ext_out, bias_in = map(s_, ("const_in", "rev_in", "ext_out", "bias_in"))
        x_in = [s_(f"x_in{i}") for i in range(2)]
        mix_out = [s_(f"mix_out{i}") for i in range(2)]
        pool_const, ext_set, gq8_set = map(s_, ("pool_const", "ext_set", "gq8_set"))
        ssx_done, msx_done, rx_done = map(s_, ("ssx_done", "msx_done", "rx_done"))
        sq_done, ssh_done, msh_done, rh_done, qkn_done = map(s_, ("sq_done", "ssh_done", "msh_done", "rh_done", "qkn_done"))
        s_done, biased, max_done, exp_done, pt_done, ptc_done, pv_done = map(
            s_, ("s_done", "biased", "max_done", "exp_done", "pt_done", "ptc_done", "pv_done"))
        rinv_done, mix_done = s_("rinv_done"), s_("mix_done")
        block = st.enter_context(nc.Block())
        N = NT * AH
        CONSTS = 16 * 5

        def nblk(t):
            return min(t, WIN - 1) + 1

        PIECES = [[XT0, XT1], [Q], [K], [(V_, 0)], [(V_, 1)], [QT], [KT], []]

        def whole(h):
            return [f[0] if isinstance(f, tuple) else f for f in PIECES[h] if f != (V_, 0)]

        @block.sync
        def _(sp):
            sp.dma_start(xb[:, 0, :], d["x"][0:P, :]).then_inc(x_in[0], 16)
            sp.dma_start(ident[:], d["ident"]).then_inc(const_in, 16)
            W.load(sp, [0])
            for half in range(2):
                sp.dma_start(gq[64 * half:64 * half + 64, :], d["qn_a"].rearrange("(p a) -> p a", a=1)).then_inc(const_in, 16)
                sp.dma_start(gk[64 * half:64 * half + 64, :], d["kn_a"].rearrange("(p a) -> p a", a=1)).then_inc(const_in, 16)
            W.load(sp, [1])
            sp.dma_start(rev[:], d["rel_bias"]).then_inc(rev_in, 16)
            W.load(sp, range(2, KD))
            sp.wait_ge(ext_set, 1)
            sp.dma_start(d["ext_dram"], ext[:]).then_inc(ext_out, 16)
            sp.wait_ge(ext_out, 16)
            toeplitz = bass.AP(d["ext_dram"].tensor, 0, [[1, P], [EXT, AH], [1, 2 * P]])
            sp.dma_start(bias[:], toeplitz).then_inc(bias_in, 16)

            def store(t):
                sp.wait_ge(mix_done, t + 1)
                sp.dma_start(d["mix"][t * P:(t + 1) * P, 0:AW], mixt[:, t % 2, :]).then_inc(mix_out[t % 2], 16)

            for t in range(1, NT):
                if t >= 2:
                    sp.wait_ge(ssx_done, t - 1)
                    pj.wait_full(sp, t - 2, XT1)
                sp.dma_start(xb[:, t % 2, :], d["x"][t * P:(t + 1) * P, :]).then_inc(x_in[t % 2], 16)
                if t >= 2:
                    store(t - 2)
            store(NT - 2)
            store(NT - 1)
            for i in range(2):
                sp.wait_ge(mix_out[i], 16 * (NT // 2))

        @block.gpsimd
        def _(pool):
            pool.memset(mhalf[:], -0.5).then_inc(pool_const, 1)
            pool.wait_ge(pool_const, 1)

            def x_scale(t):
                pool.wait_ge(ssx_done, t + 1)
                pool.tensor_scalar(msx[:], ssx[:, t:t + 1], 1.0 / D, EPS, ALU.mult, ALU.add).then_inc(msx_done, 1)
                pool.wait_ge(msx_done, t + 1)
                pool.tensor_tensor(rx[:, t:t + 1], msx[:], mhalf[:, 0:1], ALU.pow).then_inc(rx_done, 1)

            def head_scale(t, i):
                n = 2 * t + i + 1
                pj.wait_hi(pool, t, Q + i)
                if n >= 2:
                    pool.wait_ge(ssh_done, n - 1)
                pool.tensor_tensor(sq[:], qk[:, i, :], qk[:, i, :], ALU.mult).then_inc(sq_done, 1)
                pool.wait_ge(ssh_done, n)
                pool.tensor_scalar(msh[:, i, :], ssh[:, i, :], 1.0 / HD, EPS, ALU.mult, ALU.add).then_inc(msh_done, 1)
                pool.wait_ge(msh_done, n)
                pool.tensor_tensor(rh[:, i, :], msh[:, i, :], mhalf[:], ALU.pow).then_inc(rh_done, 1)

            for t in range(NT):
                x_scale(t)
                head_scale(t, 0)
                head_scale(t, 1)

        @block.scalar
        def _(act):
            def sum_squares(t):
                act.wait_ge(x_in[t % 2], 16 * (t // 2 + 1))
                if t:
                    act.wait_ge(ssx_done, t)
                act.activation(junk[:], xb[:, t % 2, :], ACT.Square, accum_out=ssx[:, t:t + 1]).then_inc(ssx_done, 1)

            def take(t, f):
                if f not in pj.by_act:
                    return
                pj.wait_full(act, t, f)
                if f in (XT0, XT1):
                    i = act.activation(xTh[:, 4 * f:4 * f + 4, :], tiles(PJ[:]), ACT.Copy)
                elif f in (Q, K):
                    act.wait_ge(rx_done, t + 1)
                    i = act.activation(qk[:, f - Q, :], PJ[:], ACT.Copy, scale=rx[:, t:t + 1])
                elif f == V_:
                    i = act.activation(V[:, t % KEEP, :], PJ[:], ACT.Copy, scale=rx[:, t:t + 1])
                else:
                    i = act.activation(qT[:, t % 2], tiles(PJ[:]), ACT.Copy, scale=gq8[:])
                i.then_inc(pj.hi, 1)

            def exps(n):
                t, h = divmod(n, AH)
                w = nblk(t) * P
                act.wait_ge(max_done, n + 1)
                if n >= 2:
                    act.wait_ge(pt_done, n - 1)
                act.activation(Pr[:, n % 2, 0:w], S[n % 2][:, 640 - w:640], ACT.Exp, bias=nmax[:, n % 2:n % 2 + 1],
                               accum_out=rs[:, t % 2, h:h + 1]).then_inc(exp_done, 1)

            def turned(n):
                w = nblk(n // AH) * P
                act.wait_ge(pt_done, n + 1)
                if n >= 2:
                    act.wait_ge(pv_done, n - 1)
                act.activation(PTs[:, n % 2, 0:w], PT[:, 0:w], ACT.Copy).then_inc(ptc_done, 1)

            take(0, XT0)
            W.split_hi(act, 0)
            take(0, XT1)
            for k in range(1, KD):
                W.split_hi(act, k)
                if k == 2:
                    sum_squares(0)
            act.wait_ge(gq8_set, 1)
            for f in range(Q, KT):
                take(0, f)
            sum_squares(1)
            exps(0)
            for t in range(NT):
                for h in range(AH):
                    n = t * AH + h
                    turned(n)
                    if n + 1 < N:
                        exps(n + 1)
                    for f in whole(h):
                        if t + 1 < NT:
                            take(t + 1, f)
                    if h == AH - 1 and t + 2 < NT:
                        sum_squares(t + 2)

        @block.tensor
        def _(pe):
            def fill(t, f):
                f, part = f if isinstance(f, tuple) else (f, None)
                if part != 1:
                    pj.wait_before(pe, t, f, t == 0)
                if f in (XT0, XT1):
                    pe.wait_ge(x_in[t % 2], 16 * (t // 2 + 1))
                    xs = xb[:, t % 2, :].rearrange("p (m k) -> p k m", k=KD)
                    for j in range(4):
                        mm = pe.transpose(PJ[:, j * P:(j + 1) * P], xs[:, 4 * f + j, :], ident[:])
                elif f in (Q, K, V_):
                    cols = slice((f - Q) * AW, (f - Q + 1) * AW)
                    for k in range(KD) if part is None else range(4 * part, 4 * part + 4):
                        if t == 0 and f == Q:
                            pe.wait_ge(W.lo, k + 1)
                        mm = product(pe, PJ[:], (xTh[:, k, :], xTl[:, k, :]), (W.h[:, k, cols], W.l[:, k, cols]),
                                     k == 0, k == KD - 1)
                else:
                    pe.wait_ge(qkn_done, 2 * t + f - QT + 1)
                    for p in range(NP):
                        mm = pe.transpose(PJ[:, p * P:(p + 1) * P], qkn[:, f - QT, p * P:(p + 1) * P], ident[:])
                if part != 0:
                    mm.then_inc(pj.full, 1)

            def runs(t):
                out = []
                for kt in range(t + 1 - nblk(t), t + 1):
                    at = WIN - (t + 1 - kt)
                    if out and kt % KEEP and at != 4:
                        out[-1][2] += 1
                    else:
                        out.append([kt % KEEP, at, 1])
                return out

            def scores(n):
                t, h = divmod(n, AH)
                p, r = h // 2, slice(64 * (h % 2), 64 * (h % 2) + 64)
                if h == 0:
                    pj.wait_free(pe, t, KT)
                if n >= 2:
                    pe.wait_ge(exp_done, n - 1)
                for slot, at, length in runs(t):
                    mm = pe.matmul(S[n % 2][:, at * P:(at + length) * P], qT[r, t % 2, p, :],
                                   kT[r, p, slot * P:(slot + length) * P], start=True, stop=True)
                mm.then_inc(s_done, 1)

            def turn(n):
                pe.wait_ge(exp_done, n + 1)
                if n >= 1:
                    pe.wait_ge(ptc_done, n)
                for b in range(nblk(n // AH)):
                    mm = pe.transpose(PT[:, b * P:(b + 1) * P], Pr[:, n % 2, b * P:(b + 1) * P], ident[:])
                mm.then_inc(pt_done, 1)

            def values(n):
                t, h = divmod(n, AH)
                pe.wait_ge(ptc_done, n + 1)
                if h == 0 and t >= 1:
                    pe.wait_ge(mix_done, t)
                cols, last = slice(h * HD, (h + 1) * HD), nblk(t) - 1
                for b in range(last + 1):
                    mm = pe.matmul(O[:, cols], PTs[:, n % 2, b * P:(b + 1) * P], V[:, (t - last + b) % KEEP, cols],
                                   start=b == 0, stop=b == last, skip_group_check=True)
                mm.then_inc(pv_done, 1)

            pe.wait_ge(const_in, CONSTS)
            for f in range(7):
                fill(0, f)
            scores(0)
            scores(1)
            for t in range(NT):
                for h in range(AH):
                    n = t * AH + h
                    turn(n)
                    for f in PIECES[h]:
                        if t + 1 < NT:
                            fill(t + 1, f)
                    if n:
                        values(n - 1)
                    if n + 2 < N:
                        scores(n + 2)
            values(N - 1)

        @block.vector
        def _(dve):
            own = Steps(dve, c.sem("a_dve"))

            def take(t, f):
                slot = t % KEEP
                if f in (XT0, XT1):
                    pj.wait_hi(dve, t, f)
                    dve.tensor_tensor(xTl[:, 4 * f:4 * f + 4, :], tiles(PJ[:]), xTh[:, 4 * f:4 * f + 4, :].bitcast(F32),
                                      ALU.subtract).then_inc(pj.lo, 1)
                elif f == KT:
                    pj.wait_full(dve, t, f)
                    dve.tensor_scalar(kT[:, :, slot * P:(slot + 1) * P], tiles(PJ[:]), gk[:], None, ALU.mult).then_inc(pj.lo, 1)

            def head_sums(t, i):
                dve.wait_ge(sq_done, 2 * t + i + 1)
                dve.tensor_reduce(ssh[:, i, :], heads(sq[:]), AX.X, ALU.add).then_inc(ssh_done, 1)

            def head_norm(t, i):
                dve.wait_ge(rh_done, 2 * t + i + 1)
                dve.tensor_tensor(heads(qkn[:, i, :]), heads(qk[:, i, :]), wide(rh[:, i, :], HD), ALU.mult).then_inc(qkn_done, 1)

            def maxes(n):
                t, h = divmod(n, AH)
                w = nblk(t) * P
                s = S[n % 2]
                dve.wait_ge(s_done, n + 1)
                if n >= 2:
                    dve.wait_ge(exp_done, n - 1)
                if t == 0:
                    ins = dve.tensor_tensor(s[:, 512:640], s[:, 512:640], bias[:, h, P - 1::-1], ALU.add)
                else:
                    ins = dve.tensor_tensor(s[:, 384:640], s[:, 384:640], bias[:, h, ::-1], ALU.add)
                if nblk(t) == WIN:
                    ins = dve.tensor_scalar(s[64:128, 0:64], s[64:128, 0:64], NEG, None, ALU.add)
                ins.then_inc(biased, 1)
                dve.wait_ge(biased, n + 1)
                dve.tensor_reduce(nmax[:, n % 2:n % 2 + 1], s[:, 640 - w:640], AX.X, ALU.max, negate=True).then_inc(max_done, 1)

            def finish(t):
                dve.wait_ge(exp_done, AH * (t + 1))
                dve.reciprocal(rinv[:], rs[:, t % 2, :]).then_inc(rinv_done, 1)
                dve.wait_ge(rinv_done, t + 1)
                dve.wait_ge(pv_done, AH * (t + 1))
                if t >= 2:
                    dve.wait_ge(mix_out[t % 2], 16 * (t // 2))
                dve.tensor_tensor(heads(mixt[:, t % 2, :]), heads(O[:]), wide(rinv[:], HD), ALU.mult).then_inc(mix_done, 1)

            dve.wait_ge(const_in, CONSTS)
            dve.tensor_scalar(gq8[:], gq[:], HD ** -0.5, None, ALU.mult).then_inc(gq8_set, 1)
            take(0, XT0)
            W.split_lo(dve, 0)
            take(0, XT1)
            for k in range(1, KD):
                W.split_lo(dve, k)
            dve.wait_ge(rev_in, 16)
            dve.memset(ext[:, 0:CHUNK], NEG)
            dve.memset(ext[:, CHUNK + REL:EXT], 0.0)
            dve.tensor_scalar(ext[:, CHUNK:CHUNK + REL], rev[:], rev[:, REL - 1:REL], None, ALU.subtract).then_inc(ext_set, 1)
            for i in range(2):
                head_sums(0, i)
                head_norm(0, i)
            take(0, KT)
            dve.wait_ge(bias_in, 16)
            own(dve.memset(bias[0:64, :, 0:64], NEG))
            maxes(0)
            for t in range(NT):
                for h in range(AH):
                    n = t * AH + h
                    if n + 1 < N:
                        maxes(n + 1)
                    if t + 1 < NT:
                        if h == 2:
                            head_sums(t + 1, 0)
                        elif h == 3:
                            head_norm(t + 1, 0)
                            head_sums(t + 1, 1)
                        elif h == 4:
                            head_norm(t + 1, 1)
                        for f in whole(h):
                            take(t + 1, f)
                    if h == 0 and t:
                        finish(t - 1)
            finish(NT - 1)


TWO_PI = 2 * np.pi
TURN1 = 6.28125
TURN2 = float(np.float32(round((TWO_PI - TURN1) * 2 ** 21) / 2 ** 21))
TURN3 = float(np.float32(TWO_PI - TURN1 - TURN2))
ROUND = 1.5 * 2 ** 23
PI_BELOW = 3.1415925


def phase_m(c, d, kT, V, cos, sin, WB):
    nc = c.nc
    with ExitStack() as st:
        W = Weights(c, st, "m", rows(d["w_mem_kv"], KD), d["mem_norm_g"], 2 * CW, KD)
        mb = sbuf(nc, st, "m_mem", [P, MT, D])
        mTh = sbuf(nc, st, "m_mth", [P, KD, P], F32R)
        mTl = sbuf(nc, st, "m_mtl", [P, KD, P], F32R)
        km = sbuf(nc, st, "m_k", [P, MT, CW])
        kn = sbuf(nc, st, "m_kn", [P, MT, CW])
        sq = sbuf(nc, st, "m_sq", [P, CW])
        junk = sbuf(nc, st, "m_junk", [P, D], BF16)
        ident = sbuf(nc, st, "m_ident", [P, P])
        gk = sbuf(nc, st, "m_gk", [P, 1])
        mhalf = sbuf(nc, st, "m_mhalf", [P, CH])
        ss = sbuf(nc, st, "m_ss", [P, MT])
        ms = sbuf(nc, st, "m_ms", [P, MT])
        r = sbuf(nc, st, "m_r", [P, MT])
        ssh = sbuf(nc, st, "m_ssh", [P, MT, CH])
        msh = sbuf(nc, st, "m_msh", [P, MT, CH])
        rh = sbuf(nc, st, "m_rh", [P, MT, CH])
        pos = sbuf(nc, st, "m_pos", [P, NT], I32)
        posf = sbuf(nc, st, "m_posf", [P, NT])
        inv = sbuf(nc, st, "m_inv", [P, HD // 2])
        ang = sbuf(nc, st, "m_ang", [P, NT, HD // 2])
        turns = sbuf(nc, st, "m_turns", [P, 2, NT, HD // 2])
        rest = sbuf(nc, st, "m_rest", [P, 2, NT, HD // 2])
        PJ = c.bank[1]
        XT0, XT1, KV, KT = range(4)
        pj = Filled(c, "m_pj", 4, [XT0, XT1, KT], [XT0, XT1, KV])
        const_in, mem_in = c.sem("m_const_in"), [c.sem(f"m_mem_in{i}") for i in range(MT)]
        pool_own, ss_done, r_done, sq_done, ssh_done, rh_done, kn_done = (
            c.sem(f"m_{n}") for n in ("pool", "ss_done", "r_done", "sq_done", "ssh_done", "rh_done", "kn_done"))
        angles, sines = c.sem("m_angles"), c.sem("m_sines")
        CONSTS = 16 * 5
        block = st.enter_context(nc.Block())

        @block.sync
        def _(sp):
            for m in range(MT):
                sp.dma_start(mb[:, m, :], d["mem"][m * P:(m + 1) * P, :]).then_inc(mem_in[m], 16)
            sp.dma_start(ident[:], d["ident"]).then_inc(const_in, 16)
            for half in range(2):
                sp.dma_start(gk[64 * half:64 * half + 64, :], d["kn_c"].rearrange("(p a) -> p a", a=1)).then_inc(const_in, 16)
            sp.dma_start(pos[:], d["positions"]).then_inc(const_in, 16)
            sp.dma_start(inv[:], d["inv_freq"].partition_broadcast(P)).then_inc(const_in, 16)
            W.load(sp, range(KD))
            WB.load(sp, range(KD))

        @block.gpsimd
        def _(pool):
            own = Steps(pool, pool_own)
            own(pool.memset(mhalf[:], -0.5))
            for m in range(MT):
                pool.wait_ge(ss_done, m + 1)
                own(pool.tensor_scalar(ms[:, m:m + 1], ss[:, m:m + 1], 1.0 / D, EPS, ALU.mult, ALU.add))
                pool.tensor_tensor(r[:, m:m + 1], ms[:, m:m + 1], mhalf[:, 0:1], ALU.pow).then_inc(r_done, 1)
            for m in range(MT):
                pj.wait_hi(pool, m, KV)
                pool.tensor_tensor(sq[:], km[:, m, :], km[:, m, :], ALU.mult).then_inc(sq_done, 1)
                pool.wait_ge(ssh_done, m + 1)
                own(pool.tensor_scalar(msh[:, m, :], ssh[:, m, :], 1.0 / HD, EPS, ALU.mult, ALU.add))
                pool.tensor_tensor(rh[:, m, :], msh[:, m, :], mhalf[:], ALU.pow).then_inc(rh_done, 1)

        @block.scalar
        def _(act):
            for m in range(MT):
                act.wait_ge(mem_in[m], 16)
                if m:
                    act.wait_ge(ss_done, m)
                act.activation(junk[:], mb[:, m, :], ACT.Square, accum_out=ss[:, m:m + 1]).then_inc(ss_done, 1)
            for m in range(MT):
                for f in (XT0, XT1):
                    pj.wait_full(act, m, f)
                    act.activation(mTh[:, 4 * f:4 * f + 4, :], tiles(PJ[:]), ACT.Copy).then_inc(pj.hi, 1)
                if m == 0:
                    for k in range(KD):
                        W.split_hi(act, k)
                act.wait_ge(r_done, m + 1)
                pj.wait_full(act, m, KV)
                act.activation(km[:, m, :], PJ[:, 0:CW], ACT.Copy, scale=r[:, m:m + 1])
                act.activation(V[:, m, :], PJ[:, CW:2 * CW], ACT.Copy, scale=r[:, m:m + 1]).then_inc(pj.hi, 1)
                for k in range(m * KD // MT, (m + 1) * KD // MT):
                    WB.split_hi(act, k)
            act.wait_ge(angles, 1)
            act.activation(sin[:], rest[:, 0], ACT.Sin).then_inc(sines, 1)
            act.activation(cos[:], rest[:, 1], ACT.Sin).then_inc(sines, 1)

        @block.tensor
        def _(pe):
            pe.wait_ge(const_in, CONSTS)
            for m in range(MT):
                pe.wait_ge(mem_in[m], 16)
                xs = mb[:, m, :].rearrange("p (m k) -> p k m", k=KD)
                for f in (XT0, XT1):
                    pj.wait_before(pe, m, f, m == 0)
                    for j in range(4):
                        mm = pe.transpose(PJ[:, j * P:(j + 1) * P], xs[:, 4 * f + j, :], ident[:])
                    mm.then_inc(pj.full, 1)
                pj.wait_before(pe, m, KV, False)
                for k in range(KD):
                    if m == 0:
                        pe.wait_ge(W.lo, k + 1)
                    mm = product(pe, PJ[:], (mTh[:, k, :], mTl[:, k, :]), (W.h[:, k, :], W.l[:, k, :]), k == 0, k == KD - 1)
                mm.then_inc(pj.full, 1)
                pj.wait_before(pe, m, KT, False)
                pe.wait_ge(kn_done, m + 1)
                for p in range(CH // 2):
                    mm = pe.transpose(PJ[:, p * P:(p + 1) * P], kn[:, m, p * P:(p + 1) * P], ident[:])
                mm.then_inc(pj.full, 1)

        @block.vector
        def _(dve):
            own = Steps(dve, c.sem("m_dve"))

            def transposed(m):
                for f in (XT0, XT1):
                    pj.wait_hi(dve, m, f)
                    dve.tensor_tensor(mTl[:, 4 * f:4 * f + 4, :], tiles(PJ[:]), mTh[:, 4 * f:4 * f + 4, :].bitcast(F32),
                                      ALU.subtract).then_inc(pj.lo, 1)

            transposed(0)
            for k in range(KD):
                W.split_lo(dve, k)
            dve.wait_ge(const_in, CONSTS)
            own(dve.tensor_copy(posf[:], pos[:]))
            own(dve.tensor_tensor(ang[:], wide(posf[:], HD // 2), inv[:].unsqueeze(1).to_broadcast([P, NT, HD // 2]), ALU.mult))
            for i, quarter in enumerate((0.0, 0.25)):
                own(dve.tensor_scalar(turns[:, i], ang[:], 1 / TWO_PI, quarter, ALU.mult, ALU.add))
                own(dve.tensor_scalar(turns[:, i], turns[:, i], ROUND, None, ALU.add))
                own(dve.tensor_scalar(turns[:, i], turns[:, i], -ROUND, None, ALU.add))
                own(dve.scalar_tensor_tensor(rest[:, i], turns[:, i], -TURN1, ang[:], ALU.mult, ALU.add))
                own(dve.scalar_tensor_tensor(rest[:, i], turns[:, i], -TURN2, rest[:, i], ALU.mult, ALU.add))
                own(dve.scalar_tensor_tensor(rest[:, i], turns[:, i], -TURN3, rest[:, i], ALU.mult, ALU.add))
                own(dve.tensor_scalar(rest[:, i], rest[:, i], quarter * TWO_PI, PI_BELOW, ALU.add, ALU.min))
                own(dve.tensor_scalar(rest[:, i], rest[:, i], -PI_BELOW, None, ALU.max))
            dve.sem_inc(angles, 1)
            for m in range(MT):
                if m:
                    transposed(m)
                dve.wait_ge(sq_done, m + 1)
                dve.tensor_reduce(ssh[:, m, :], heads(sq[:]), AX.X, ALU.add).then_inc(ssh_done, 1)
                dve.wait_ge(rh_done, m + 1)
                dve.tensor_tensor(heads(kn[:, m, :]), heads(km[:, m, :]), wide(rh[:, m, :], HD), ALU.mult).then_inc(kn_done, 1)
                pj.wait_full(dve, m, KT)
                dve.tensor_scalar(kT[:, :, m * P:(m + 1) * P], tiles(PJ[:, 0:CW]), gk[:], None, ALU.mult).then_inc(pj.lo, 1)
                for k in range(m * KD // MT, (m + 1) * KD // MT):
                    WB.split_lo(dve, k)


def phase_bc(c, d):
    nc = c.nc
    with ExitStack() as st:
        kTC = sbuf(nc, st, "c_kt", [P, CH // 2, N_MEM])
        VC = sbuf(nc, st, "c_v", [P, MT, CW])
        cos = sbuf(nc, st, "b_cos", [P, NT, HD // 2])
        sin = sbuf(nc, st, "b_sin", [P, NT, HD // 2])
        W = Weights(c, st, "b", rows(d["w_in"], KD)[:, :, BC0:COLS], d["mix_norm_g"], BCW, 4)
        phase_m(c, d, kTC, VC, cos, sin, W)
        t_ = lambda name, shape, dt=F32: sbuf(nc, st, "b_" + name, shape, dt)
        xb = t_("x", [P, 2, D])
        xTh, xTl = t_("xth", [P, KD, P], F32R), t_("xtl", [P, KD, P], F32R)
        junk = t_("junk", [P, D], BF16)
        ident, tri = t_("ident", [P, P]), t_("tri", [P, P])
        dec, g128 = t_("dec", [P, 2 * BH]), t_("g128", [P, BH // 2])
        gng = t_("gng", [P, BW])
        gqc, gqc8 = t_("gqc", [P, 1]), t_("gqc8", [P, 1])
        mhalf = t_("mhalf", [P, CH])
        ssx, msx, rx = t_("ssx", [P, 1]), t_("msx", [P, 1]), t_("rx", [P, 1])
        qk = t_("qk", [P, 2 * BW])
        byc, bys = t_("byc", [P, 2 * BW]), t_("bys", [P, 2 * BW])
        rot, qkr = t_("rot", [P, 2 * BW]), t_("qkr", [P, 2 * BW])
        v = t_("v", [P, BW])
        g, eg, sg = t_("g", [P, BW]), t_("eg", [P, BW]), t_("sg", [P, BW])
        qkT = t_("qkt", [P, BH, P])
        Sm = t_("sm", [P, BH, P])
        R, Rt = t_("r", [P, BH // 2, HD]), t_("rt", [P, BH // 2, HD])
        qc, qcn, sqc = t_("qc", [P, CW]), t_("qcn", [P, CW]), t_("sqc", [P, CW])
        ssc, msc, rc = t_("ssc", [P, CH]), t_("msc", [P, CH]), t_("rc", [P, CH])
        qTC = t_("qtc", [P, CH // 2, P])
        nmax, rs, rinv = t_("nmax", [P, CH]), t_("rs", [P, CH]), t_("rinv", [P, CH])
        Pr = t_("p", [P, CH, N_MEM])
        PTs = t_("pt", [P, CH * N_MEM])
        sm4, mean, ss4, ms4, r4 = (t_(n, [P, BH]) for n in ("sm4", "mean", "ss4", "ms4", "r4"))
        cent, csq, y, yg = (t_(n, [P, BW]) for n in ("cent", "csq", "y", "yg"))
        mixt = t_("mix", [P, BW + CW])

        SC, PT, O = c.bank2[0], c.bank2[1], c.bank2[2]
        SB = PT
        TR, PJ = c.bank[0], c.bank[1]

        def place(h, width, base=0):
            at = (h % 2) * 512 + base + (h // 2) * width
            return slice(at, at + width)

        def by_head(ap, width, base=0):
            return ap.rearrange("p (s c) -> p s c", s=2)[:, :, base:base + 2 * width].rearrange("p s (a e) -> p s a e", a=2)

        def halves(ap):
            return ap.rearrange("p (a s e) -> p s a e", s=2, a=2)

        def halves1(ap):
            return ap.rearrange("p (a s) -> p s a", s=2)

        XT0, XT1, QK, VG, QC = range(5)
        pj = Filled(c, "b_pj", 5, [XT0, XT1])
        QKT, QCT, U = range(3)
        tr = Filled(c, "b_tr", 3, [QCT, U], [QKT])
        s_ = lambda name: c.sem("b_" + name)
        x_in = [s_(f"x_in{i}") for i in range(2)]
        const_in, mix_out, mhalf_set, state0 = map(s_, ("const_in", "mix_out", "mhalf_set", "state0"))
        ssx_done, rx_done, pool_own, dve_own = map(s_, ("ssx_done", "rx_done", "pool", "dve"))
        rotated, qkr_done, sb_done, sm_done = map(s_, ("rotated", "qkr_done", "sb_done", "sm_done"))
        sc_done, max_done, exp_done, pt_done, ptc_done, r_done = map(
            s_, ("sc_done", "max_done", "exp_done", "pt_done", "ptc_done", "r_done"))
        sqc_done, ssc_done, rc_done, qcn_done = map(s_, ("sqc_done", "ssc_done", "rc_done", "qcn_done"))
        o_done, cent_done, csq_done, ss4_done, r4_done, y_done, yg_done, eg_done, sig_done, sg_done, mix_done, o_free = map(
            s_, ("o_done", "cent_done", "csq_done", "ss4_done", "r4_done", "y_done", "yg_done", "eg_done", "sig_done", "sg_done",
                 "mix_done", "o_free"))
        CONSTS = 16 * 7
        block = st.enter_context(nc.Block())

        @block.sync
        def _(sp):
            for t in range(2):
                sp.dma_start(xb[:, t, :], d["x"][t * P:(t + 1) * P, :]).then_inc(x_in[t], 16)
            for dst, src in ((ident, d["ident"]), (tri, d["tri"]), (dec, d["decay"]), (g128, d["decay_tile"])):
                sp.dma_start(dst[:], src).then_inc(const_in, 16)
            sp.dma_start(gng[:], d["ret_gn_g"].partition_broadcast(P)).then_inc(const_in, 16)
            for half in range(2):
                sp.dma_start(gqc[64 * half:64 * half + 64, :], d["qn_c"].rearrange("(p a) -> p a", a=1)).then_inc(const_in, 16)

            def tile(t):
                if t + 2 < NT:
                    sp.wait_ge(ssx_done, t + 1)
                    pj.wait_full(sp, t, XT1)
                    sp.dma_start(xb[:, t % 2, :], d["x"][(t + 2) * P:(t + 3) * P, :]).then_inc(x_in[t % 2], 16)
                sp.wait_ge(mix_done, 2 * t + 2)
                sp.dma_start(d["mix"][bass.ds(t * P, P), AW:D], mixt[:]).then_inc(mix_out, 16)

            for t in range(NT):
                tile(t)
            sp.wait_ge(mix_out, 16 * NT)

        @block.gpsimd
        def _(pool):
            PER = 3
            setup = Steps(pool, mhalf_set)
            setup(pool.memset(mhalf[:], -0.5))
            pool.wait_ge(const_in, CONSTS)

            def scale_x(t, own):
                pool.wait_ge(ssx_done, t + 1)
                own(pool.tensor_scalar(msx[:], ssx[:], 1.0 / D, EPS, ALU.mult, ALU.add))
                pool.tensor_tensor(rx[:], msx[:], mhalf[:, 0:1], ALU.pow).then_inc(rx_done, 1)

            def rotate(t):
                pj.wait_hi(pool, t, QK)
                for out, table in ((byc, cos), (bys, sin)):
                    i = pool.tensor_tensor(heads2(out[:]), heads2(qk[:]), across(table[:, bass.ds(t, 1), :]), ALU.mult)
                i.then_inc(rotated, 1)

            def heads2(ap):
                return ap.rearrange("p (h e) -> p h e", e=HD // 2)

            def across(ap):
                return ap.to_broadcast([P, 4 * BH, HD // 2])

            def scale_qc(t, own):
                pj.wait_hi(pool, t, QC)
                pool.tensor_tensor(sqc[:], qc[:], qc[:], ALU.mult).then_inc(sqc_done, 1)
                pool.wait_ge(ssc_done, t + 1)
                own(pool.tensor_scalar(msc[:], ssc[:], 1.0 / HD, EPS, ALU.mult, ALU.add))
                pool.tensor_tensor(rc[:], msc[:], mhalf[:], ALU.pow).then_inc(rc_done, 1)

            def norm(t, own):
                pool.wait_ge(sig_done, t + 1)
                pool.tensor_tensor(sg[:], g[:], eg[:], ALU.mult).then_inc(sg_done, 1)
                pool.wait_ge(cent_done, t + 1)
                pool.tensor_tensor(csq[:], cent[:], cent[:], ALU.mult).then_inc(csq_done, 1)
                pool.wait_ge(ss4_done, t + 1)
                own(pool.tensor_scalar(ms4[:], ss4[:], 1.0 / HD, EPS, ALU.mult, ALU.add))
                pool.tensor_tensor(r4[:], ms4[:], mhalf[:], ALU.pow).then_inc(r4_done, 1)
                pool.wait_ge(y_done, t + 1)
                pool.tensor_tensor(yg[:], y[:], gng[:], ALU.mult).then_inc(yg_done, 1)

            own = Steps(pool, pool_own)
            scale_x(0, own)
            rotate(0)
            scale_qc(0, own)

            def tile(t, more):
                own = Steps(pool, pool_own, PER * t + 2)
                if more:
                    scale_x(t + 1, own)
                    rotate(t + 1)
                norm(t, own)
                if more:
                    scale_qc(t + 1, own)
                    assert own.n == PER

            for t in range(NT):
                tile(t, t + 1 < NT)

        @block.scalar
        def _(act):
            def sum_squares(t):
                act.wait_ge(x_in[t % 2], 16 * (t // 2 + 1))
                act.activation(junk[:], xb[:, t % 2, :], ACT.Square, accum_out=ssx[:]).then_inc(ssx_done, 1)

            def take(t, f):
                pj.wait_full(act, t, f)
                if f in (XT0, XT1):
                    i = act.activation(xTh[:, 4 * f:4 * f + 4, :], tiles(PJ[:]), ACT.Copy)
                elif f == QK:
                    act.wait_ge(rx_done, t + 1)
                    i = act.activation(qk[:], PJ[:], ACT.Copy, scale=rx[:])
                elif f == VG:
                    act.activation(v[:], PJ[:, 0:BW], ACT.Copy, scale=rx[:])
                    i = act.activation(g[:], PJ[:, BW:2 * BW], ACT.Copy, scale=rx[:])
                else:
                    i = act.activation(qc[:], PJ[:, 0:CW], ACT.Copy, scale=rx[:])
                i.then_inc(pj.hi, 1)

            sum_squares(0)
            for f in range(5):
                take(0, f)

            def tile(t, more):
                tr.wait_full(act, t, QKT)
                act.activation(qkT[:], tiles(TR[:]), ACT.Copy).then_inc(tr.hi, 1)
                if more:
                    act.wait_ge(rx_done, t + 1)
                    sum_squares(t + 1)
                    take(t + 1, XT0)
                    take(t + 1, XT1)
                act.wait_ge(max_done, t + 1)
                for h in range(CH):
                    act.activation(Pr[:, h, :], SC[:, place(h, N_MEM)], ACT.Exp, bias=nmax[:, h:h + 1],
                                   accum_out=rs[:, h:h + 1]).then_inc(exp_done, 1)
                if more:
                    take(t + 1, QK)
                act.activation(eg[:], g[:], ACT.Exp, scale=-1.0).then_inc(eg_done, 1)
                act.wait_ge(pt_done, t + 1)
                act.activation(PTs[:], PT[:], ACT.Copy).then_inc(ptc_done, 1)
                if more:
                    act.wait_ge(sg_done, t + 1)
                    take(t + 1, VG)
                    take(t + 1, QC)

            for t in range(NT):
                tile(t, t + 1 < NT)

        @block.tensor
        def _(pe):
            def fill(t, f, first_tile=False):
                pj.wait_before(pe, t, f, first_tile)
                if f in (XT0, XT1):
                    pe.wait_ge(x_in[t % 2], 16 * (t // 2 + 1))
                    xs = xb[:, t % 2, :].rearrange("p (m k) -> p k m", k=KD)
                    for j in range(4):
                        mm = pe.transpose(PJ[:, j * P:(j + 1) * P], xs[:, 4 * f + j, :], ident[:])
                else:
                    at, n = (f - QK) * 2 * BW, CW if f == QC else 2 * BW
                    for k in range(KD):
                        mm = product(pe, PJ[:, 0:n], (xTh[:, k, :], xTl[:, k, :]),
                                     (W.h[:, k, at:at + n], W.l[:, k, at:at + n]), k == 0, k == KD - 1)
                mm.then_inc(pj.full, 1)

            def half(h):
                return slice(64 * (h % 2), 64 * (h % 2) + 64)

            def tile(t, more, first):
                tr.wait_before(pe, t, QKT, first)
                pe.wait_ge(qkr_done, t + 1)
                for j in range(4):
                    mm = pe.transpose(TR[:, j * P:(j + 1) * P], qkr[:, j * P:(j + 1) * P], ident[:])
                mm.then_inc(tr.full, 1)
                if more:
                    fill(t + 1, XT0)
                    fill(t + 1, XT1)
                pe.wait_ge(qcn_done, t + 1)
                tr.wait_before(pe, t, QCT, False)
                for p in range(CH // 2):
                    mm = pe.transpose(TR[:, p * P:(p + 1) * P], qcn[:, p * P:(p + 1) * P], ident[:])
                mm.then_inc(tr.full, 1)
                if not first:
                    pe.wait_ge(ptc_done, t)
                for h in range(BH):
                    p, r = h // 2, half(h)
                    mm = pe.matmul(SB[:, place(h, P)], qkT[r, 2 + p, :], qkT[r, p, :], start=True, stop=True)
                mm.then_inc(sb_done, 1)
                tr.wait_free(pe, t, QCT)
                for h in range(CH):
                    p, r = h // 2, half(h)
                    mm = pe.matmul(SC[:, place(h, N_MEM)], qTC[r, p, :], kTC[r, p, :], start=True, stop=True)
                mm.then_inc(sc_done, 1)
                if more:
                    fill(t + 1, QK)
                pe.wait_ge(exp_done, CH * (t + 1))
                pe.wait_ge(sm_done, t + 1)
                for h in range(CH):
                    for b in range(MT):
                        j = h * MT + b
                        mm = pe.transpose(PT[:, j * P:(j + 1) * P], Pr[:, h, b * P:(b + 1) * P], ident[:])
                mm.then_inc(pt_done, 1)
                if first:
                    pe.wait_ge(state0, 1)
                else:
                    pe.wait_ge(o_free, t)
                    pe.wait_ge(r_done, t)
                for h in range(BH):
                    p, r, cols = h // 2, half(h), slice(h * HD, (h + 1) * HD)
                    pe.matmul(O[:, place(h, HD)], Sm[:, h, :], v[:, cols], start=True, stop=False, skip_group_check=True)
                    pe.matmul(O[:, place(h, HD)], qkT[r, p, :], R[r, p, :], start=False, stop=True, skip_group_check=True)
                tr.wait_before(pe, t, U, False)
                for p in range(BH // 2):
                    cols = slice(p * P, (p + 1) * P)
                    mm = pe.matmul(TR[:, cols], qkr[:, BW + p * P:BW + (p + 1) * P], v[:, cols], start=True, stop=True)
                mm.then_inc(tr.full, 1)
                if more:
                    fill(t + 1, VG)
                pe.wait_ge(ptc_done, t + 1)
                for h in range(CH):
                    cols = slice(h * HD, (h + 1) * HD)
                    for b in range(MT):
                        j = slice((h * MT + b) * P, (h * MT + b + 1) * P)
                        mm = pe.matmul(O[:, place(h, HD, 2 * HD)], PTs[:, j], VC[:, b, cols], start=b == 0,
                                       stop=b == MT - 1, skip_group_check=True)
                mm.then_inc(o_done, 1)
                if more:
                    fill(t + 1, QC)

            pe.wait_ge(const_in, CONSTS)
            for f in range(5):
                fill(0, f, True)
            for t in range(NT):
                tile(t, t + 1 < NT, t == 0)

        @block.vector
        def _(dve):
            PER = 2
            dve.wait_ge(const_in, CONSTS)
            Steps(dve, s_("gqc8_set"))(dve.tensor_scalar(gqc8[:], gqc[:], HD ** -0.5, None, ALU.mult))
            dve.memset(R[:], 0.0).then_inc(state0, 1)

            def take(t, f):
                pj.wait_hi(dve, t, f)
                dve.tensor_tensor(xTl[:, 4 * f:4 * f + 4, :], tiles(PJ[:]), xTh[:, 4 * f:4 * f + 4, :].bitcast(F32),
                                  ALU.subtract).then_inc(pj.lo, 1)

            def rotate(t):
                dve.wait_ge(rotated, t + 1)
                sides = lambda ap: ap.rearrange("p (h s e) -> p h s e", s=2, e=HD // 2)
                i = dve.tensor_tensor(sides(rot[:])[:, :, 0, :], sides(byc[:])[:, :, 0, :], sides(bys[:])[:, :, 1, :], ALU.subtract)
                i.then_inc(dve_rot, 1)
                i = dve.tensor_tensor(sides(rot[:])[:, :, 1, :], sides(bys[:])[:, :, 0, :], sides(byc[:])[:, :, 1, :], ALU.add)
                i.then_inc(dve_rot, 1)
                dve.wait_ge(dve_rot, 2 * t + 2)
                dve.tensor_tensor(heads(qkr[:]), heads(rot[:]), wide(dec[:], HD), ALU.mult).then_inc(qkr_done, 1)

            def scale_qc(t):
                dve.wait_ge(sqc_done, t + 1)
                dve.tensor_reduce(ssc[:], heads(sqc[:]), AX.X, ALU.add).then_inc(ssc_done, 1)
                dve.wait_ge(rc_done, t + 1)
                dve.tensor_tensor(heads(qcn[:]), heads(qc[:]), wide(rc[:], HD), ALU.mult).then_inc(qcn_done, 1)

            dve_rot = s_("dve_rot")
            take(0, XT0)
            take(0, XT1)
            rotate(0)
            scale_qc(0)

            def tile(t, more, first):
                own = Steps(dve, dve_own, OWN * t)
                if more:
                    take(t + 1, XT0)
                    take(t + 1, XT1)
                tr.wait_full(dve, t, QCT)
                dve.tensor_scalar(qTC[:], tiles(TR[:, 0:CW]), gqc8[:], None, ALU.mult).then_inc(tr.lo, 1)
                dve.wait_ge(sb_done, t + 1)
                for s in range(2):
                    i = dve.tensor_tensor(Sm[:].rearrange("p (a s) n -> p s a n", s=2)[:, s], by_head(SB[:], P)[:, s],
                                          tri[:].unsqueeze(1).to_broadcast([P, 2, P]), ALU.mult)
                i.then_inc(sm_done, 1)
                dve.wait_ge(sc_done, t + 1)
                dve.tensor_reduce(halves1(nmax[:]), by_head(SC[:], N_MEM), AX.X, ALU.max,
                                  negate=True).then_inc(max_done, 1)
                dve.wait_ge(eg_done, t + 1)
                own(dve.tensor_scalar(eg[:], eg[:], 1.0, None, ALU.add))
                dve.reciprocal(eg[:], eg[:]).then_inc(sig_done, 1)
                tr.wait_full(dve, t, U)
                u = TR[:, 0:BW].rearrange("p (a b e) -> p a b e", b=2, e=HD)
                dve.tensor_tensor(Rt[0:64], R[0:64], u[0:64, :, 0, :], ALU.add)
                own(dve.tensor_tensor(Rt[64:128], R[64:128], u[64:128, :, 1, :], ALU.add))
                own(dve.tensor_tensor(R[:], Rt[:], wide(g128[:], HD), ALU.mult))
                dve.sem_inc(tr.lo, 1)
                dve.sem_inc(r_done, 1)
                if more:
                    rotate(t + 1)
                dve.wait_ge(o_done, t + 1)
                own(dve.tensor_reduce(halves1(sm4[:]), by_head(O[:], HD), AX.X, ALU.add))
                own(dve.tensor_scalar(mean[:], sm4[:], 1.0 / HD, None, ALU.mult))
                dve.tensor_tensor(halves(cent[:]), by_head(O[:], HD),
                                  halves1(mean[:]).unsqueeze(3).to_broadcast([P, 2, 2, HD]), ALU.subtract).then_inc(cent_done, 1)
                own(dve.reciprocal(rinv[:], rs[:]))
                if not first:
                    dve.wait_ge(mix_out, 16 * t)
                dve.tensor_tensor(halves(mixt[:, BW:BW + CW]), by_head(O[:], HD, 2 * HD),
                                  halves1(rinv[:]).unsqueeze(3).to_broadcast([P, 2, 2, HD]), ALU.mult).then_inc(mix_done, 1)
                dve.wait_ge(mix_done, 2 * t + 1)
                dve.sem_inc(o_free, 1)
                dve.wait_ge(csq_done, t + 1)
                dve.tensor_reduce(ss4[:], heads(csq[:]), AX.X, ALU.add).then_inc(ss4_done, 1)
                dve.wait_ge(r4_done, t + 1)
                dve.tensor_tensor(heads(y[:]), heads(cent[:]), wide(r4[:], HD), ALU.mult).then_inc(y_done, 1)
                if more:
                    scale_qc(t + 1)
                dve.wait_ge(yg_done, t + 1)
                dve.wait_ge(sg_done, t + 1)
                dve.tensor_tensor(mixt[:, 0:BW], yg[:], sg[:], ALU.mult).then_inc(mix_done, 1)
                assert own.n == OWN

            OWN = 6
            for t in range(NT):
                tile(t, t + 1 < NT, t == 0)



NLG = NG + NE
CAP = P
FULL = SEQ * 2 // CAP
BLOCKS = NE + FULL
KF = DE // P
SKIP = 1 << 20


def phase_o(c, d, lg):
    nc = c.nc
    with ExitStack() as st:
        Wh = sbuf(nc, st, "o_wh", [P, KD, D], F32R)
        Wl = sbuf(nc, st, "o_wl", [P, KD, D], F32R)
        Rh = sbuf(nc, st, "o_rh", [P, KD, NLG], F32R)
        Rl = sbuf(nc, st, "o_rl", [P, KD, NLG], F32R)
        split_weights(c, "o_w", rows(d["w_out"], KD), None, Wh, Wl, KD, D)
        t_ = lambda name, shape, dt=F32: sbuf(nc, st, "o_" + name, shape, dt)
        wr = t_("wr", [P, KD, NLG])
        B = 2
        mx, xb, h, hn = t_("m", [P, B, D]), t_("x", [P, B, D]), t_("h", [P, B, D]), t_("hn", [P, B, D])
        mTh, mTl = t_("mth", [P, B, KD * P], F32R), t_("mtl", [P, B, KD * P], F32R)
        nTh, nTl = t_("nth", [P, KD * P], F32R), t_("ntl", [P, KD * P], F32R)
        junk = t_("junk", [P, D], BF16)
        ident = t_("ident", [P, P])
        gf, br = t_("gf", [P, D]), t_("br", [P, NLG])
        mhalf, ss, ms, r = t_("mhalf", [P, 1]), t_("ss", [P, NT]), t_("ms", [P, NT]), t_("r", [P, NT])
        Y, XT, HT, LG = *c.bank2, c.bank[0]
        s_ = lambda name: c.sem("o_" + name)
        const_in, wr_in, wr_hi, wr_lo, pool_set = map(s_, ("const_in", "wr_in", "wr_hi", "wr_lo", "pool_set"))
        m_in, x_in, h_out, hn_out = ([s_(f"{n}{b}") for b in range(B)] for n in ("m_in", "x_in", "h_out", "hn_out"))
        xt_done, xt_hi, xt_lo, ht_done, ht_hi, ht_lo = map(s_, ("xt_done", "xt_hi", "xt_lo", "ht_done", "ht_hi", "ht_lo"))
        y_done, h_done = s_("y_done"), s_("h_done")
        ss_done, ms_done, r_done, hn_done, lg_full, lg_done = map(s_, ("ss_done", "ms_done", "r_done", "hn_done", "lg_full", "lg_done"))
        CONSTS = 16 * 4
        block = st.enter_context(nc.Block())

        def loads(t):
            return 16 * (t // B + 1)

        @block.sync
        def _(sp):
            def load_m(t):
                if t >= B:
                    sp.wait_ge(xt_done, t - B + 1)
                sp.dma_start(mx[:, t % B, :], d["mix"][t * P:(t + 1) * P, :]).then_inc(m_in[t % B], 16)

            def load_x(t):
                if t >= B:
                    sp.wait_ge(h_done, 2 * (t - B + 1))
                sp.dma_start(xb[:, t % B, :], d["x"][t * P:(t + 1) * P, :]).then_inc(x_in[t % B], 16)

            load_m(0)
            sp.dma_start(ident[:], d["ident"]).then_inc(const_in, 16)
            sp.dma_start(wr[:, :, 0:NG], rows(d["w_router_group"], KD)).then_inc(wr_in, 16)
            sp.dma_start(wr[:, :, NG:NLG], rows(d["w_router_expert"], KD)).then_inc(wr_in, 16)
            load_m(1)
            sp.dma_start(gf[:], d["ffn_norm_g"].partition_broadcast(P)).then_inc(const_in, 16)
            sp.dma_start(br[:, 0:NG], d["b_router_group"].partition_broadcast(P)).then_inc(const_in, 16)
            sp.dma_start(br[:, NG:NLG], d["b_router_expert"].partition_broadcast(P)).then_inc(const_in, 16)
            load_x(0)
            load_x(1)
            for t in range(NT):
                if t + B < NT:
                    load_m(t + B)
                sp.wait_ge(h_done, 2 * (t + 1))
                sp.dma_start(d["out"][t * P:(t + 1) * P, :], h[:, t % B, :]).then_inc(h_out[t % B], 16)
                if t + B < NT:
                    load_x(t + B)
                sp.wait_ge(hn_done, t + 1)
                sp.dma_start(d["hn"][t * P:(t + 1) * P, :], hn[:, t % B, :]).then_inc(hn_out[t % B], 16)
            for b in range(B):
                sp.wait_ge(h_out[b], 16 * (NT // B))
                sp.wait_ge(hn_out[b], 16 * (NT // B))

        @block.gpsimd
        def _(pool):
            pool.memset(mhalf[:], -0.5).then_inc(pool_set, 1)
            pool.wait_ge(pool_set, 1)
            for t in range(NT):
                pool.wait_ge(ss_done, t + 1)
                pool.tensor_scalar(ms[:, t:t + 1], ss[:, t:t + 1], 1.0 / D, EPS, ALU.mult, ALU.add).then_inc(ms_done, 1)
                pool.wait_ge(ms_done, t + 1)
                pool.tensor_tensor(r[:, t:t + 1], ms[:, t:t + 1], mhalf[:], ALU.pow).then_inc(r_done, 1)

        @block.scalar
        def _(act):
            def mixed(t):
                act.wait_ge(xt_done, t + 1)
                if t >= B:
                    act.wait_ge(y_done, 2 * (t - B + 1))
                act.activation(mTh[:, t % B, :], XT[:], ACT.Copy).then_inc(xt_hi, 1)

            mixed(0)
            mixed(1)
            act.wait_ge(wr_in, 32)
            act.activation(Rh[:], wr[:], ACT.Copy).then_inc(wr_hi, 1)
            for t in range(NT):
                act.wait_ge(h_done, 2 * (t + 1))
                if t:
                    act.wait_ge(ss_done, t)
                act.activation(junk[:], h[:, t % B, :], ACT.Square, accum_out=ss[:, t:t + 1]).then_inc(ss_done, 1)
                if t + B < NT:
                    mixed(t + B)
                act.wait_ge(ht_done, t + 1)
                if t:
                    act.wait_ge(lg_full, t)
                act.activation(nTh[:], HT[:], ACT.Copy).then_inc(ht_hi, 1)

        @block.tensor
        def _(pe):
            def turn(out, src, done):
                xs = src.rearrange("p (m k) -> p k m", k=KD)
                for k in range(KD):
                    mm = pe.transpose(out[:, k * P:(k + 1) * P], xs[:, k, :], ident[:])
                mm.then_inc(done, 1)

            def turn_mixed(t):
                pe.wait_ge(m_in[t % B], loads(t))
                if t:
                    pe.wait_ge(xt_lo, t)
                turn(XT, mx[:, t % B, :], xt_done)

            def w_out(t, half):
                if half == 0:
                    pe.wait_ge(xt_lo, t + 1)
                if t:
                    pe.wait_ge(h_done, 2 * (t - 1) + half + 1)
                cols = slice(512 * half, 512 * half + 512)
                for k in range(KD):
                    m = slice(k * P, (k + 1) * P)
                    mm = product(pe, Y[:, cols], (mTh[:, t % B, m], mTl[:, t % B, m]), (Wh[:, k, cols], Wl[:, k, cols]),
                                 k == 0, k == KD - 1)
                mm.then_inc(y_done, 1)

            def turn_normed(t):
                pe.wait_ge(hn_done, t + 1)
                if t:
                    pe.wait_ge(ht_lo, t)
                turn(HT, hn[:, t % B, :], ht_done)

            def logits(t):
                pe.wait_ge(ht_lo, t + 1)
                if t:
                    pe.wait_ge(lg_done, t)
                for k in range(KD):
                    m = slice(k * P, (k + 1) * P)
                    mm = product(pe, LG[:, 0:NLG], (nTh[:, m], nTl[:, m]), (Rh[:, k, :], Rl[:, k, :]), k == 0, k == KD - 1)
                mm.then_inc(lg_full, 1)

            pe.wait_ge(const_in, CONSTS)
            turn_mixed(0)
            turn_mixed(1)
            w_out(0, 0)
            w_out(0, 1)
            pe.wait_ge(wr_lo, 1)
            for t in range(NT):
                if t + 2 < NT:
                    turn_mixed(t + 2)
                if t + 1 < NT:
                    w_out(t + 1, 0)
                if t:
                    logits(t - 1)
                if t + 1 < NT:
                    w_out(t + 1, 1)
                turn_normed(t)
            logits(NT - 1)

        @block.vector
        def _(dve):
            def mixed(t):
                dve.wait_ge(xt_hi, t + 1)
                dve.tensor_tensor(mTl[:, t % B, :], XT[:], mTh[:, t % B, :].bitcast(F32), ALU.subtract).then_inc(xt_lo, 1)

            def residual(t, half):
                dve.wait_ge(y_done, 2 * t + half + 1)
                if half == 0:
                    dve.wait_ge(x_in[t % B], loads(t))
                    if t >= B:
                        dve.wait_ge(h_out[t % B], loads(t - B))
                        dve.wait_ge(hn_done, t - B + 1)
                cols = slice(512 * half, 512 * half + 512)
                dve.tensor_tensor(h[:, t % B, cols], Y[:, cols], xb[:, t % B, cols], ALU.add).then_inc(h_done, 1)

            mixed(0)
            mixed(1)
            residual(0, 0)
            dve.wait_ge(wr_hi, 1)
            dve.tensor_tensor(Rl[:], wr[:], Rh[:].bitcast(F32), ALU.subtract).then_inc(wr_lo, 1)
            dve.wait_ge(const_in, CONSTS)
            for t in range(NT):
                residual(t, 1)
                if t + B < NT:
                    mixed(t + B)
                dve.wait_ge(r_done, t + 1)
                if t >= B:
                    dve.wait_ge(hn_out[t % B], loads(t - B))
                    dve.wait_ge(ht_done, t - B + 1)
                dve.scalar_tensor_tensor(hn[:, t % B, :], h[:, t % B, :], r[:, t:t + 1], gf[:], ALU.mult, ALU.mult).then_inc(hn_done, 1)
                if t + 1 < NT:
                    residual(t + 1, 0)
                if t:
                    dve.wait_ge(lg_full, t)
                    dve.tensor_tensor(lg[:, t - 1, :], LG[:, 0:NLG], br[:], ALU.add).then_inc(lg_done, 1)
                dve.wait_ge(ht_hi, t + 1)
                dve.tensor_tensor(nTl[:], HT[:], nTh[:].bitcast(F32), ALU.subtract).then_inc(ht_lo, 1)
            dve.wait_ge(lg_full, NT)
            dve.tensor_tensor(lg[:, NT - 1, :], LG[:, 0:NLG], br[:], ALU.add).then_inc(lg_done, 1)


def phase_r(c, d, lg, btab, ids):
    nc = c.nc
    with ExitStack() as st:
        t_ = lambda name, shape, dt=F32: sbuf(nc, st, "r_" + name, shape, dt)
        g8, gtop, gix = t_("g8", [P, NT, 8]), t_("gtop", [P, NT, 8]), t_("gix", [P, NT, 8], U32)
        gf, gsum, pg = t_("gf", [P, NT]), t_("gsum", [P, NT]), t_("pg", [P, NT])
        ge = t_("ge", [P, NT, NG])
        tab = t_("tab", [P, 2 * NE + 8 + FULL])
        ones, before = t_("ones", [P, P]), t_("before", [P, P])
        mask, pen, em = t_("mask", [P, NT, NE]), t_("pen", [P, NT, NE]), t_("em", [P, NT, NE])
        top, ix, ixf = t_("top", [P, NT, 8]), t_("ix", [P, NT, 8], U32), t_("ixf", [P, NT, 2])
        dv, ev = t_("dv", [P, NT]), t_("ev", [P, NT])
        A1, A2, A = t_("a1", [P, NT, NE]), t_("a2", [P, NT, NE]), t_("a", [P, NT, NE])
        rank, prior, cnt = t_("rank", [P, NT, NE]), t_("prior", [P, NT, NE]), t_("cnt", [P, NE])
        over, extra, upto, one = t_("over", [P, NE, 8]), t_("extra", [P, NE]), t_("upto", [P, NE]), t_("one", [P, NE])
        shift, late, row, pick = t_("shift", [P, NE]), t_("late", [P, NT, NE]), t_("row", [P, NT, NE]), t_("pick", [P, NT, NE])
        destf, dest = t_("destf", [P, 2, NT]), t_("dest", [P, 2, NT], U32)
        pair, wt = t_("pair", [P, 2, NT, 2], I32), t_("wt", [P, 2, NT])
        bm, bsum = t_("bm", [P, FULL, NE]), t_("bsum", [P, FULL + 1])
        tok = t_("tok", [P, NT], I32)
        blank = t_("blank", [P, BLOCKS, 2], I32)
        C0, C1 = c.bank[0], c.bank[1]
        s_ = lambda name: c.sem("r_" + name)
        const_in, own_s, ge_in, ge_out, ev_in, ev_out, a_done, sums, dest_done, blank_set, blank_out, tok_out, ids_in = map(
            s_, ("const_in", "own", "ge_in", "ge_out", "ev_in", "ev_out", "a_done", "sums", "dest_done", "blank_set",
                 "blank_out", "tok_out", "ids_in"))
        pair_done = s_("pair_done")
        GOF, EOF, BND, LATER = tab[:, 0:NE], tab[:, NE:2 * NE], tab[:, 2 * NE:2 * NE + 7], tab[:, 2 * NE + 8:]
        block = st.enter_context(nc.Block())

        def over_tiles(ap):
            return ap.unsqueeze(1).to_broadcast([P, NT, ap.shape[1]])

        @block.sync
        def _(sp):
            sp.dma_start(tab[:], d["route_tab"].partition_broadcast(P)).then_inc(const_in, 16)
            sp.dma_start(before[:], d["before"]).then_inc(const_in, 16)
            sp.dma_start(tok[:], d["token"]).then_inc(const_in, 16)
            sp.wait_ge(blank_set, 1)
            sp.dma_start(d["row"].rearrange("(i p) a -> p i a", p=P), blank[:], allow_slow_non_contiguous=True).then_inc(blank_out, 16)
            sp.wait_ge(tok_out, 16 * 2 * NT)
            sp.dma_start(ids[:], d["row"].rearrange("(i p) a -> p i a", p=P), allow_slow_non_contiguous=True).then_inc(ids_in, 16)
            sp.wait_ge(ids_in, 16)

        @block.gpsimd
        def _(pool):
            pool.memset(blank[:, :, 0:1], SKIP)
            pool.memset(blank[:, :, 1:2], 0).then_inc(blank_set, 1)
            pool.wait_ge(const_in, 48)
            pool.wait_ge(pair_done, 1)
            pool.wait_ge(blank_out, 16)
            pool.wait_ge(dest_done, 1)
            for j in range(2):
                for t in range(NT):
                    pool.indirect_dma_start(out=d["row"], out_offset=bass.IndirectOffsetOnAxis(ap=dest[:, j, t:t + 1], axis=0),
                                            in_=pair[:, j, t, :], in_offset=None).then_inc(tok_out, 16)

        @block.scalar
        def _(act):
            act.wait_ge(ge_in, 1)
            act.activation(ge[:], ge[:], ACT.Exp).then_inc(ge_out, 1)
            act.wait_ge(ev_in, 1)
            act.activation(ev[:], dv[:], ACT.Exp).then_inc(ev_out, 1)

        @block.tensor
        def _(pe):
            pe.wait_ge(const_in, 48)
            pe.wait_ge(a_done, 1)
            flat = A[:].rearrange("p t e -> p (t e)")
            pe.matmul(C0[:, 0:NT * NE], before[:], flat, start=True, stop=True)
            pe.matmul(C1[:, 0:NT * NE], ones[:], flat, start=True, stop=True).then_inc(sums, 1)

        @block.vector
        def _(dve):
            own = Steps(dve, own_s)
            own(dve.memset(ones[:], 1.0))
            own(dve.memset(one[:], 1.0))
            own(dve.memset(g8[:], NEG))
            own(dve.tensor_copy(g8[:, :, 0:NG], lg[:, :, 0:NG]))
            for t in range(NT):
                last = dve.max(gtop[:, t, :], g8[:, t, :])
            own(last)
            for t in range(NT):
                last = dve.max_index(gix[:, t, :], gtop[:, t, :], g8[:, t, :])
            own(last)
            dve.tensor_tensor(ge[:], lg[:, :, 0:NG], gtop[:, :, 0:1].to_broadcast([P, NT, NG]), ALU.subtract).then_inc(ge_in, 1)
            own(dve.tensor_copy(gf[:], gix[:, :, 0]))
            dve.wait_ge(const_in, 48)
            own(dve.tensor_tensor(mask[:], over_tiles(GOF), wide(gf[:], NE), ALU.is_equal))
            own(dve.tensor_scalar(pen[:], mask[:], -NEG, NEG, ALU.mult, ALU.add))
            own(dve.tensor_tensor(em[:], lg[:, :, NG:NLG], mask[:], ALU.mult))
            own(dve.tensor_tensor(em[:], em[:], pen[:], ALU.add))
            for t in range(NT):
                last = dve.max(top[:, t, :], em[:, t, :])
            own(last)
            for t in range(NT):
                last = dve.max_index(ix[:, t, :], top[:, t, :], em[:, t, :])
            own(last)
            dve.tensor_tensor(dv[:], top[:, :, 1], top[:, :, 0], ALU.subtract).then_inc(ev_in, 1)
            own(dve.tensor_copy(ixf[:], ix[:, :, 0:2]))
            own(dve.tensor_tensor(A1[:], over_tiles(EOF), ixf[:, :, 0:1].to_broadcast([P, NT, NE]), ALU.is_equal))
            own(dve.tensor_tensor(A2[:], over_tiles(EOF), ixf[:, :, 1:2].to_broadcast([P, NT, NE]), ALU.is_equal))
            dve.tensor_tensor(A[:], A1[:], A2[:], ALU.add).then_inc(a_done, 1)
            dve.wait_ge(ge_out, 1)
            own(dve.tensor_reduce(gsum[:], ge[:], AX.X, ALU.add))
            own(dve.reciprocal(pg[:], gsum[:]))
            dve.wait_ge(ev_out, 1)
            own(dve.tensor_scalar(dv[:], ev[:], 1.0, None, ALU.add))
            own(dve.reciprocal(dv[:], dv[:]))
            own(dve.tensor_tensor(wt[:, 0, :], pg[:], dv[:], ALU.mult))
            own(dve.tensor_tensor(wt[:, 1, :], wt[:, 0, :], ev[:], ALU.mult))
            dve.tensor_copy(pair[:, :, :, 1].bitcast(F32), wt[:])
            dve.tensor_copy(pair[:, :, :, 0], tok[:].unsqueeze(1).to_broadcast([P, 2, NT])).then_inc(pair_done, 1)
            dve.wait_ge(sums, 1)
            own(dve.memset(prior[:, 0, :], 0.0))
            for t in range(NT - 1):
                own(dve.tensor_tensor(prior[:, t + 1, :], prior[:, t, :], C1[:, t * NE:(t + 1) * NE], ALU.add))
            own(dve.tensor_tensor(cnt[:], prior[:, NT - 1, :], C1[:, (NT - 1) * NE:NT * NE], ALU.add))
            own(dve.tensor_tensor(rank[:].rearrange("p t e -> p (t e)"), C0[:, 0:NT * NE], prior[:].rearrange("p t e -> p (t e)"), ALU.add))
            own(dve.tensor_tensor(over[:, :, 0:7], wide(cnt[:], 7), BND.unsqueeze(1).to_broadcast([P, NE, 7]), ALU.is_gt))
            own(dve.tensor_reduce(extra[:], over[:, :, 0:7], AX.X, ALU.add))
            own(dve.tensor_tensor_scan(upto[:], one[:], extra[:], 0.0, ALU.mult, ALU.add))
            own(dve.tensor_tensor(shift[:], upto[:], extra[:], ALU.subtract))
            own(dve.tensor_tensor(shift[:], shift[:], EOF, ALU.subtract))
            own(dve.tensor_scalar(shift[:], shift[:], NE - 1.0, float(CAP), ALU.add, ALU.mult))
            own(dve.tensor_scalar(late[:], rank[:], float(CAP), None, ALU.is_ge))
            own(dve.tensor_tensor(late[:], late[:], over_tiles(shift[:]), ALU.mult))
            own(dve.tensor_tensor(row[:], rank[:], late[:], ALU.add))
            own(dve.scalar_tensor_tensor(row[:], over_tiles(EOF), float(CAP), row[:], ALU.mult, ALU.add))
            for j, a in enumerate((A1, A2)):
                own(dve.tensor_tensor(pick[:], row[:], a[:], ALU.mult))
                own(dve.tensor_reduce(destf[:, j, :], pick[:], AX.X, ALU.add))
            dve.tensor_copy(dest[:], destf[:]).then_inc(dest_done, 1)
            own(dve.tensor_tensor(bm[:], upto[:].unsqueeze(1).to_broadcast([P, FULL, NE]), wide(LATER, NE), ALU.is_le))
            own(dve.tensor_reduce(bsum[:, 0:FULL], bm[:], AX.X, ALU.add))
            own(dve.tensor_scalar(bsum[:, 0:FULL], bsum[:, 0:FULL], NE - 1.0, None, ALU.min))
            own(dve.tensor_scalar(bsum[:, FULL:FULL + 1], upto[:, NE - 1:NE], NE - 3.0, None, ALU.add))
            own(dve.tensor_copy(btab[:, 0:NE], EOF))
            own(dve.tensor_copy(btab[:, NE:], bsum[:]))


def phase_e(c, d, btab, ids):
    nc = c.nc
    with ExitStack() as st:
        t_ = lambda name, shape, dt=F32: sbuf(nc, st, "e_" + name, shape, dt)
        raw = t_("raw", [P, 3, KD * DE])
        Wh, Wl = t_("wh", [P, 3, KD * DE], F32R), t_("wl", [P, 3, KD * DE], F32R)
        ident = t_("ident", [P, P])
        ix, ix_y, w_y = t_("ix", [P, 1], U32), t_("ix_y", [P, 1], U32), t_("w_y", [P, 1])
        xg = t_("xg", [P, D])
        xTh, xTl = t_("xth", [P, KD, P], F32R), t_("xtl", [P, KD, P], F32R)
        sg, hs = t_("sg", [P, DE]), t_("hs", [P, DE])
        hTh, hTl = t_("hth", [P, KF, P], F32R), t_("htl", [P, KF, P], F32R)
        y = t_("y", [P, D])
        XT, Y = c.bank2[0], c.bank2[1]
        G, U = c.bank2[2][:, 0:512], c.bank2[2][:, 512:1024]
        HT = c.bank[0]
        s_ = lambda name: c.sem("e_" + name)
        const_in, ix_set, w_set, xg_set, xg_in, y_out, sp_passed, pool_passed = map(
            s_, ("const_in", "ix_set", "w_set", "xg_set", "xg_in", "y_out", "sp_passed", "pool_passed"))
        GU, DN = range(KD // 2), range(KD // 2, KD // 2 + KF // 2)
        CH_ = [*GU, *DN]
        loaded, hi, lo, used = ([s_(f"{n}{j}") for j in CH_] for n in ("loaded", "hi", "lo", "used"))
        xt_done, xt_hi, xt_lo, ht_done, ht_hi, ht_lo = map(s_, ("xt_done", "xt_hi", "xt_lo", "ht_done", "ht_hi", "ht_lo"))
        sg_done, hs_done, y_done = map(s_, ("sg_done", "hs_done", "y_done"))
        BY_POOL = (GU[1],)
        block = st.enter_context(nc.Block())
        GATE, UP, DOWN = range(3)

        def part(buf, j):
            if j in GU:
                return buf[:, 0:2, 2 * j * DE:2 * (j + 1) * DE]
            return buf[:, DOWN, 2 * (j - DN[0]) * D:2 * (j - DN[0] + 1) * D]

        def is_first(i):
            return isinstance(i, int) and i == 0

        def turns(eng, body, after=1):
            n = eng.value_load(btab[0:1, BLOCKS:BLOCKS + 1], min_val=NE - 3, max_val=BLOCKS - 4)
            body(0, None, after)
            body(1, 0, after)
            with eng.Fori(1, n + (2 - after)) as p:
                body(p + 1, p, after)
            for more in reversed(range(after)):
                body(n + (3 - more) - 1, n + (3 - more) - 2, more)
            return n + 2

        def split_lo(eng, i, j):
            eng.wait_ge(hi[j], i + 1)
            eng.tensor_tensor(part(Wl, j), part(raw, j), part(Wh, j).bitcast(F32), ALU.subtract).then_inc(lo[j], 1)

        @block.sync
        def _(sp):
            sp.dma_start(ident[:], d["ident"]).then_inc(const_in, 16)

            def load(e, j):
                if j in GU:
                    for m, w in ((GATE, d["w_gate"]), (UP, d["w_up"])):
                        src = w.rearrange("e (p k) n -> e p (k n)", p=P)[bass.ds(e, 1), :, 2 * j * DE:2 * (j + 1) * DE]
                        sp.dma_start(raw[:, m, 2 * j * DE:2 * (j + 1) * DE], src.rearrange("a p n -> p (a n)")).then_inc(loaded[j], 16)
                else:
                    k = j - DN[0]
                    src = d["w_down"].rearrange("e (p k) n -> e p (k n)", p=P)[bass.ds(e, 1), :, 2 * k * D:2 * (k + 1) * D]
                    sp.dma_start(part(raw, j), src.rearrange("a p n -> p (a n)")).then_inc(loaded[j], 16)

            def expert(i):
                return i if isinstance(i, int) else sp.value_load(btab[0:1, bass.ds(i, 1)], min_val=0, max_val=NE - 1)

            def load_next(i, chunks):
                e = expert(i)
                for j in chunks:
                    wait_apart(sp, lo[j], i, sp_passed)
                    load(e, j)

            def turn(i, p, more):
                if p is not None:
                    load_next(i, DN)
                if more == 2:
                    load_next(i + 2, GU)

            for j in CH_:
                load(0, j)
            load_next(1, GU)
            turns(sp, turn, 2)

        @block.gpsimd
        def _(pool):
            pool.memset(xg[:], 0.0).then_inc(xg_set, 1)
            pool.wait_ge(xg_set, 1)

            def gather(i):
                if not is_first(i):
                    wait_apart(pool, xt_done, i, pool_passed)
                pool.tensor_copy(ix[:], ids[:, bass.ds(i, 1), 0]).then_inc(ix_set, 1)
                wait_apart(pool, ix_set, i + 1, pool_passed)
                pool.indirect_dma_start(out=xg[:], out_offset=None, in_=d["hn"],
                                        in_offset=bass.IndirectOffsetOnAxis(ap=ix[:], axis=0),
                                        bounds_check=SEQ - 1, oob_is_err=False).then_inc(xg_in, 16)

            def row_weights(i):
                if not is_first(i):
                    wait_apart(pool, y_out, 16 * i, pool_passed)
                pool.tensor_copy(ix_y[:], ids[:, bass.ds(i, 1), 0])
                pool.tensor_copy(w_y[:], ids[:, bass.ds(i, 1), 1].bitcast(F32)).then_inc(w_set, 1)

            def add_out(i):
                wait_apart(pool, y_done, i + 1, pool_passed)
                pool.indirect_dma_start(out=d["out"], out_offset=bass.IndirectOffsetOnAxis(ap=ix_y[:], axis=0),
                                        in_=y[:], in_offset=None, bounds_check=SEQ - 1, oob_is_err=False,
                                        compute_op=ALU.add).then_inc(y_out, 16)

            def turn(i, p, more):
                if more:
                    gather(i + 1)
                if p is not None:
                    row_weights(p)
                if more:
                    for j in BY_POOL:
                        split_lo(pool, i + 1, j)
                if p is not None:
                    add_out(p)

            gather(0)
            for j in BY_POOL:
                split_lo(pool, 0, j)
            last = turns(pool, turn)
            row_weights(last)
            add_out(last)
            wait_apart(pool, y_out, 16 * (last + 1), pool_passed)

        @block.scalar
        def _(act):
            def split(i, j):
                act.wait_ge(loaded[j], (32 if j in GU else 16) * (i + 1))
                if not is_first(i):
                    act.wait_ge(used[j], i)
                act.activation(part(Wh, j), part(raw, j), ACT.Copy).then_inc(hi[j], 1)

            def turn_x(i):
                act.wait_ge(xt_done, i + 1)
                act.activation(xTh[:], tiles(XT[:]), ACT.Copy).then_inc(xt_hi, 1)

            def turn_h(i):
                act.wait_ge(ht_done, i + 1)
                act.activation(hTh[:], tiles(HT[:]), ACT.Copy).then_inc(ht_hi, 1)

            def turn(i, p, more):
                if p is not None:
                    for j in DN:
                        split(p, j)
                if more:
                    split(i + 1, GU[0])
                    split(i + 1, GU[1])
                if p is not None:
                    turn_h(p)
                if more:
                    split(i + 1, GU[2])
                act.wait_ge(used[GU[-1]], i + 1)
                if p is not None:
                    act.wait_ge(hs_done, i)
                act.activation(sg[:], G, ACT.Silu).then_inc(sg_done, 1)
                if more:
                    split(i + 1, GU[3])
                    turn_x(i + 1)

            turn_x(0)
            for j in GU:
                split(0, j)
            last = turns(act, turn)
            for j in DN:
                split(last, j)
            turn_h(last)

        @block.tensor
        def _(pe):
            def turn_x(i):
                pe.wait_ge(xg_in, 16 * (i + 1))
                xs = xg[:].rearrange("p (m k) -> p k m", k=KD)
                for k in range(KD):
                    mm = pe.transpose(XT[:, k * P:(k + 1) * P], xs[:, k, :], ident[:])
                mm.then_inc(xt_done, 1)

            def turn_h(i):
                pe.wait_ge(hs_done, i + 1)
                hk = hs[:].rearrange("p (m k) -> p k m", k=KF)
                for k in range(KF):
                    mm = pe.transpose(HT[:, k * P:(k + 1) * P], hk[:, k, :], ident[:])
                mm.then_inc(ht_done, 1)

            def down(i, more=0):
                pe.wait_ge(ht_lo, i + 1)
                if not is_first(i):
                    pe.wait_ge(y_done, i)
                for j in DN:
                    if j == DN[-1] and more:
                        turn_x(i + 2)
                    pe.wait_ge(lo[j], i + 1)
                    for k in (2 * (j - DN[0]), 2 * (j - DN[0]) + 1):
                        for half in range(2):
                            w = slice(k * D + 512 * half, k * D + 512 * half + 512)
                            mm = product(pe, Y[:, 512 * half:512 * half + 512], (hTh[:, k, :], hTl[:, k, :]),
                                         (Wh[:, DOWN, w], Wl[:, DOWN, w]), k == 0, k == KF - 1)
                    mm.then_inc(used[j], 1)

            def turn(i, p, more):
                pe.wait_ge(xt_lo, i + 1)
                if p is not None:
                    pe.wait_ge(hs_done, i)
                for j in GU:
                    pe.wait_ge(lo[j], i + 1)
                    for k in (2 * j, 2 * j + 1):
                        x = (xTh[:, k, :], xTl[:, k, :])
                        for out, m in ((G, GATE), (U, UP)):
                            cols = slice(k * DE, (k + 1) * DE)
                            mm = product(pe, out, x, (Wh[:, m, cols], Wl[:, m, cols]), k == 0, k == KD - 1)
                    mm.then_inc(used[j], 1)
                    if j == GU[1] and p is not None:
                        turn_h(p)
                if p is None:
                    turn_x(i + 1)
                else:
                    down(p, more)

            pe.wait_ge(const_in, 16)
            turn_x(0)
            last = turns(pe, turn)
            turn_h(last)
            down(last)

        @block.vector
        def _(dve):
            def split(i, j):
                if j not in BY_POOL:
                    split_lo(dve, i, j)

            def turn_x(i):
                dve.wait_ge(xt_hi, i + 1)
                dve.tensor_tensor(xTl[:], tiles(XT[:]), xTh[:].bitcast(F32), ALU.subtract).then_inc(xt_lo, 1)

            def turn_h(i):
                dve.wait_ge(ht_hi, i + 1)
                dve.tensor_tensor(hTl[:], tiles(HT[:]), hTh[:].bitcast(F32), ALU.subtract).then_inc(ht_lo, 1)

            def store(i):
                dve.wait_ge(used[DN[-1]], i + 1)
                if not is_first(i):
                    dve.wait_ge(y_out, 16 * i)
                dve.wait_ge(w_set, i + 1)
                dve.tensor_scalar(y[:], Y[:], w_y[:], None, ALU.mult).then_inc(y_done, 1)

            def turn(i, p, more):
                if p is not None:
                    for j in DN:
                        split(p, j)
                if more:
                    split(i + 1, GU[0])
                    split(i + 1, GU[1])
                if p is not None:
                    turn_h(p)
                if more:
                    split(i + 1, GU[2])
                if p is not None:
                    dve.wait_ge(ht_done, i)
                dve.wait_ge(sg_done, i + 1)
                dve.tensor_tensor(hs[:], U, sg[:], ALU.mult).then_inc(hs_done, 1)
                if more:
                    split(i + 1, GU[3])
                    turn_x(i + 1)
                if p is not None:
                    store(p)

            turn_x(0)
            for j in GU:
                split(0, j)
            last = turns(dve, turn)
            for j in DN:
                split(last, j)
            turn_h(last)
            store(last)


def constants():
    n = np.arange(P, dtype=np.float64)[:, None]
    gamma = 1.0 - np.exp2(-5.0 - np.arange(BH, dtype=np.float64))
    half = HD // 2
    return {
        "ident": np.eye(P, dtype=np.float32),
        "tri": (np.arange(P)[:, None] <= np.arange(P)[None, :]).astype(np.float32),
        "decay": np.concatenate([gamma ** n, gamma ** -n * HD ** -0.5], axis=1).astype(np.float32),
        "decay_tile": np.repeat((gamma ** P).reshape(BH // 2, 2).T, HD, axis=0).astype(np.float32),
        "before": (np.arange(P)[:, None] < np.arange(P)[None, :]).astype(np.float32),
        "token": np.arange(SEQ, dtype=np.int32).reshape(NT, P).T,
        "route_tab": np.concatenate([np.arange(NE) // EG, np.arange(NE), CAP * np.arange(1, 9), np.arange(FULL)]).astype(np.float32),
        "inv_freq": (np.float32(10000.0) ** (-np.arange(half, dtype=np.float32) / np.float32(half))).astype(np.float32),
    }




SCRATCH = {
    "ext_dram": ((AH, EXT), F32),
    "mix": ((SEQ, D), F32),
    "hn": ((SEQ, D), F32),
    "row": ((BLOCKS * P, 2), I32),
}


def build(nc, d):
    with ExitStack() as ctx:
        c = Core(nc, ctx)
        c.bank2 = [c.psum(f"pair{i}", 2) for i in range(3)]
        c.bank = [c.psum(f"bank{i}") for i in range(2)]
        phase_a(c, d)
        c.reuse_sems()
        phase_bc(c, d)
        c.reuse_sems()
        lg = sbuf(nc, ctx, "logits", [P, NT, NLG])
        btab = sbuf(nc, ctx, "block_expert", [P, BLOCKS + 1], I32)
        ids = sbuf(nc, ctx, "row_ids", [P, BLOCKS, 2], I32)
        phase_o(c, d, lg)
        phase_r(c, d, lg, btab, ids)
        c.reuse_sems()
        phase_e(c, d, btab, ids)


def kernel(**inputs):
    import numpy as _np
    import concourse.bacc as _bacc
    from concourse.bass_utils import run_bass_kernel_spmd as _run

    arrays = {name: _np.asarray(a) for name, a in inputs.items()}
    arrays["x"], arrays["mem"] = arrays["x"][0], arrays["mem"][0]
    arrays["positions"] = arrays["positions"][0].reshape(NT, P).T
    arrays.update(constants())
    arrays = {name + "_dram": _np.ascontiguousarray(a) for name, a in arrays.items()}
    nc = _bacc.Bacc("TRN2", target_bir_lowering=False, num_devices=1)
    args = {name[:-5]: nc.dram_tensor(name, a.shape, mybir.dt.from_np(a.dtype), kind="ExternalInput").ap()
            for name, a in arrays.items()}
    args["out"] = nc.dram_tensor("out_dram", (SEQ, D), F32, kind="ExternalOutput").ap()
    for name, (shape, dt) in SCRATCH.items():
        args[name] = nc.dram_tensor(name + "_dram", shape, dt, kind="Internal").ap()
    build(nc, args)
    return _run(nc, [arrays], core_ids=[0]).results[0]["out_dram"][None]
```

```python
from contextlib import ExitStack

import numpy as np

import concourse.bass as bass
from concourse import mybir

F32 = mybir.dt.float32
F32R = mybir.dt.float32r
I32 = mybir.dt.int32
U32 = mybir.dt.uint32
BF16 = mybir.dt.bfloat16
ALU = mybir.AluOpType
ACT = mybir.ActivationFunctionType
AX = mybir.AxisListType

P = 128
D = 1024
SEQ = 1024
NT = SEQ // P
KD = D // P
HD = 64
AH, BH, CH = 8, 4, 4
AW, BW, CW = AH * HD, BH * HD, CH * HD
COLS = 3 * AW + 4 * BW + CW
BC0 = 3 * AW
BCW = COLS - BC0
N_MEM = 256
MT = N_MEM // P
CHUNK = 64
LEFT = 8
WIN = (LEFT * CHUNK) // P + 1
KEEP = WIN + 1
MAX_REL = 128
REL = MAX_REL + CHUNK
EXT = 2 * P + P - 1
NG, EG = 4, 8
NE = NG * EG
DE = D // 2
NLG = NG + NE
CAP = P
FULL = SEQ * 2 // CAP
BLOCKS = NE + FULL
LEVELS = SEQ // CAP
PLACES = LEVELS * NE
KF = DE // P
SKIP = 1 << 20
EPS = 1e-6
NEG = -1e30


class Steps:

    def __init__(self, eng, sem, base=0):
        self.eng, self.sem, self.base, self.n = eng, sem, base, 0

    def __call__(self, ins):
        self.n += 1
        ins.then_inc(self.sem, 1)
        self.eng.wait_ge(self.sem, self.base + self.n)


class Core:

    def __init__(self, nc, ctx):
        self.nc, self.ctx = nc, ctx
        self.sems = []

    def sem(self, name):
        self.sems.append(self.nc.alloc_semaphore(name=name))
        return self.sems[-1]

    def reuse_sems(self):
        self.nc.clear_and_free_semaphores(self.sems)
        self.nc.all_engine_barrier()
        self.sems = []

    def psum(self, name, banks=1):
        return self.ctx.enter_context(self.nc.psum_tensor(name, [P, 512 * banks], F32))


def sbuf(nc, stack, name, shape, dt=F32):
    return stack.enter_context(nc.sbuf_tensor(name, shape, dt))


def rows(ap, k):
    return ap.rearrange("(p k) n -> p k n", k=k)


def product(pe, out, a, b, first=True, last=True):
    (ah, al), (bh, bl) = a, b
    pe.matmul(out, ah, bh, start=first, stop=False, skip_group_check=True)
    pe.matmul(out, ah, bl, start=False, stop=False, skip_group_check=True)
    return pe.matmul(out, al, bh, start=False, stop=last, skip_group_check=True)


class Filled:

    def __init__(self, c, name, fills, by_dve, by_act=None):
        self.fills, self.by_dve = fills, by_dve
        self.by_act = list(range(fills)) if by_act is None else by_act
        self.full, self.hi, self.lo = c.sem(f"{name}_full"), c.sem(f"{name}_hi"), c.sem(f"{name}_lo")

    def wait_full(self, eng, t, f):
        eng.wait_ge(self.full, self.fills * t + f + 1)

    def wait_hi(self, eng, t, f):
        eng.wait_ge(self.hi, len(self.by_act) * t + self.by_act.index(f) + 1)

    def wait_free(self, eng, t, f):
        if f in self.by_dve:
            eng.wait_ge(self.lo, len(self.by_dve) * t + self.by_dve.index(f) + 1)
        else:
            self.wait_hi(eng, t, f)

    def wait_before(self, eng, t, f, first):
        if f:
            self.wait_free(eng, t, f - 1)
        elif not first:
            self.wait_free(eng, t - 1, self.fills - 1)


def wait_apart(eng, sem, value, passed):
    eng.wait_ge(sem, value)
    eng.sem_inc(passed, 1)


def heads(ap):
    return ap.rearrange("p (h e) -> p h e", e=HD)


def tiles(ap):
    return ap.rearrange("p (k n) -> p k n", n=P)


def wide(ap, n):
    return ap.unsqueeze(2).to_broadcast([ap.shape[0], ap.shape[1], n])


class Weights:

    def __init__(self, c, st, name, src, gain, width, slots, raw=None):
        self.src, self.gain, self.slots = src, gain, slots
        self.raw = sbuf(c.nc, st, f"{name}_raw", [P, slots, width]) if raw is None else raw
        self.h = sbuf(c.nc, st, f"{name}_wh", [P, KD, width], F32R)
        self.l = sbuf(c.nc, st, f"{name}_wl", [P, KD, width], F32R)
        self.loaded = [c.sem(f"{name}_w_loaded{i}") for i in range(slots)]
        self.hi, self.lo = c.sem(f"{name}_w_hi"), c.sem(f"{name}_w_lo")
        self.g, self.gained = sbuf(c.nc, st, f"{name}_w_g", [P, KD]), c.sem(f"{name}_w_gained")

    def load(self, sp, ks):
        for k in ks:
            if k == 0:
                sp.dma_start(self.g[:], self.gain.rearrange("(p k) -> p k", k=KD)).then_inc(self.gained, 16)
            if k >= self.slots:
                sp.wait_ge(self.lo, k - self.slots + 1)
            sp.dma_start(self.raw[:, k % self.slots, :], self.src[:, k, :]).then_inc(self.loaded[k % self.slots], 16)

    def split_hi(self, act, k):
        if k == 0:
            act.wait_ge(self.gained, 16)
        act.wait_ge(self.loaded[k % self.slots], 16 * (k // self.slots + 1))
        act.activation(self.h[:, k, :], self.raw[:, k % self.slots, :], ACT.Copy, scale=self.g[:, k:k + 1]).then_inc(self.hi, 1)

    def split_lo(self, dve, k):
        dve.wait_ge(self.hi, k + 1)
        dve.scalar_tensor_tensor(self.l[:, k, :], self.raw[:, k % self.slots, :], self.g[:, k:k + 1],
                                 self.h[:, k, :].bitcast(F32), ALU.mult, ALU.subtract).then_inc(self.lo, 1)


def phase_a(c, d):
    nc = c.nc
    with ExitStack() as st:
        W = Weights(c, st, "a", rows(d["w_in"], KD)[:, :, 0:3 * AW], d["mix_norm_g"], 3 * AW, 4)
        NP = AH // 2
        t_ = lambda name, shape, dt=F32: sbuf(nc, st, "a_" + name, shape, dt)
        kT, V = t_("kt", [P, NP, KEEP * P]), t_("v", [P, KEEP, AW])
        bias, ext, rev = t_("bias", [P, AH, 2 * P]), t_("ext", [AH, EXT]), t_("rev", [AH, REL])
        xb = t_("x", [P, 2, D])
        xTh, xTl = t_("xth", [P, KD, P], F32R), t_("xtl", [P, KD, P], F32R)
        qT = t_("qt", [P, 2, NP, P])
        qk, qkn, sq = t_("qk", [P, 2, AW]), t_("qkn", [P, 2, AW]), t_("sq", [P, AW])
        junk = t_("junk", [P, D], BF16)
        Pr, PTs = t_("p", [P, 2, WIN * P]), t_("pt", [P, 2, WIN * P])
        ident = t_("ident", [P, P])
        gq, gk, gq8, mhalf = t_("gq", [P, 1]), t_("gk", [P, 1]), t_("gq8", [P, 1]), t_("mhalf", [P, AH])
        ssx, msx, rx = t_("ssx", [P, NT]), t_("msx", [P, 1]), t_("rx", [P, NT])
        ssh, msh, rh = t_("ssh", [P, 2, AH]), t_("msh", [P, 2, AH]), t_("rh", [P, 2, AH])
        nmax, rs, rinv = t_("nmax", [P, 2]), t_("rs", [P, 2, AH]), t_("rinv", [P, AH])
        mixt = t_("mix", [P, 2, AW])

        S = [c.bank2[0], c.bank2[1]]
        PT = c.bank2[2]
        O, PJ = c.bank[0], c.bank[1]

        XT0, XT1, Q, K, V_, QT, KT = range(7)
        pj = Filled(c, "a_pj", 7, [XT0, XT1, KT], [XT0, XT1, Q, K, V_, QT])
        s_ = lambda name: c.sem("a_" + name)
        const_in, rev_in, ext_out, bias_in = map(s_, ("const_in", "rev_in", "ext_out", "bias_in"))
        x_in = [s_(f"x_in{i}") for i in range(2)]
        mix_out = [s_(f"mix_out{i}") for i in range(2)]
        pool_const, ext_set, gq8_set = map(s_, ("pool_const", "ext_set", "gq8_set"))
        ssx_done, msx_done, rx_done = map(s_, ("ssx_done", "msx_done", "rx_done"))
        sq_done, ssh_done, msh_done, rh_done, qkn_done = map(s_, ("sq_done", "ssh_done", "msh_done", "rh_done", "qkn_done"))
        s_done, biased, max_done, exp_done, pt_done, ptc_done, pv_done = map(
            s_, ("s_done", "biased", "max_done", "exp_done", "pt_done", "ptc_done", "pv_done"))
        rinv_done, mix_done = s_("rinv_done"), s_("mix_done")
        block = st.enter_context(nc.Block())
        N = NT * AH
        CONSTS = 16 * 5

        def nblk(t):
            return min(t, WIN - 1) + 1

        PIECES = [XT1, Q, K, (V_, 0), (V_, 1), QT, KT, XT0]

        def pieces(t, h):
            tile = t + 1 + (h == AH - 1)
            return [(tile, PIECES[h])] if tile < NT else []

        def whole(t, h):
            return [(tile, f[0] if isinstance(f, tuple) else f) for tile, f in pieces(t, h) if f != (V_, 0)]

        @block.sync
        def _(sp):
            sp.dma_start(xb[:, 0, :], d["x"][0:P, :]).then_inc(x_in[0], 16)
            sp.dma_start(ident[:], d["ident"]).then_inc(const_in, 16)
            W.load(sp, [0])
            for half in range(2):
                sp.dma_start(gq[64 * half:64 * half + 64, :], d["qn_a"].rearrange("(p a) -> p a", a=1)).then_inc(const_in, 16)
                sp.dma_start(gk[64 * half:64 * half + 64, :], d["kn_a"].rearrange("(p a) -> p a", a=1)).then_inc(const_in, 16)
            W.load(sp, [1])
            sp.dma_start(rev[:], d["rel_bias"]).then_inc(rev_in, 16)
            W.load(sp, range(2, KD))
            sp.wait_ge(ext_set, 1)
            sp.dma_start(d["ext_dram"], ext[:]).then_inc(ext_out, 16)
            sp.wait_ge(ext_out, 16)
            toeplitz = bass.AP(d["ext_dram"].tensor, 0, [[1, P], [EXT, AH], [1, 2 * P]])
            sp.dma_start(bias[:], toeplitz).then_inc(bias_in, 16)

            def store(t):
                sp.wait_ge(mix_done, t + 1)
                sp.dma_start(d["mix"][t * P:(t + 1) * P, 0:AW], mixt[:, t % 2, :]).then_inc(mix_out[t % 2], 16)

            for t in range(1, NT):
                if t >= 2:
                    sp.wait_ge(ssx_done, t - 1)
                    pj.wait_full(sp, t - 2, XT1)
                sp.dma_start(xb[:, t % 2, :], d["x"][t * P:(t + 1) * P, :]).then_inc(x_in[t % 2], 16)
                if t >= 2:
                    store(t - 2)
            store(NT - 2)
            store(NT - 1)
            for i in range(2):
                sp.wait_ge(mix_out[i], 16 * (NT // 2))

        @block.gpsimd
        def _(pool):
            pool.memset(mhalf[:], -0.5).then_inc(pool_const, 1)
            pool.wait_ge(pool_const, 1)

            def x_scale(t):
                pool.wait_ge(ssx_done, t + 1)
                pool.tensor_scalar(msx[:], ssx[:, t:t + 1], 1.0 / D, EPS, ALU.mult, ALU.add).then_inc(msx_done, 1)
                pool.wait_ge(msx_done, t + 1)
                pool.tensor_tensor(rx[:, t:t + 1], msx[:], mhalf[:, 0:1], ALU.pow).then_inc(rx_done, 1)

            def head_scale(t, i):
                n = 2 * t + i + 1
                pj.wait_hi(pool, t, Q + i)
                if n >= 2:
                    pool.wait_ge(ssh_done, n - 1)
                pool.tensor_tensor(sq[:], qk[:, i, :], qk[:, i, :], ALU.mult).then_inc(sq_done, 1)
                pool.wait_ge(ssh_done, n)
                pool.tensor_scalar(msh[:, i, :], ssh[:, i, :], 1.0 / HD, EPS, ALU.mult, ALU.add).then_inc(msh_done, 1)
                pool.wait_ge(msh_done, n)
                pool.tensor_tensor(rh[:, i, :], msh[:, i, :], mhalf[:], ALU.pow).then_inc(rh_done, 1)

            for t in range(NT):
                x_scale(t)
                head_scale(t, 0)
                head_scale(t, 1)

        @block.scalar
        def _(act):
            def sum_squares(t):
                act.wait_ge(x_in[t % 2], 16 * (t // 2 + 1))
                if t:
                    act.wait_ge(ssx_done, t)
                act.activation(junk[:], xb[:, t % 2, :], ACT.Square, accum_out=ssx[:, t:t + 1]).then_inc(ssx_done, 1)

            def take(t, f):
                if f not in pj.by_act:
                    return
                pj.wait_full(act, t, f)
                if f in (XT0, XT1):
                    i = act.activation(xTh[:, 4 * f:4 * f + 4, :], tiles(PJ[:]), ACT.Copy)
                elif f in (Q, K):
                    act.wait_ge(rx_done, t + 1)
                    i = act.activation(qk[:, f - Q, :], PJ[:], ACT.Copy, scale=rx[:, t:t + 1])
                elif f == V_:
                    i = act.activation(V[:, t % KEEP, :], PJ[:], ACT.Copy, scale=rx[:, t:t + 1])
                else:
                    i = act.activation(qT[:, t % 2], tiles(PJ[:]), ACT.Copy, scale=gq8[:])
                i.then_inc(pj.hi, 1)

            def exps(n):
                t, h = divmod(n, AH)
                w = nblk(t) * P
                act.wait_ge(max_done, n + 1)
                if n >= 2:
                    act.wait_ge(pt_done, n - 1)
                act.activation(Pr[:, n % 2, 0:w], S[n % 2][:, 640 - w:640], ACT.Exp, bias=nmax[:, n % 2:n % 2 + 1],
                               accum_out=rs[:, t % 2, h:h + 1]).then_inc(exp_done, 1)

            def turned(n):
                w = nblk(n // AH) * P
                act.wait_ge(pt_done, n + 1)
                if n >= 2:
                    act.wait_ge(pv_done, n - 1)
                act.activation(PTs[:, n % 2, 0:w], PT[:, 0:w], ACT.Copy).then_inc(ptc_done, 1)

            take(0, XT0)
            W.split_hi(act, 0)
            take(0, XT1)
            for k in range(1, KD):
                W.split_hi(act, k)
                if k == 2:
                    sum_squares(0)
            act.wait_ge(gq8_set, 1)
            for f in range(Q, KT):
                take(0, f)
            take(1, XT0)
            sum_squares(1)
            exps(0)
            for t in range(NT):
                for h in range(AH):
                    n = t * AH + h
                    turned(n)
                    if n + 1 < N:
                        exps(n + 1)
                    for tile, f in whole(t, h):
                        take(tile, f)
                    if h == AH - 1 and t + 2 < NT:
                        sum_squares(t + 2)

        @block.tensor
        def _(pe):
            def fill(t, f):
                f, part = f if isinstance(f, tuple) else (f, None)
                if part != 1:
                    pj.wait_before(pe, t, f, t == 0)
                if f in (XT0, XT1):
                    pe.wait_ge(x_in[t % 2], 16 * (t // 2 + 1))
                    xs = xb[:, t % 2, :].rearrange("p (m k) -> p k m", k=KD)
                    for j in range(4):
                        mm = pe.transpose(PJ[:, j * P:(j + 1) * P], xs[:, 4 * f + j, :], ident[:])
                elif f in (Q, K, V_):
                    cols = slice((f - Q) * AW, (f - Q + 1) * AW)
                    for k in range(KD) if part is None else range(4 * part, 4 * part + 4):
                        if t == 0 and f == Q:
                            pe.wait_ge(W.lo, k + 1)
                        mm = product(pe, PJ[:], (xTh[:, k, :], xTl[:, k, :]), (W.h[:, k, cols], W.l[:, k, cols]),
                                     k == 0, k == KD - 1)
                else:
                    pe.wait_ge(qkn_done, 2 * t + f - QT + 1)
                    for p in range(NP):
                        mm = pe.transpose(PJ[:, p * P:(p + 1) * P], qkn[:, f - QT, p * P:(p + 1) * P], ident[:])
                if part != 0:
                    mm.then_inc(pj.full, 1)

            def runs(t):
                out = []
                for kt in range(t + 1 - nblk(t), t + 1):
                    at = WIN - (t + 1 - kt)
                    if out and kt % KEEP and at != 4:
                        out[-1][2] += 1
                    else:
                        out.append([kt % KEEP, at, 1])
                return out

            def scores(n):
                t, h = divmod(n, AH)
                p, r = h // 2, slice(64 * (h % 2), 64 * (h % 2) + 64)
                if h == 0:
                    pj.wait_free(pe, t, KT)
                if n >= 2:
                    pe.wait_ge(exp_done, n - 1)
                for slot, at, length in runs(t):
                    mm = pe.matmul(S[n % 2][:, at * P:(at + length) * P], qT[r, t % 2, p, :],
                                   kT[r, p, slot * P:(slot + length) * P], start=True, stop=True)
                mm.then_inc(s_done, 1)

            def turn(n):
                pe.wait_ge(exp_done, n + 1)
                if n >= 1:
                    pe.wait_ge(ptc_done, n)
                for b in range(nblk(n // AH)):
                    mm = pe.transpose(PT[:, b * P:(b + 1) * P], Pr[:, n % 2, b * P:(b + 1) * P], ident[:])
                mm.then_inc(pt_done, 1)

            def values(n):
                t, h = divmod(n, AH)
                pe.wait_ge(ptc_done, n + 1)
                if h == 0 and t >= 1:
                    pe.wait_ge(mix_done, t)
                cols, last = slice(h * HD, (h + 1) * HD), nblk(t) - 1
                for b in range(last + 1):
                    mm = pe.matmul(O[:, cols], PTs[:, n % 2, b * P:(b + 1) * P], V[:, (t - last + b) % KEEP, cols],
                                   start=b == 0, stop=b == last, skip_group_check=True)
                mm.then_inc(pv_done, 1)

            pe.wait_ge(const_in, CONSTS)
            for f in range(7):
                fill(0, f)
            fill(1, XT0)
            scores(0)
            scores(1)
            for t in range(NT):
                for h in range(AH):
                    n = t * AH + h
                    turn(n)
                    for tile, f in pieces(t, h):
                        fill(tile, f)
                    if n:
                        values(n - 1)
                    if n + 2 < N:
                        scores(n + 2)
            values(N - 1)

        @block.vector
        def _(dve):
            own = Steps(dve, c.sem("a_dve"))

            def take(t, f):
                slot = t % KEEP
                if f in (XT0, XT1):
                    pj.wait_hi(dve, t, f)
                    dve.tensor_tensor(xTl[:, 4 * f:4 * f + 4, :], tiles(PJ[:]), xTh[:, 4 * f:4 * f + 4, :].bitcast(F32),
                                      ALU.subtract).then_inc(pj.lo, 1)
                elif f == KT:
                    pj.wait_full(dve, t, f)
                    dve.tensor_scalar(kT[:, :, slot * P:(slot + 1) * P], tiles(PJ[:]), gk[:], None, ALU.mult).then_inc(pj.lo, 1)

            def head_sums(t, i):
                dve.wait_ge(sq_done, 2 * t + i + 1)
                dve.tensor_reduce(ssh[:, i, :], heads(sq[:]), AX.X, ALU.add).then_inc(ssh_done, 1)

            def head_norm(t, i):
                dve.wait_ge(rh_done, 2 * t + i + 1)
                dve.tensor_tensor(heads(qkn[:, i, :]), heads(qk[:, i, :]), wide(rh[:, i, :], HD), ALU.mult).then_inc(qkn_done, 1)

            def maxes(n):
                t, h = divmod(n, AH)
                w = nblk(t) * P
                s = S[n % 2]
                dve.wait_ge(s_done, n + 1)
                if n >= 2:
                    dve.wait_ge(exp_done, n - 1)
                if t == 0:
                    ins = dve.tensor_tensor(s[:, 512:640], s[:, 512:640], bias[:, h, P - 1::-1], ALU.add)
                else:
                    ins = dve.tensor_tensor(s[:, 384:640], s[:, 384:640], bias[:, h, ::-1], ALU.add)
                if nblk(t) == WIN:
                    ins = dve.tensor_scalar(s[64:128, 0:64], s[64:128, 0:64], NEG, None, ALU.add)
                ins.then_inc(biased, 1)
                dve.wait_ge(biased, n + 1)
                dve.tensor_reduce(nmax[:, n % 2:n % 2 + 1], s[:, 640 - w:640], AX.X, ALU.max, negate=True).then_inc(max_done, 1)

            def finish(t):
                dve.wait_ge(exp_done, AH * (t + 1))
                dve.reciprocal(rinv[:], rs[:, t % 2, :]).then_inc(rinv_done, 1)
                dve.wait_ge(rinv_done, t + 1)
                dve.wait_ge(pv_done, AH * (t + 1))
                if t >= 2:
                    dve.wait_ge(mix_out[t % 2], 16 * (t // 2))
                dve.tensor_tensor(heads(mixt[:, t % 2, :]), heads(O[:]), wide(rinv[:], HD), ALU.mult).then_inc(mix_done, 1)

            dve.wait_ge(const_in, CONSTS)
            dve.tensor_scalar(gq8[:], gq[:], HD ** -0.5, None, ALU.mult).then_inc(gq8_set, 1)
            take(0, XT0)
            W.split_lo(dve, 0)
            take(0, XT1)
            for k in range(1, KD):
                W.split_lo(dve, k)
            dve.wait_ge(rev_in, 16)
            dve.memset(ext[:, 0:CHUNK], NEG)
            dve.memset(ext[:, CHUNK + REL:EXT], 0.0)
            dve.tensor_scalar(ext[:, CHUNK:CHUNK + REL], rev[:], rev[:, REL - 1:REL], None, ALU.subtract).then_inc(ext_set, 1)
            for i in range(2):
                head_sums(0, i)
                head_norm(0, i)
            take(0, KT)
            take(1, XT0)
            dve.wait_ge(bias_in, 16)
            own(dve.memset(bias[0:64, :, 0:64], NEG))
            maxes(0)
            for t in range(NT):
                for h in range(AH):
                    n = t * AH + h
                    if n + 1 < N:
                        maxes(n + 1)
                    if t + 1 < NT:
                        if h == 2:
                            head_sums(t + 1, 0)
                        elif h == 3:
                            head_norm(t + 1, 0)
                            head_sums(t + 1, 1)
                        elif h == 4:
                            head_norm(t + 1, 1)
                    for tile, f in whole(t, h):
                        take(tile, f)
                    if h == 0 and t:
                        finish(t - 1)
            finish(NT - 1)


TWO_PI = 2 * np.pi
TURN1 = 6.28125
TURN2 = float(np.float32(round((TWO_PI - TURN1) * 2 ** 21) / 2 ** 21))
TURN3 = float(np.float32(TWO_PI - TURN1 - TURN2))
ROUND = 1.5 * 2 ** 23
PI_BELOW = 3.1415925


assert NT == KD


def w_out_row(raw, k):
    per = KD * DE // D
    return raw[:, k // per, (k % per) * D:(k % per + 1) * D]


AHEAD = 4


def phase_m(c, d, kT, V, cos, sin, WB, raw, ident, xb, x_in):
    nc = c.nc
    with ExitStack() as st:
        W = Weights(c, st, "m", rows(d["w_mem_kv"], KD), d["mem_norm_g"], 2 * CW, KD,
                    raw[:, 0, :].rearrange("p (k n) -> p k n", n=2 * CW))
        mb = raw[:, 1, 0:MT * D].rearrange("p (m n) -> p m n", m=MT)
        mTh = sbuf(nc, st, "m_mth", [P, MT, KD * P], F32R)
        mTl = sbuf(nc, st, "m_mtl", [P, MT, KD * P], F32R)
        km = sbuf(nc, st, "m_k", [P, MT, CW])
        kn = sbuf(nc, st, "m_kn", [P, MT, CW])
        sq = sbuf(nc, st, "m_sq", [P, CW])
        junk = sbuf(nc, st, "m_junk", [P, D], BF16)
        gk = sbuf(nc, st, "m_gk", [P, 1])
        mhalf = sbuf(nc, st, "m_mhalf", [P, CH])
        ss = sbuf(nc, st, "m_ss", [P, MT])
        ms = sbuf(nc, st, "m_ms", [P, MT])
        r = sbuf(nc, st, "m_r", [P, MT])
        ssh = sbuf(nc, st, "m_ssh", [P, MT, CH])
        msh = sbuf(nc, st, "m_msh", [P, MT, CH])
        rh = sbuf(nc, st, "m_rh", [P, MT, CH])
        pos = sbuf(nc, st, "m_pos", [P, NT], I32)
        posf = sbuf(nc, st, "m_posf", [P, NT])
        inv = sbuf(nc, st, "m_inv", [P, HD // 2])
        ang = sbuf(nc, st, "m_ang", [P, NT, HD // 2])
        turns = sbuf(nc, st, "m_turns", [P, 2, NT, HD // 2])
        rest = sbuf(nc, st, "m_rest", [P, 2, NT, HD // 2])
        XT, KV, KT = c.bank2[0:2], c.bank, [c.bank2[2][:, 512 * m:512 * m + CW] for m in range(MT)]
        xt_done, xt_hi, xt_lo, kv_done, k_taken, kt_done = (
            c.sem(f"m_{n}") for n in ("xt_done", "xt_hi", "xt_lo", "kv_done", "k_taken", "kt_done"))
        const_in, mem_in = c.sem("m_const_in"), [c.sem(f"m_mem_in{i}") for i in range(MT)]
        pool_own, ss_done, r_done, sq_done, ssh_done, rh_done, kn_done = (
            c.sem(f"m_{n}") for n in ("pool", "ss_done", "r_done", "sq_done", "ssh_done", "rh_done", "kn_done"))
        angles, sines = c.sem("m_angles"), c.sem("m_sines")
        CONSTS = 16 * 5
        block = st.enter_context(nc.Block())

        @block.sync
        def _(sp):
            sp.dma_start(mb[:, 0, :], d["mem"][0:P, :]).then_inc(mem_in[0], 16)
            sp.dma_start(ident[:], d["ident"]).then_inc(const_in, 16)
            sp.dma_start(mb[:, 1, :], d["mem"][P:2 * P, :]).then_inc(mem_in[1], 16)
            for half in range(2):
                sp.dma_start(gk[64 * half:64 * half + 64, :], d["kn_c"].rearrange("(p a) -> p a", a=1)).then_inc(const_in, 16)
            sp.dma_start(pos[:], d["positions"]).then_inc(const_in, 16)
            sp.dma_start(inv[:], d["inv_freq"].partition_broadcast(P)).then_inc(const_in, 16)
            W.load(sp, range(KD))
            for t in range(2):
                sp.dma_start(xb[:, t, :], d["x"][t * P:(t + 1) * P, :]).then_inc(x_in[t], 16)
            WB.load(sp, range(AHEAD + WB.slots))

        @block.gpsimd
        def _(pool):
            own = Steps(pool, pool_own)
            own(pool.memset(mhalf[:], -0.5))
            for m in range(MT):
                pool.wait_ge(ss_done, m + 1)
                own(pool.tensor_scalar(ms[:, m:m + 1], ss[:, m:m + 1], 1.0 / D, EPS, ALU.mult, ALU.add))
                pool.tensor_tensor(r[:, m:m + 1], ms[:, m:m + 1], mhalf[:, 0:1], ALU.pow).then_inc(r_done, 1)
            for m in range(MT):
                pool.wait_ge(k_taken, m + 1)
                pool.tensor_tensor(sq[:], km[:, m, :], km[:, m, :], ALU.mult).then_inc(sq_done, 1)
                pool.wait_ge(ssh_done, m + 1)
                own(pool.tensor_scalar(msh[:, m, :], ssh[:, m, :], 1.0 / HD, EPS, ALU.mult, ALU.add))
                pool.tensor_tensor(rh[:, m, :], msh[:, m, :], mhalf[:], ALU.pow).then_inc(rh_done, 1)

        @block.scalar
        def _(act):
            def transposed(m):
                act.wait_ge(xt_done, m + 1)
                act.activation(mTh[:, m, :], XT[m][:], ACT.Copy).then_inc(xt_hi, 1)

            def take(m):
                act.wait_ge(r_done, m + 1)
                act.wait_ge(kv_done, m + 1)
                act.activation(km[:, m, :], KV[m][:, 0:CW], ACT.Copy, scale=r[:, m:m + 1]).then_inc(k_taken, 1)
                act.activation(V[:, m, :], KV[m][:, CW:2 * CW], ACT.Copy, scale=r[:, m:m + 1])

            transposed(0)
            for k in range(KD):
                W.split_hi(act, k)
            transposed(1)
            for m in range(MT):
                if m:
                    act.wait_ge(ss_done, m)
                act.activation(junk[:], mb[:, m, :], ACT.Square, accum_out=ss[:, m:m + 1]).then_inc(ss_done, 1)
            take(0)
            for k in range(AHEAD):
                WB.split_hi(act, k)
            take(1)
            act.wait_ge(angles, 1)
            act.activation(sin[:], rest[:, 0], ACT.Sin).then_inc(sines, 1)
            act.activation(cos[:], rest[:, 1], ACT.Sin).then_inc(sines, 1)

        @block.tensor
        def _(pe):
            pe.wait_ge(const_in, CONSTS)
            for m in range(MT):
                pe.wait_ge(mem_in[m], 16)
                xs = mb[:, m, :].rearrange("p (m k) -> p k m", k=KD)
                for k in range(KD):
                    mm = pe.transpose(XT[m][:, k * P:(k + 1) * P], xs[:, k, :], ident[:])
                mm.then_inc(xt_done, 1)
            for m in range(MT):
                pe.wait_ge(xt_lo, m + 1)
                for k in range(KD):
                    if m == 0:
                        pe.wait_ge(W.lo, k + 1)
                    at = slice(k * P, (k + 1) * P)
                    mm = product(pe, KV[m][:], (mTh[:, m, at], mTl[:, m, at]), (W.h[:, k, :], W.l[:, k, :]), k == 0, k == KD - 1)
                mm.then_inc(kv_done, 1)
            for m in range(MT):
                pe.wait_ge(kn_done, m + 1)
                for p in range(CH // 2):
                    mm = pe.transpose(KT[m][:, p * P:(p + 1) * P], kn[:, m, p * P:(p + 1) * P], ident[:])
                mm.then_inc(kt_done, 1)

        @block.vector
        def _(dve):
            own = Steps(dve, c.sem("m_dve"))

            def transposed(m):
                dve.wait_ge(xt_hi, m + 1)
                dve.tensor_tensor(mTl[:, m, :], XT[m][:], mTh[:, m, :].bitcast(F32), ALU.subtract).then_inc(xt_lo, 1)

            transposed(0)
            for k in range(KD):
                W.split_lo(dve, k)
            transposed(1)
            dve.wait_ge(const_in, CONSTS)
            own(dve.tensor_copy(posf[:], pos[:]))
            own(dve.tensor_tensor(ang[:], wide(posf[:], HD // 2), inv[:].unsqueeze(1).to_broadcast([P, NT, HD // 2]), ALU.mult))
            for i, quarter in enumerate((0.0, 0.25)):
                own(dve.tensor_scalar(turns[:, i], ang[:], 1 / TWO_PI, quarter, ALU.mult, ALU.add))
                own(dve.tensor_scalar(turns[:, i], turns[:, i], ROUND, None, ALU.add))
                own(dve.tensor_scalar(turns[:, i], turns[:, i], -ROUND, None, ALU.add))
                own(dve.scalar_tensor_tensor(rest[:, i], turns[:, i], -TURN1, ang[:], ALU.mult, ALU.add))
                own(dve.scalar_tensor_tensor(rest[:, i], turns[:, i], -TURN2, rest[:, i], ALU.mult, ALU.add))
                own(dve.scalar_tensor_tensor(rest[:, i], turns[:, i], -TURN3, rest[:, i], ALU.mult, ALU.add))
                own(dve.tensor_scalar(rest[:, i], rest[:, i], quarter * TWO_PI, PI_BELOW, ALU.add, ALU.min))
                own(dve.tensor_scalar(rest[:, i], rest[:, i], -PI_BELOW, None, ALU.max))
            dve.sem_inc(angles, 1)
            for m in range(MT):
                dve.wait_ge(sq_done, m + 1)
                dve.tensor_reduce(ssh[:, m, :], heads(sq[:]), AX.X, ALU.add).then_inc(ssh_done, 1)
                dve.wait_ge(rh_done, m + 1)
                dve.tensor_tensor(heads(kn[:, m, :]), heads(km[:, m, :]), wide(rh[:, m, :], HD), ALU.mult).then_inc(kn_done, 1)
                if m == 0:
                    for k in range(AHEAD):
                        WB.split_lo(dve, k)
            for m in range(MT):
                dve.wait_ge(kt_done, m + 1)
                dve.tensor_scalar(kT[:, :, m * P:(m + 1) * P], tiles(KT[m]), gk[:], None, ALU.mult)


def phase_bc(c, d, raw):
    nc = c.nc
    with ExitStack() as st:
        kTC = sbuf(nc, st, "c_kt", [P, CH // 2, N_MEM])
        VC = sbuf(nc, st, "c_v", [P, MT, CW])
        cos = sbuf(nc, st, "b_cos", [P, NT, HD // 2])
        sin = sbuf(nc, st, "b_sin", [P, NT, HD // 2])
        W = Weights(c, st, "b", rows(d["w_in"], KD)[:, :, BC0:COLS], d["mix_norm_g"], BCW, 3,
                    raw[:, 2, 0:3 * BCW].rearrange("p (k n) -> p k n", n=BCW))
        t_ = lambda name, shape, dt=F32: sbuf(nc, st, "b_" + name, shape, dt)
        xb, ident = t_("x", [P, 2, D]), t_("ident", [P, P])
        x_in = [c.sem(f"b_x_in{i}") for i in range(2)]
        phase_m(c, d, kTC, VC, cos, sin, W, raw, ident, xb, x_in)
        xTh, xTl = t_("xth", [P, 2, KD * P], F32R), t_("xtl", [P, 2, KD * P], F32R)
        junk = t_("junk", [P, D], BF16)
        tri = t_("tri", [P, P])
        dec, g128 = t_("dec", [P, 2 * BH]), t_("g128", [P, BH // 2])
        gng = t_("gng", [P, BW])
        gqc, gqc8 = t_("gqc", [P, 1]), t_("gqc8", [P, 1])
        mhalf = t_("mhalf", [P, CH])
        ssx, msx, rx = t_("ssx", [P, 1]), t_("msx", [P, 1]), t_("rx", [P, 1])
        qk = t_("qk", [P, 2 * BW])
        byc, bys = t_("byc", [P, 2 * BW]), t_("bys", [P, 2 * BW])
        rot, qkr = t_("rot", [P, 2 * BW]), t_("qkr", [P, 2 * BW])
        v, g = t_("v", [P, 2, BW]), t_("g", [P, 2, BW])
        eg, sg = t_("eg", [P, BW]), t_("sg", [P, BW])
        qkT = t_("qkt", [P, BH, P])
        Sm = t_("sm", [P, BH, P])
        R, Rt = t_("r", [P, BH // 2, HD]), t_("rt", [P, BH // 2, HD])
        qc, qcn, sqc = t_("qc", [P, CW]), t_("qcn", [P, CW]), t_("sqc", [P, CW])
        ssc, msc, rc = t_("ssc", [P, CH]), t_("msc", [P, CH]), t_("rc", [P, CH])
        qTC = t_("qtc", [P, CH // 2, P])
        nmax, rs, rinv = t_("nmax", [P, CH]), t_("rs", [P, CH]), t_("rinv", [P, CH])
        Pr = t_("p", [P, CH, N_MEM])
        PTs = t_("pt", [P, CH * N_MEM])
        sm4, mean, ss4, ms4, r4 = (t_(n, [P, BH]) for n in ("sm4", "mean", "ss4", "ms4", "r4"))
        cent, csq, y, yg = (t_(n, [P, BW]) for n in ("cent", "csq", "y", "yg"))
        mixt = t_("mix", [P, BW + CW])

        SC, PT, O = c.bank2[0], c.bank2[1], c.bank2[2]
        SB, XT = PT, SC
        TR, PJ = c.bank[0], c.bank[1]

        def place(h, width, base=0):
            at = (h % 2) * 512 + base + (h // 2) * width
            return slice(at, at + width)

        def by_head(ap, width, base=0):
            return ap.rearrange("p (s c) -> p s c", s=2)[:, :, base:base + 2 * width].rearrange("p s (a e) -> p s a e", a=2)

        def halves(ap):
            return ap.rearrange("p (a s e) -> p s a e", s=2, a=2)

        def halves1(ap):
            return ap.rearrange("p (a s) -> p s a", s=2)

        QK, VG, QC = range(3)
        pj = Filled(c, "b_pj", 3, [])
        QKT, QCT, U = range(3)
        tr = Filled(c, "b_tr", 3, [QCT, U], [QKT])
        s_ = lambda name: c.sem("b_" + name)
        w_out_in = s_("w_out_in")
        xt_done, xt_hi, xt_lo = map(s_, ("xt_done", "xt_hi", "xt_lo"))
        const_in, mix_out, state0 = map(s_, ("const_in", "mix_out", "state0"))
        ssx_done, rx_done, pool_own, dve_own = map(s_, ("ssx_done", "rx_done", "pool", "dve"))
        rotated, qkr_done, sb_done, sm_done = map(s_, ("rotated", "qkr_done", "sb_done", "sm_done"))
        sc_done, max_done, exp_done, pt_done, ptc_done, r_done = map(
            s_, ("sc_done", "max_done", "exp_done", "pt_done", "ptc_done", "r_done"))
        sqc_done, ssc_done, rc_done, qcn_done = map(s_, ("sqc_done", "ssc_done", "rc_done", "qcn_done"))
        o_done, cent_done, csq_done, ss4_done, r4_done, y_done, yg_done, eg_done, sig_done, sg_done, mix_done, o_free = map(
            s_, ("o_done", "cent_done", "csq_done", "ss4_done", "r4_done", "y_done", "yg_done", "eg_done", "sig_done", "sg_done",
                 "mix_done", "o_free"))
        CONSTS = 16 * 6
        block = st.enter_context(nc.Block())

        @block.sync
        def _(sp):
            def load(t):
                sp.wait_ge(ssx_done, t - 1)
                sp.wait_ge(xt_done, t - 1)
                sp.dma_start(xb[:, t % 2, :], d["x"][t * P:(t + 1) * P, :]).then_inc(x_in[t % 2], 16)

            for dst, src in ((tri, d["tri"]), (dec, d["decay"]), (g128, d["decay_tile"])):
                sp.dma_start(dst[:], src).then_inc(const_in, 16)
            sp.dma_start(gng[:], d["ret_gn_g"].partition_broadcast(P)).then_inc(const_in, 16)
            for half in range(2):
                sp.dma_start(gqc[64 * half:64 * half + 64, :], d["qn_c"].rearrange("(p a) -> p a", a=1)).then_inc(const_in, 16)

            W.load(sp, range(AHEAD + W.slots, KD))
            load(2)
            load(3)
            for t in range(NT):
                sp.dma_start(w_out_row(raw, t), rows(d["w_out"], KD)[:, t, :]).then_inc(w_out_in, 16)
                if t + 4 < NT:
                    load(t + 4)
                sp.wait_ge(mix_done, 2 * t + 2)
                sp.dma_start(d["mix"][t * P:(t + 1) * P, AW:D], mixt[:]).then_inc(mix_out, 16)
            sp.wait_ge(w_out_in, 16 * KD)
            sp.wait_ge(mix_out, 16 * NT)

        @block.gpsimd
        def _(pool):
            own = Steps(pool, pool_own)
            own(pool.memset(mhalf[:], -0.5))
            pool.wait_ge(const_in, CONSTS)

            def scale_x(t):
                pool.wait_ge(ssx_done, t + 1)
                own(pool.tensor_scalar(msx[:], ssx[:], 1.0 / D, EPS, ALU.mult, ALU.add))
                if t:
                    pj.wait_hi(pool, t - 1, QC)
                pool.tensor_tensor(rx[:], msx[:], mhalf[:, 0:1], ALU.pow).then_inc(rx_done, 1)

            def quarters(ap):
                return ap.rearrange("p (h e) -> p h e", e=HD // 2)

            def rotate(t):
                pj.wait_hi(pool, t, QK)
                for out, table in ((byc, cos), (bys, sin)):
                    i = pool.tensor_tensor(quarters(out[:]), quarters(qk[:]), table[:, t:t + 1, :].to_broadcast([P, 4 * BH, HD // 2]), ALU.mult)
                i.then_inc(rotated, 1)

            def square_qc(t):
                pj.wait_hi(pool, t, QC)
                pool.tensor_tensor(sqc[:], qc[:], qc[:], ALU.mult).then_inc(sqc_done, 1)

            def scale_qc(t):
                pool.wait_ge(ssc_done, t + 1)
                own(pool.tensor_scalar(msc[:], ssc[:], 1.0 / HD, EPS, ALU.mult, ALU.add))
                pool.tensor_tensor(rc[:], msc[:], mhalf[:], ALU.pow).then_inc(rc_done, 1)

            def square_cent(t):
                pool.wait_ge(cent_done, t + 1)
                pool.tensor_tensor(csq[:], cent[:], cent[:], ALU.mult).then_inc(csq_done, 1)

            def scale_ret(t):
                pool.wait_ge(ss4_done, t + 1)
                own(pool.tensor_scalar(ms4[:], ss4[:], 1.0 / HD, EPS, ALU.mult, ALU.add))
                pool.tensor_tensor(r4[:], ms4[:], mhalf[:], ALU.pow).then_inc(r4_done, 1)

            def gain(t):
                pool.wait_ge(y_done, t + 1)
                pool.tensor_tensor(yg[:], y[:], gng[:], ALU.mult).then_inc(yg_done, 1)

            def gate(t):
                pool.wait_ge(sig_done, t + 1)
                pool.tensor_tensor(sg[:], g[:, t % 2, :], eg[:], ALU.mult).then_inc(sg_done, 1)

            scale_x(0)
            rotate(0)
            for t in range(NT):
                square_qc(t)
                if t:
                    square_cent(t - 1)
                scale_qc(t)
                if t:
                    scale_ret(t - 1)
                    gain(t - 1)
                if t == 0:
                    scale_x(1)
                if t + 1 < NT:
                    rotate(t + 1)
                gate(t)
                if t + 2 < NT:
                    scale_x(t + 2)
            square_cent(NT - 1)
            scale_ret(NT - 1)
            gain(NT - 1)

        @block.scalar
        def _(act):
            def sum_squares(t):
                act.wait_ge(x_in[t % 2], 16 * (t // 2 + 1))
                if t:
                    act.wait_ge(rx_done, t)
                act.activation(junk[:], xb[:, t % 2, :], ACT.Square, accum_out=ssx[:]).then_inc(ssx_done, 1)

            def turned(t):
                act.wait_ge(xt_done, t + 1)
                act.activation(xTh[:, t % 2, :], XT[:], ACT.Copy).then_inc(xt_hi, 1)

            def take(t, f):
                pj.wait_full(act, t, f)
                if f == QK:
                    act.wait_ge(rx_done, t + 1)
                    i = act.activation(qk[:], PJ[:], ACT.Copy, scale=rx[:])
                elif f == VG:
                    if t >= 2:
                        act.wait_ge(sg_done, t - 1)
                    act.activation(v[:, t % 2, :], PJ[:, 0:BW], ACT.Copy, scale=rx[:])
                    i = act.activation(g[:, t % 2, :], PJ[:, BW:2 * BW], ACT.Copy, scale=rx[:])
                else:
                    i = act.activation(qc[:], PJ[:, 0:CW], ACT.Copy, scale=rx[:])
                i.then_inc(pj.hi, 1)

            turned(0)
            for k in range(AHEAD, KD):
                W.split_hi(act, k)
            sum_squares(0)
            turned(1)
            for f in (QK, VG, QC):
                take(0, f)
            sum_squares(1)
            for t in range(NT):
                tr.wait_full(act, t, QKT)
                act.activation(qkT[:], tiles(TR[:]), ACT.Copy).then_inc(tr.hi, 1)
                if t:
                    act.wait_ge(sg_done, t)
                act.activation(eg[:], g[:, t % 2, :], ACT.Exp, scale=-1.0).then_inc(eg_done, 1)
                if t + 1 < NT:
                    take(t + 1, QK)
                act.wait_ge(max_done, t + 1)
                for h in range(CH):
                    act.activation(Pr[:, h, :], SC[:, place(h, N_MEM)], ACT.Exp, bias=nmax[:, h:h + 1],
                                   accum_out=rs[:, h:h + 1]).then_inc(exp_done, 1)
                if t + 1 < NT:
                    take(t + 1, VG)
                act.wait_ge(pt_done, t + 1)
                act.activation(PTs[:], PT[:], ACT.Copy).then_inc(ptc_done, 1)
                if t + 2 < NT:
                    turned(t + 2)
                if t + 1 < NT:
                    take(t + 1, QC)
                if t + 2 < NT:
                    sum_squares(t + 2)

        @block.tensor
        def _(pe):
            def turn_x(t):
                pe.wait_ge(x_in[t % 2], 16 * (t // 2 + 1))
                if t:
                    pe.wait_ge(xt_lo, t)
                xs = xb[:, t % 2, :].rearrange("p (m k) -> p k m", k=KD)
                for k in range(KD):
                    mm = pe.transpose(XT[:, k * P:(k + 1) * P], xs[:, k, :], ident[:])
                mm.then_inc(xt_done, 1)

            def project(t, f):
                pj.wait_before(pe, t, f, t == 0)
                pe.wait_ge(xt_lo, t + 1)
                at, n = f * 2 * BW, CW if f == QC else 2 * BW
                for k in range(KD):
                    if t == 0 and f == QK:
                        pe.wait_ge(W.lo, k + 1)
                    m = slice(k * P, (k + 1) * P)
                    mm = product(pe, PJ[:, 0:n], (xTh[:, t % 2, m], xTl[:, t % 2, m]),
                                 (W.h[:, k, at:at + n], W.l[:, k, at:at + n]), k == 0, k == KD - 1)
                mm.then_inc(pj.full, 1)

            def half(h):
                return slice(64 * (h % 2), 64 * (h % 2) + 64)

            turn_x(0)
            turn_x(1)
            for f in (QK, VG, QC):
                project(0, f)
            pe.wait_ge(state0, 1)
            for t in range(NT):
                tr.wait_before(pe, t, QKT, t == 0)
                pe.wait_ge(qkr_done, t + 1)
                for j in range(4):
                    mm = pe.transpose(TR[:, j * P:(j + 1) * P], qkr[:, j * P:(j + 1) * P], ident[:])
                mm.then_inc(tr.full, 1)
                if t + 1 < NT:
                    project(t + 1, QK)
                pe.wait_ge(qcn_done, t + 1)
                tr.wait_before(pe, t, QCT, False)
                for p in range(CH // 2):
                    mm = pe.transpose(TR[:, p * P:(p + 1) * P], qcn[:, p * P:(p + 1) * P], ident[:])
                mm.then_inc(tr.full, 1)
                if t:
                    pe.wait_ge(ptc_done, t)
                for h in range(BH):
                    p, r = h // 2, half(h)
                    mm = pe.matmul(SB[:, place(h, P)], qkT[r, 2 + p, :], qkT[r, p, :], start=True, stop=True)
                mm.then_inc(sb_done, 1)
                tr.wait_free(pe, t, QCT)
                pe.wait_ge(xt_lo, min(t + 2, NT))
                for h in range(CH):
                    p, r = h // 2, half(h)
                    mm = pe.matmul(SC[:, place(h, N_MEM)], qTC[r, p, :], kTC[r, p, :], start=True, stop=True)
                mm.then_inc(sc_done, 1)
                if t + 1 < NT:
                    project(t + 1, VG)
                pe.wait_ge(exp_done, CH * (t + 1))
                pe.wait_ge(sm_done, t + 1)
                for h in range(CH):
                    for b in range(MT):
                        j = h * MT + b
                        mm = pe.transpose(PT[:, j * P:(j + 1) * P], Pr[:, h, b * P:(b + 1) * P], ident[:])
                mm.then_inc(pt_done, 1)
                if t + 2 < NT:
                    turn_x(t + 2)
                if t:
                    pe.wait_ge(o_free, t)
                    pe.wait_ge(r_done, t)
                for h in range(BH):
                    p, r, cols = h // 2, half(h), slice(h * HD, (h + 1) * HD)
                    pe.matmul(O[:, place(h, HD)], Sm[:, h, :], v[:, t % 2, cols], start=True, stop=False, skip_group_check=True)
                    pe.matmul(O[:, place(h, HD)], qkT[r, p, :], R[r, p, :], start=False, stop=True, skip_group_check=True)
                tr.wait_before(pe, t, U, False)
                for p in range(BH // 2):
                    cols = slice(p * P, (p + 1) * P)
                    mm = pe.matmul(TR[:, cols], qkr[:, BW + p * P:BW + (p + 1) * P], v[:, t % 2, cols], start=True, stop=True)
                mm.then_inc(tr.full, 1)
                if t + 1 < NT:
                    project(t + 1, QC)
                pe.wait_ge(ptc_done, t + 1)
                for h in range(CH):
                    cols = slice(h * HD, (h + 1) * HD)
                    for b in range(MT):
                        j = slice((h * MT + b) * P, (h * MT + b + 1) * P)
                        mm = pe.matmul(O[:, place(h, HD, 2 * HD)], PTs[:, j], VC[:, b, cols], start=b == 0,
                                       stop=b == MT - 1, skip_group_check=True)
                mm.then_inc(o_done, 1)

        @block.vector
        def _(dve):
            own = Steps(dve, dve_own)

            def turned(t):
                dve.wait_ge(xt_hi, t + 1)
                dve.tensor_tensor(xTl[:, t % 2, :], XT[:], xTh[:, t % 2, :].bitcast(F32), ALU.subtract).then_inc(xt_lo, 1)

            turned(0)
            for k in range(AHEAD, KD):
                W.split_lo(dve, k)
            dve.wait_ge(const_in, CONSTS)
            own(dve.tensor_scalar(gqc8[:], gqc[:], HD ** -0.5, None, ALU.mult))
            dve.memset(R[:], 0.0).then_inc(state0, 1)
            dve.wait_ge(state0, 1)

            def rotate(t):
                dve.wait_ge(rotated, t + 1)
                sides = lambda ap: ap.rearrange("p (h s e) -> p h s e", s=2, e=HD // 2)
                dve.tensor_tensor(sides(rot[:])[:, :, 0, :], sides(byc[:])[:, :, 0, :], sides(bys[:])[:, :, 1, :], ALU.subtract)
                own(dve.tensor_tensor(sides(rot[:])[:, :, 1, :], sides(bys[:])[:, :, 0, :], sides(byc[:])[:, :, 1, :], ALU.add))
                dve.tensor_tensor(heads(qkr[:]), heads(rot[:]), wide(dec[:], HD), ALU.mult).then_inc(qkr_done, 1)

            def center(t):
                dve.wait_ge(o_done, t + 1)
                own(dve.tensor_reduce(halves1(sm4[:]), by_head(O[:], HD), AX.X, ALU.add))
                own(dve.tensor_scalar(mean[:], sm4[:], 1.0 / HD, None, ALU.mult))
                dve.tensor_tensor(halves(cent[:]), by_head(O[:], HD),
                                  halves1(mean[:]).unsqueeze(3).to_broadcast([P, 2, 2, HD]), ALU.subtract).then_inc(cent_done, 1)
                own(dve.reciprocal(rinv[:], rs[:]))
                if t:
                    dve.wait_ge(mix_out, 16 * t)
                dve.tensor_tensor(halves(mixt[:, BW:BW + CW]), by_head(O[:], HD, 2 * HD),
                                  halves1(rinv[:]).unsqueeze(3).to_broadcast([P, 2, 2, HD]), ALU.mult).then_inc(mix_done, 1)
                dve.wait_ge(mix_done, 2 * t + 1)
                dve.sem_inc(o_free, 1)

            def cent_sums(t):
                dve.wait_ge(csq_done, t + 1)
                dve.tensor_reduce(ss4[:], heads(csq[:]), AX.X, ALU.add).then_inc(ss4_done, 1)

            def norm(t):
                dve.wait_ge(r4_done, t + 1)
                dve.tensor_tensor(heads(y[:]), heads(cent[:]), wide(r4[:], HD), ALU.mult).then_inc(y_done, 1)

            def finish(t):
                dve.wait_ge(yg_done, t + 1)
                dve.wait_ge(sg_done, t + 1)
                dve.tensor_tensor(mixt[:, 0:BW], yg[:], sg[:], ALU.mult).then_inc(mix_done, 1)

            turned(1)
            rotate(0)
            for t in range(NT):
                if t:
                    center(t - 1)
                dve.wait_ge(sqc_done, t + 1)
                dve.tensor_reduce(ssc[:], heads(sqc[:]), AX.X, ALU.add).then_inc(ssc_done, 1)
                if t:
                    cent_sums(t - 1)
                dve.wait_ge(rc_done, t + 1)
                dve.tensor_tensor(heads(qcn[:]), heads(qc[:]), wide(rc[:], HD), ALU.mult).then_inc(qcn_done, 1)
                if t:
                    norm(t - 1)
                    finish(t - 1)
                tr.wait_full(dve, t, QCT)
                dve.tensor_scalar(qTC[:], tiles(TR[:, 0:CW]), gqc8[:], None, ALU.mult).then_inc(tr.lo, 1)
                dve.wait_ge(sb_done, t + 1)
                for s in range(2):
                    i = dve.tensor_tensor(Sm[:].rearrange("p (a s) n -> p s a n", s=2)[:, s], by_head(SB[:], P)[:, s],
                                          tri[:].unsqueeze(1).to_broadcast([P, 2, P]), ALU.mult)
                i.then_inc(sm_done, 1)
                dve.wait_ge(sc_done, t + 1)
                dve.tensor_reduce(halves1(nmax[:]), by_head(SC[:], N_MEM), AX.X, ALU.max,
                                  negate=True).then_inc(max_done, 1)
                dve.wait_ge(eg_done, t + 1)
                own(dve.tensor_scalar(eg[:], eg[:], 1.0, None, ALU.add))
                dve.reciprocal(eg[:], eg[:]).then_inc(sig_done, 1)
                if t + 2 < NT:
                    turned(t + 2)
                tr.wait_full(dve, t, U)
                u = TR[:, 0:BW].rearrange("p (a b e) -> p a b e", b=2, e=HD)
                dve.tensor_tensor(Rt[0:64], R[0:64], u[0:64, :, 0, :], ALU.add)
                own(dve.tensor_tensor(Rt[64:128], R[64:128], u[64:128, :, 1, :], ALU.add))
                own(dve.tensor_tensor(R[:], Rt[:], wide(g128[:], HD), ALU.mult))
                dve.sem_inc(tr.lo, 1)
                dve.sem_inc(r_done, 1)
                if t + 1 < NT:
                    rotate(t + 1)
            center(NT - 1)
            cent_sums(NT - 1)
            norm(NT - 1)
            finish(NT - 1)


def phase_o(c, d, counts, routed, X):
    nc = c.nc
    with ExitStack() as st:
        Wh = sbuf(nc, st, "o_wh", [P, KD, D], F32R)
        Wl = sbuf(nc, st, "o_wl", [P, KD, D], F32R)
        t_ = lambda name, shape, dt=F32: sbuf(nc, st, "o_" + name, shape, dt)
        wr = t_("wr", [P, KD, NLG])
        B = 2
        mx, xb, h, hn = t_("m", [P, B, D]), t_("x", [P, B, D]), t_("h", [P, B, D]), t_("hn", [P, B, D])
        mTh, mTl = t_("mth", [P, B, KD * P], F32R), t_("mtl", [P, B, KD * P], F32R)
        nT = t_("nt", [P, KD * P])
        junk = t_("junk", [P, D], BF16)
        ident = t_("ident", [P, P])
        gf, br = t_("gf", [P, D]), t_("br", [P, NLG])
        mhalf, ss, ms, r = t_("mhalf", [P, 1]), t_("ss", [P, NT]), t_("ms", [P, NT]), t_("r", [P, NT])
        Y, XT, HT, LG, RK = *c.bank2, *c.bank
        lg, tab = t_("lg", [P, NT, NLG]), t_("tab", [P, 2 * NE + LEVELS - 1 + FULL])
        GOF, EOF, BND = tab[:, 0:NE], tab[:, NE:2 * NE], tab[:, 2 * NE:2 * NE + LEVELS - 1]
        tok, ones, before = t_("tok", [P, NT], I32), t_("ones", [P, P]), t_("before", [P, P])
        g8, gtop, gix = t_("g8", [P, NT, 8]), t_("gtop", [P, NT, 8]), t_("gix", [P, NT, 8], U32)
        grp, gsum, pg = t_("grp", [P, NT]), t_("gsum", [P, NT]), t_("pg", [P, NT])
        ge, gex = t_("ge", [P, NT, NG]), t_("gex", [P, NT, NG])
        mask, pen, em = t_("mask", [P, NE]), t_("pen", [P, NE]), t_("em", [P, NE])
        top, ix, ixf = t_("top", [P, NT, 8]), t_("ix", [P, NT, 8], U32), t_("ixf", [P, NT, 2])
        dv, ev, share = t_("dv", [P, NT]), t_("ev", [P, NT]), t_("share", [P, NT])
        A12, A, Asum = t_("a12", [P, 2, 2, NE]), t_("a", [P, NT, NE]), t_("asum", [P, NT, NE])
        pick, rj, over, lv, row = t_("pick", [P, 2, NE]), t_("rj", [P, 2]), t_("over", [P, 2, LEVELS - 1]), t_("lv", [P, 2]), t_("row", [P, 2])
        dest, pair = t_("dest", [P, NT, 2], U32), t_("pair", [P, NT, 2, 2], I32)
        blank = t_("blank", [P, PLACES, 2], I32)
        s_ = lambda name: c.sem("o_" + name)
        const_in, wr_in, pool_set, ident_in = map(s_, ("const_in", "wr_in", "pool_set", "ident_in"))
        m_in, x_in, h_out, hn_out = ([s_(f"{n}{b}") for b in range(B)] for n in ("m_in", "x_in", "h_out", "hn_out"))
        xt_done, xt_hi, xt_lo, ht_done, nt_done = map(s_, ("xt_done", "xt_hi", "xt_lo", "ht_done", "nt_done"))
        y_done, h_done = s_("y_done"), s_("h_done")
        w_hi, w_lo = s_("w_hi"), s_("w_lo")
        own_s, tab_in, ge_in, ge_out, ev_in, ev_out, a_done, rank_done, rank_used, dest_done, blank_set, blank_out = map(
            s_, ("own", "tab_in", "ge_in", "ge_out", "ev_in", "ev_out", "a_done", "rank_done", "rank_used", "dest_done",
                 "blank_set", "blank_out"))
        ss_done, ms_done, r_done, hn_done, lg_full, lg_done = map(s_, ("ss_done", "ms_done", "r_done", "hn_done", "lg_full", "lg_done"))
        CONSTS = 16 * 3
        block = st.enter_context(nc.Block())

        def loads(t):
            return 16 * (t // B + 1)

        @block.sync
        def _(sp):
            def load_m(t):
                if t >= B:
                    sp.wait_ge(xt_done, t - B + 1)
                sp.dma_start(mx[:, t % B, :], d["mix"][t * P:(t + 1) * P, :]).then_inc(m_in[t % B], 16)

            def load_x(t):
                if t >= B:
                    sp.wait_ge(h_done, 2 * (t - B + 1))
                sp.dma_start(xb[:, t % B, :], d["x"][t * P:(t + 1) * P, :]).then_inc(x_in[t % B], 16)

            load_m(0)
            sp.dma_start(ident[:], d["ident"]).then_inc(ident_in, 16)
            sp.dma_start(wr[:, :, 0:NG], rows(d["w_router_group"], KD)).then_inc(wr_in, 16)
            sp.dma_start(wr[:, :, NG:NLG], rows(d["w_router_expert"], KD)).then_inc(wr_in, 16)
            load_m(1)
            sp.dma_start(gf[:], d["ffn_norm_g"].partition_broadcast(P)).then_inc(const_in, 16)
            sp.dma_start(br[:, 0:NG], d["b_router_group"].partition_broadcast(P)).then_inc(const_in, 16)
            sp.dma_start(br[:, NG:NLG], d["b_router_expert"].partition_broadcast(P)).then_inc(const_in, 16)
            load_x(0)
            load_x(1)
            sp.dma_start(tab[:], d["route_tab"].partition_broadcast(P)).then_inc(tab_in, 16)
            sp.dma_start(before[:], d["before"]).then_inc(tab_in, 16)
            sp.dma_start(tok[:], d["token"]).then_inc(tab_in, 16)
            sp.wait_ge(blank_set, 2)
            sp.dma_start(d["row"].rearrange("(p v) a -> p v a", p=P), blank[:]).then_inc(blank_out, 16)
            for t in range(NT):
                if t + B < NT:
                    load_m(t + B)
                if t == 1:
                    sp.wait_ge(w_lo, KD)
                    for j in X.CHUNKS:
                        X.load(sp, 0, j)
                sp.wait_ge(h_done, 2 * (t + 1))
                sp.dma_start(d["out"][t * P:(t + 1) * P, :], h[:, t % B, :]).then_inc(h_out[t % B], 16)
                if t + B < NT:
                    load_x(t + B)
                sp.wait_ge(hn_done, t + 1)
                sp.dma_start(d["hn"][t * P:(t + 1) * P, :], hn[:, t % B, :]).then_inc(hn_out[t % B], 16)
            for b in range(B):
                sp.wait_ge(h_out[b], 16 * (NT // B))
                sp.wait_ge(hn_out[b], 16 * (NT // B))

        @block.gpsimd
        def _(pool):
            pool.memset(mhalf[:], -0.5).then_inc(pool_set, 1)
            pool.wait_ge(pool_set, 1)
            pool.memset(blank[:, :, 0:1], SKIP).then_inc(blank_set, 1)
            pool.memset(blank[:, :, 1:2], 0).then_inc(blank_set, 1)

            def scatter(t):
                pool.wait_ge(dest_done, t + 1)
                for j in range(2):
                    pool.indirect_dma_start(out=d["row"], out_offset=bass.IndirectOffsetOnAxis(ap=dest[:, t, j:j + 1], axis=0),
                                            in_=pair[:, t, j, :], in_offset=None).then_inc(routed, 16)

            for t in range(NT):
                pool.wait_ge(ss_done, t + 1)
                pool.tensor_scalar(ms[:, t:t + 1], ss[:, t:t + 1], 1.0 / D, EPS, ALU.mult, ALU.add).then_inc(ms_done, 1)
                pool.wait_ge(ms_done, t + 1)
                pool.tensor_tensor(r[:, t:t + 1], ms[:, t:t + 1], mhalf[:], ALU.pow).then_inc(r_done, 1)
                if t == 0:
                    pool.wait_ge(blank_out, 16)
                if t >= 3:
                    scatter(t - 3)
            for t in range(NT - 3, NT):
                scatter(t)
            pool.wait_ge(routed, 16 * 2 * NT)

        @block.scalar
        def _(act):
            def mixed(t):
                act.wait_ge(xt_done, t + 1)
                if t >= B:
                    act.wait_ge(y_done, 2 * (t - B + 1))
                act.activation(mTh[:, t % B, :], XT[:], ACT.Copy).then_inc(xt_hi, 1)

            def exps(t):
                act.wait_ge(ge_in, t + 1)
                act.activation(gex[:, t, :], ge[:, t, :], ACT.Exp, accum_out=gsum[:, t:t + 1]).then_inc(ge_out, 1)
                act.wait_ge(ev_in, t + 1)
                act.activation(ev[:, t:t + 1], dv[:, t:t + 1], ACT.Exp).then_inc(ev_out, 1)

            def split(k):
                act.activation(Wh[:, k, :], w_out_row(X.raw, k), ACT.Copy).then_inc(w_hi, 1)

            split(0)
            split(1)
            mixed(0)
            for k in range(2, KD):
                split(k)
            mixed(1)
            for t in range(NT):
                act.wait_ge(h_done, 2 * (t + 1))
                if t:
                    act.wait_ge(ss_done, t)
                act.activation(junk[:], h[:, t % B, :], ACT.Square, accum_out=ss[:, t:t + 1]).then_inc(ss_done, 1)
                if t + B < NT:
                    mixed(t + B)
                act.wait_ge(ht_done, t + 1)
                if t:
                    act.wait_ge(lg_full, t)
                act.activation(nT[:], HT[:], ACT.Copy).then_inc(nt_done, 1)
                if t:
                    exps(t - 1)
            exps(NT - 1)

        @block.tensor
        def _(pe):
            def turn(out, src, done):
                xs = src.rearrange("p (m k) -> p k m", k=KD)
                for k in range(KD):
                    mm = pe.transpose(out[:, k * P:(k + 1) * P], xs[:, k, :], ident[:])
                mm.then_inc(done, 1)

            def turn_mixed(t):
                pe.wait_ge(m_in[t % B], loads(t))
                if t:
                    pe.wait_ge(xt_lo, t)
                turn(XT, mx[:, t % B, :], xt_done)

            def w_out(t, half):
                if half == 0:
                    pe.wait_ge(xt_lo, t + 1)
                if t:
                    pe.wait_ge(h_done, 2 * (t - 1) + half + 1)
                cols = slice(512 * half, 512 * half + 512)
                for k in range(KD):
                    if t == 0 and half == 0:
                        pe.wait_ge(w_lo, k + 1)
                    m = slice(k * P, (k + 1) * P)
                    mm = product(pe, Y[:, cols], (mTh[:, t % B, m], mTl[:, t % B, m]), (Wh[:, k, cols], Wl[:, k, cols]),
                                 k == 0, k == KD - 1)
                mm.then_inc(y_done, 1)

            def turn_normed(t):
                pe.wait_ge(hn_done, t + 1)
                if t:
                    pe.wait_ge(nt_done, t)
                turn(HT, hn[:, t % B, :], ht_done)

            def logits(t):
                pe.wait_ge(nt_done, t + 1)
                if t:
                    pe.wait_ge(lg_done, t)
                for k in range(KD):
                    m = slice(k * P, (k + 1) * P)
                    mm = pe.matmul(LG[:, 0:NLG], nT[:, m], wr[:, k, :], start=k == 0, stop=k == KD - 1)
                mm.then_inc(lg_full, 1)

            def ranks(t):
                pe.wait_ge(a_done, t + 1)
                if t:
                    pe.wait_ge(rank_used, t)
                pe.matmul(RK[:, 0:NE], before[:], A[:, t, :], start=True, stop=False, skip_group_check=True)
                mm = pe.matmul(RK[:, 0:NE], ones[:], Asum[:, t, :], start=False, stop=True, skip_group_check=True)
                if t == NT - 1:
                    pe.matmul(RK[:, NE:2 * NE], ones[:], A[:, t, :], start=True, stop=False, skip_group_check=True)
                    mm = pe.matmul(RK[:, NE:2 * NE], ones[:], Asum[:, t, :], start=False, stop=True, skip_group_check=True)
                mm.then_inc(rank_done, 1)

            pe.wait_ge(ident_in, 16)
            turn_mixed(0)
            w_out(0, 0)
            turn_mixed(1)
            w_out(0, 1)
            pe.wait_ge(wr_in, 32)
            for t in range(NT):
                if t + 2 < NT:
                    turn_mixed(t + 2)
                if t + 1 < NT:
                    w_out(t + 1, 0)
                if t >= 2:
                    ranks(t - 2)
                if t:
                    logits(t - 1)
                if t + 1 < NT:
                    w_out(t + 1, 1)
                turn_normed(t)
            logits(NT - 1)
            ranks(NT - 2)
            ranks(NT - 1)

        @block.vector
        def _(dve):
            def mixed(t):
                dve.wait_ge(xt_hi, t + 1)
                dve.tensor_tensor(mTl[:, t % B, :], XT[:], mTh[:, t % B, :].bitcast(F32), ALU.subtract).then_inc(xt_lo, 1)

            def residual(t, half):
                dve.wait_ge(y_done, 2 * t + half + 1)
                if half == 0:
                    dve.wait_ge(x_in[t % B], loads(t))
                    if t >= B:
                        dve.wait_ge(h_out[t % B], loads(t - B))
                        dve.wait_ge(hn_done, t - B + 1)
                cols = slice(512 * half, 512 * half + 512)
                dve.tensor_tensor(h[:, t % B, cols], Y[:, cols], xb[:, t % B, cols], ALU.add).then_inc(h_done, 1)

            def split(k):
                dve.wait_ge(w_hi, k + 1)
                dve.tensor_tensor(Wl[:, k, :], w_out_row(X.raw, k), Wh[:, k, :].bitcast(F32), ALU.subtract).then_inc(w_lo, 1)

            split(0)
            split(1)
            mixed(0)
            for k in range(2, KD):
                split(k)
            mixed(1)
            residual(0, 0)
            dve.wait_ge(const_in, CONSTS)
            own = Steps(dve, own_s)
            own(dve.memset(g8[:], NEG))
            own(dve.memset(ones[:], 1.0))
            own(dve.memset(Asum[:, 0, :], 0.0))
            dve.wait_ge(tab_in, 48)
            own(dve.tensor_copy(pair[:, :, :, 0], tok[:].unsqueeze(2).to_broadcast([P, NT, 2])))

            def logit(t):
                dve.wait_ge(lg_full, t + 1)
                dve.tensor_tensor(lg[:, t, :], LG[:, 0:NLG], br[:], ALU.add).then_inc(lg_done, 1)
                dve.wait_ge(lg_done, t + 1)

            def select(t):
                one = slice(t, t + 1)
                own(dve.tensor_copy(g8[:, t, 0:NG], lg[:, t, 0:NG]))
                own(dve.max(gtop[:, t, :], g8[:, t, :]))
                own(dve.max_index(gix[:, t, :], gtop[:, t, :], g8[:, t, :]))
                dve.tensor_tensor(ge[:, t, :], lg[:, t, 0:NG], gtop[:, t, 0:1].to_broadcast([P, NG]), ALU.subtract).then_inc(ge_in, 1)
                own(dve.tensor_copy(grp[:, one], gix[:, t, 0:1]))
                own(dve.tensor_scalar(mask[:], GOF, grp[:, one], None, ALU.is_equal))
                own(dve.tensor_scalar(pen[:], mask[:], -NEG, NEG, ALU.mult, ALU.add))
                own(dve.tensor_tensor(em[:], lg[:, t, NG:NLG], mask[:], ALU.mult))
                own(dve.tensor_tensor(em[:], em[:], pen[:], ALU.add))
                own(dve.max(top[:, t, :], em[:]))
                own(dve.max_index(ix[:, t, :], top[:, t, :], em[:]))
                dve.tensor_tensor(dv[:, one], top[:, t, 1:2], top[:, t, 0:1], ALU.subtract).then_inc(ev_in, 1)
                own(dve.tensor_copy(ixf[:, t, :], ix[:, t, 0:2]))
                own(dve.tensor_tensor(A12[:, t % 2], EOF.unsqueeze(1).to_broadcast([P, 2, NE]), wide(ixf[:, t, :], NE), ALU.is_equal))
                dve.tensor_tensor(A[:, t, :], A12[:, t % 2, 0, :], A12[:, t % 2, 1, :], ALU.add).then_inc(a_done, 1)
                if t + 1 < NT:
                    dve.wait_ge(a_done, t + 1)
                    own(dve.tensor_tensor(Asum[:, t + 1, :], Asum[:, t, :], A[:, t, :], ALU.add))

            def place(t):
                one = slice(t, t + 1)
                dve.wait_ge(rank_done, t + 1)
                own(dve.tensor_tensor(pick[:], A12[:, t % 2], RK[:, 0:NE].unsqueeze(1).to_broadcast([P, 2, NE]), ALU.mult))
                dve.sem_inc(rank_used, 1)
                own(dve.tensor_reduce(rj[:], pick[:], AX.X, ALU.add))
                own(dve.tensor_tensor(over[:], wide(rj[:], LEVELS - 1), BND.unsqueeze(1).to_broadcast([P, 2, LEVELS - 1]), ALU.is_ge))
                own(dve.tensor_reduce(lv[:], over[:], AX.X, ALU.add))
                own(dve.scalar_tensor_tensor(row[:], rj[:], float(PLACES), ixf[:, t, :], ALU.mult, ALU.add))
                own(dve.scalar_tensor_tensor(row[:], lv[:], float(NE - CAP * PLACES), row[:], ALU.mult, ALU.add))
                own(dve.tensor_copy(dest[:, t, :], row[:]))
                dve.wait_ge(ge_out, t + 1)
                own(dve.reciprocal(pg[:, one], gsum[:, one]))
                dve.wait_ge(ev_out, t + 1)
                own(dve.tensor_scalar(share[:, one], ev[:, one], 1.0, None, ALU.add))
                own(dve.reciprocal(share[:, one], share[:, one]))
                own(dve.tensor_tensor(pair[:, t, 0, 1:2].bitcast(F32), pg[:, one], share[:, one], ALU.mult))
                own(dve.tensor_tensor(pair[:, t, 1, 1:2].bitcast(F32), pair[:, t, 0, 1:2].bitcast(F32), ev[:, one], ALU.mult))
                dve.sem_inc(dest_done, 1)

            for t in range(NT):
                residual(t, 1)
                if t + B < NT:
                    mixed(t + B)
                dve.wait_ge(r_done, t + 1)
                if t >= B:
                    dve.wait_ge(hn_out[t % B], loads(t - B))
                    dve.wait_ge(ht_done, t - B + 1)
                dve.scalar_tensor_tensor(hn[:, t % B, :], h[:, t % B, :], r[:, t:t + 1], gf[:], ALU.mult, ALU.mult).then_inc(hn_done, 1)
                if t + 1 < NT:
                    residual(t + 1, 0)
                if t:
                    logit(t - 1)
                if t >= 2:
                    place(t - 2)
                if t:
                    select(t - 1)
            logit(NT - 1)
            select(NT - 1)
            place(NT - 2)
            place(NT - 1)
            own(dve.tensor_copy(counts[:], RK[:, NE:2 * NE]))


def phase_r(c, d, counts, routed, btab, ptab, ids, X):
    nc = c.nc
    with ExitStack() as st:
        t_ = lambda name, shape, dt=F32: sbuf(nc, st, "r_" + name, shape, dt)
        tab = t_("tab", [P, 2 * NE + LEVELS - 1 + FULL])
        EOF, BND, LATER = tab[:, NE:2 * NE], tab[:, 2 * NE:2 * NE + LEVELS - 1], tab[:, 2 * NE + LEVELS - 1:]
        over, extra, upto, one = t_("over", [P, NE, LEVELS - 1]), t_("extra", [P, NE]), t_("upto", [P, NE]), t_("one", [P, NE])
        past, past_n = t_("past", [P, FULL, NE]), t_("past_n", [P, FULL, NE])
        expert, prior, level, place = t_("expert", [P, FULL]), t_("prior", [P, FULL]), t_("level", [P, FULL]), t_("place", [P, FULL])
        number = t_("number", [P, 1])
        tab_in, own_s, ids_in = c.sem("r_tab_in"), c.sem("r_own"), c.sem("r_ids_in")
        block = st.enter_context(nc.Block())
        BY_POOL = (X.GU[0], X.GU[2])

        @block.sync
        def _(sp):
            sp.dma_start(tab[:], d["route_tab"].partition_broadcast(P)).then_inc(tab_in, 16)
            sp.wait_ge(routed, 16 * 2 * NT)
            sp.dma_start(ids[:], d["row"].rearrange("(p v) a -> p v a", p=P)).then_inc(ids_in, 16)
            for j in X.GU:
                X.load_next(sp, 1, 1, j)
            sp.wait_ge(ids_in, 16)

        @block.gpsimd
        def _(pool):
            for j in BY_POOL:
                X.split_lo(pool, 0, j)

        @block.scalar
        def _(act):
            for j in X.GU:
                X.split_hi(act, 0, j)

        @block.vector
        def _(dve):
            own = Steps(dve, own_s)
            own(dve.memset(one[:], 1.0))
            dve.wait_ge(tab_in, 16)
            own(dve.tensor_tensor(over[:], wide(counts[:], LEVELS - 1), BND.unsqueeze(1).to_broadcast([P, NE, LEVELS - 1]), ALU.is_gt))
            own(dve.tensor_reduce(extra[:], over[:], AX.X, ALU.add))
            own(dve.tensor_tensor_scan(upto[:], one[:], extra[:], 0.0, ALU.mult, ALU.add))
            own(dve.tensor_tensor(past[:], upto[:].unsqueeze(1).to_broadcast([P, FULL, NE]), wide(LATER, NE), ALU.is_le))
            own(dve.tensor_tensor(past_n[:], past[:], extra[:].unsqueeze(1).to_broadcast([P, FULL, NE]), ALU.mult))
            own(dve.tensor_reduce(expert[:], past[:], AX.X, ALU.add))
            own(dve.tensor_reduce(prior[:], past_n[:], AX.X, ALU.add))
            own(dve.tensor_scalar(expert[:], expert[:], NE - 1.0, None, ALU.min))
            own(dve.tensor_tensor(level[:], LATER, prior[:], ALU.subtract))
            own(dve.tensor_scalar(level[:], level[:], 1.0, LEVELS - 1.0, ALU.add, ALU.min))
            own(dve.scalar_tensor_tensor(place[:], level[:], float(NE), expert[:], ALU.mult, ALU.add))
            own(dve.tensor_scalar(number[:], upto[:, NE - 1:NE], NE - 3.0, None, ALU.add))
            own(dve.tensor_copy(btab[:, 0:NE], EOF))
            own(dve.tensor_copy(btab[:, NE:BLOCKS], expert[:]))
            own(dve.tensor_copy(btab[:, BLOCKS:], number[:]))
            own(dve.tensor_copy(ptab[:, 0:NE], EOF))
            own(dve.tensor_copy(ptab[:, NE:], place[:]))
            for j in X.GU:
                if j not in BY_POOL:
                    X.split_lo(dve, 0, j)


class Experts:

    GATE, UP, DOWN = range(3)
    GU, DN = range(KD // 2), range(KD // 2, KD // 2 + KF // 2)
    CHUNKS = [*GU, *DN]

    def __init__(self, c, d, raw):
        self.d, self.raw = d, raw
        self.loaded, self.hi, self.lo, self.used = ([c.sem(f"x_{n}{j}") for j in self.CHUNKS]
                                                    for n in ("loaded", "hi", "lo", "used"))
        self.h = self.l = None

    def place_parts(self, h, l):
        self.h, self.l = h, l

    def part(self, buf, j):
        if j in self.GU:
            return buf[:, 0:2, 2 * j * DE:2 * (j + 1) * DE]
        return buf[:, self.DOWN, 2 * (j - self.DN[0]) * D:2 * (j - self.DN[0] + 1) * D]

    def load(self, sp, e, j):
        if j in self.GU:
            for m, w in ((self.GATE, self.d["w_gate"]), (self.UP, self.d["w_up"])):
                src = w.rearrange("e (p k) n -> e p (k n)", p=P)[bass.ds(e, 1), :, 2 * j * DE:2 * (j + 1) * DE]
                sp.dma_start(self.raw[:, m, 2 * j * DE:2 * (j + 1) * DE], src.rearrange("a p n -> p (a n)")).then_inc(self.loaded[j], 16)
        else:
            k = j - self.DN[0]
            src = self.d["w_down"].rearrange("e (p k) n -> e p (k n)", p=P)[bass.ds(e, 1), :, 2 * k * D:2 * (k + 1) * D]
            sp.dma_start(self.part(self.raw, j), src.rearrange("a p n -> p (a n)")).then_inc(self.loaded[j], 16)

    def load_next(self, sp, i, e, j, passed=None):
        if passed is None:
            sp.wait_ge(self.lo[j], i)
        else:
            wait_apart(sp, self.lo[j], i, passed)
        self.load(sp, e, j)

    def split_hi(self, act, i, j):
        act.wait_ge(self.loaded[j], (32 if j in self.GU else 16) * (i + 1))
        if not is_first(i):
            act.wait_ge(self.used[j], i)
        act.activation(self.part(self.h, j), self.part(self.raw, j), ACT.Copy).then_inc(self.hi[j], 1)

    def split_lo(self, eng, i, j):
        eng.wait_ge(self.hi[j], i + 1)
        eng.tensor_tensor(self.part(self.l, j), self.part(self.raw, j), self.part(self.h, j).bitcast(F32),
                          ALU.subtract).then_inc(self.lo[j], 1)


def is_first(i):
    return isinstance(i, int) and i == 0


def phase_e(c, d, btab, ptab, ids, X):
    nc = c.nc
    with ExitStack() as st:
        t_ = lambda name, shape, dt=F32: sbuf(nc, st, "e_" + name, shape, dt)
        Wh, Wl, lo, used, GU, DN, GATE, UP, DOWN = X.h, X.l, X.lo, X.used, X.GU, X.DN, X.GATE, X.UP, X.DOWN
        ident = t_("ident", [P, P])
        ix, ix_y, w_y = t_("ix", [P, 1], U32), t_("ix_y", [P, 1], U32), t_("w_y", [P, 1])
        xg = t_("xg", [P, D])
        xTh, xTl = t_("xth", [P, KD, P], F32R), t_("xtl", [P, KD, P], F32R)
        sg, hs = t_("sg", [P, DE]), t_("hs", [P, DE])
        hTh, hTl = t_("hth", [P, KF, P], F32R), t_("htl", [P, KF, P], F32R)
        y = t_("y", [P, D])
        XT, Y = c.bank2[0], c.bank2[1]
        G, U = c.bank2[2][:, 0:512], c.bank2[2][:, 512:1024]
        HT = c.bank[0]
        s_ = lambda name: c.sem("e_" + name)
        const_in, ix_set, w_set, xg_set, xg_in, y_out, sp_passed, pool_passed = map(
            s_, ("const_in", "ix_set", "w_set", "xg_set", "xg_in", "y_out", "sp_passed", "pool_passed"))
        xt_done, xt_hi, xt_lo, ht_done, ht_hi, ht_lo = map(s_, ("xt_done", "xt_hi", "xt_lo", "ht_done", "ht_hi", "ht_lo"))
        sg_done, hs_done, y_done = map(s_, ("sg_done", "hs_done", "y_done"))
        BY_POOL = (GU[1],)
        block = st.enter_context(nc.Block())
        def turns(eng, body, after=1):
            n = eng.value_load(btab[0:1, BLOCKS:BLOCKS + 1], min_val=NE - 3, max_val=BLOCKS - 4)
            body(0, None, after)
            body(1, 0, after)
            with eng.Fori(1, n + (2 - after)) as p:
                body(p + 1, p, after)
            for more in reversed(range(after)):
                body(n + (3 - more) - 1, n + (3 - more) - 2, more)
            return n + 2

        @block.sync
        def _(sp):
            sp.dma_start(ident[:], d["ident"]).then_inc(const_in, 16)

            def expert(i):
                return i if isinstance(i, int) else sp.value_load(btab[0:1, bass.ds(i, 1)], min_val=0, max_val=NE - 1)

            def load_next(i, chunks):
                e = expert(i)
                for j in chunks:
                    X.load_next(sp, i, e, j, sp_passed)

            def turn(i, p, more):
                if p is not None:
                    load_next(i, DN)
                if more == 2:
                    load_next(i + 2, GU)

            turns(sp, turn, 2)

        @block.gpsimd
        def _(pool):
            pool.memset(xg[:], 0.0).then_inc(xg_set, 1)
            pool.wait_ge(xg_set, 1)

            def place(i):
                return i if isinstance(i, int) else pool.value_load(ptab[0:1, bass.ds(i, 1)], min_val=0, max_val=PLACES - 1)

            def gather(i):
                if not is_first(i):
                    wait_apart(pool, xt_done, i, pool_passed)
                pool.tensor_copy(ix[:], ids[:, bass.ds(place(i), 1), 0]).then_inc(ix_set, 1)
                wait_apart(pool, ix_set, i + 1, pool_passed)
                pool.indirect_dma_start(out=xg[:], out_offset=None, in_=d["hn"],
                                        in_offset=bass.IndirectOffsetOnAxis(ap=ix[:], axis=0),
                                        bounds_check=SEQ - 1, oob_is_err=False).then_inc(xg_in, 16)

            def row_weights(i):
                if not is_first(i):
                    wait_apart(pool, y_out, 16 * i, pool_passed)
                at = place(i)
                pool.tensor_copy(ix_y[:], ids[:, bass.ds(at, 1), 0])
                pool.tensor_copy(w_y[:], ids[:, bass.ds(at, 1), 1].bitcast(F32)).then_inc(w_set, 1)

            def add_out(i):
                wait_apart(pool, y_done, i + 1, pool_passed)
                pool.indirect_dma_start(out=d["out"], out_offset=bass.IndirectOffsetOnAxis(ap=ix_y[:], axis=0),
                                        in_=y[:], in_offset=None, bounds_check=SEQ - 1, oob_is_err=False,
                                        compute_op=ALU.add).then_inc(y_out, 16)

            def turn(i, p, more):
                if more:
                    gather(i + 1)
                if p is not None:
                    row_weights(p)
                if more:
                    for j in BY_POOL:
                        X.split_lo(pool, i + 1, j)
                if p is not None:
                    add_out(p)

            gather(0)
            last = turns(pool, turn)
            row_weights(last)
            add_out(last)
            wait_apart(pool, y_out, 16 * (last + 1), pool_passed)

        @block.scalar
        def _(act):
            def split(i, j):
                X.split_hi(act, i, j)

            def turn_x(i):
                act.wait_ge(xt_done, i + 1)
                act.activation(xTh[:], tiles(XT[:]), ACT.Copy).then_inc(xt_hi, 1)

            def turn_h(i):
                act.wait_ge(ht_done, i + 1)
                act.activation(hTh[:], tiles(HT[:]), ACT.Copy).then_inc(ht_hi, 1)

            def turn(i, p, more):
                if p is not None:
                    for j in DN:
                        split(p, j)
                if more:
                    split(i + 1, GU[0])
                    split(i + 1, GU[1])
                if p is not None:
                    turn_h(p)
                if more:
                    split(i + 1, GU[2])
                act.wait_ge(used[GU[-1]], i + 1)
                if p is not None:
                    act.wait_ge(hs_done, i)
                act.activation(sg[:], G, ACT.Silu).then_inc(sg_done, 1)
                if more:
                    split(i + 1, GU[3])
                    turn_x(i + 1)

            turn_x(0)
            last = turns(act, turn)
            for j in DN:
                split(last, j)
            turn_h(last)

        @block.tensor
        def _(pe):
            def turn_x(i):
                pe.wait_ge(xg_in, 16 * (i + 1))
                xs = xg[:].rearrange("p (m k) -> p k m", k=KD)
                for k in range(KD):
                    mm = pe.transpose(XT[:, k * P:(k + 1) * P], xs[:, k, :], ident[:])
                mm.then_inc(xt_done, 1)

            def turn_h(i):
                pe.wait_ge(hs_done, i + 1)
                hk = hs[:].rearrange("p (m k) -> p k m", k=KF)
                for k in range(KF):
                    mm = pe.transpose(HT[:, k * P:(k + 1) * P], hk[:, k, :], ident[:])
                mm.then_inc(ht_done, 1)

            def down(i, more=0):
                pe.wait_ge(ht_lo, i + 1)
                if not is_first(i):
                    pe.wait_ge(y_done, i)
                for j in DN:
                    if j == DN[-1] and more:
                        turn_x(i + 2)
                    pe.wait_ge(lo[j], i + 1)
                    for k in (2 * (j - DN[0]), 2 * (j - DN[0]) + 1):
                        for half in range(2):
                            w = slice(k * D + 512 * half, k * D + 512 * half + 512)
                            mm = product(pe, Y[:, 512 * half:512 * half + 512], (hTh[:, k, :], hTl[:, k, :]),
                                         (Wh[:, DOWN, w], Wl[:, DOWN, w]), k == 0, k == KF - 1)
                    mm.then_inc(used[j], 1)

            def turn(i, p, more):
                pe.wait_ge(xt_lo, i + 1)
                if p is not None:
                    pe.wait_ge(hs_done, i)
                for j in GU:
                    pe.wait_ge(lo[j], i + 1)
                    for k in (2 * j, 2 * j + 1):
                        x = (xTh[:, k, :], xTl[:, k, :])
                        for out, m in ((G, GATE), (U, UP)):
                            cols = slice(k * DE, (k + 1) * DE)
                            mm = product(pe, out, x, (Wh[:, m, cols], Wl[:, m, cols]), k == 0, k == KD - 1)
                    mm.then_inc(used[j], 1)
                    if j == GU[1] and p is not None:
                        turn_h(p)
                if p is None:
                    turn_x(i + 1)
                else:
                    down(p, more)

            pe.wait_ge(const_in, 16)
            turn_x(0)
            last = turns(pe, turn)
            turn_h(last)
            down(last)

        @block.vector
        def _(dve):
            def split(i, j):
                if j not in BY_POOL:
                    X.split_lo(dve, i, j)

            def turn_x(i):
                dve.wait_ge(xt_hi, i + 1)
                dve.tensor_tensor(xTl[:], tiles(XT[:]), xTh[:].bitcast(F32), ALU.subtract).then_inc(xt_lo, 1)

            def turn_h(i):
                dve.wait_ge(ht_hi, i + 1)
                dve.tensor_tensor(hTl[:], tiles(HT[:]), hTh[:].bitcast(F32), ALU.subtract).then_inc(ht_lo, 1)

            def store(i):
                dve.wait_ge(used[DN[-1]], i + 1)
                if not is_first(i):
                    dve.wait_ge(y_out, 16 * i)
                dve.wait_ge(w_set, i + 1)
                dve.tensor_scalar(y[:], Y[:], w_y[:], None, ALU.mult).then_inc(y_done, 1)

            def turn(i, p, more):
                if p is not None:
                    for j in DN:
                        split(p, j)
                if more:
                    split(i + 1, GU[0])
                    split(i + 1, GU[1])
                if p is not None:
                    turn_h(p)
                if more:
                    split(i + 1, GU[2])
                if p is not None:
                    dve.wait_ge(ht_done, i)
                dve.wait_ge(sg_done, i + 1)
                dve.tensor_tensor(hs[:], U, sg[:], ALU.mult).then_inc(hs_done, 1)
                if more:
                    split(i + 1, GU[3])
                    turn_x(i + 1)
                if p is not None:
                    store(p)

            turn_x(0)
            last = turns(dve, turn)
            for j in DN:
                split(last, j)
            turn_h(last)
            store(last)


def constants():
    n = np.arange(P, dtype=np.float64)[:, None]
    gamma = 1.0 - np.exp2(-5.0 - np.arange(BH, dtype=np.float64))
    half = HD // 2
    return {
        "ident": np.eye(P, dtype=np.float32),
        "tri": (np.arange(P)[:, None] <= np.arange(P)[None, :]).astype(np.float32),
        "decay": np.concatenate([gamma ** n, gamma ** -n * HD ** -0.5], axis=1).astype(np.float32),
        "decay_tile": np.repeat((gamma ** P).reshape(BH // 2, 2).T, HD, axis=0).astype(np.float32),
        "before": (np.arange(P)[:, None] < np.arange(P)[None, :]).astype(np.float32),
        "token": np.arange(SEQ, dtype=np.int32).reshape(NT, P).T,
        "route_tab": np.concatenate([np.arange(NE) // EG, np.arange(NE), CAP * np.arange(1, LEVELS), np.arange(FULL)]).astype(np.float32),
        "inv_freq": (np.float32(10000.0) ** (-np.arange(half, dtype=np.float32) / np.float32(half))).astype(np.float32),
    }




SCRATCH = {
    "ext_dram": ((AH, EXT), F32),
    "mix": ((SEQ, D), F32),
    "hn": ((SEQ, D), F32),
    "row": ((P * PLACES, 2), I32),
}


def build(nc, d):
    with ExitStack() as ctx:
        c = Core(nc, ctx)
        c.bank2 = [c.psum(f"pair{i}", 2) for i in range(3)]
        c.bank = [c.psum(f"bank{i}") for i in range(2)]
        phase_a(c, d)
        c.reuse_sems()
        raw = sbuf(nc, ctx, "weights_raw", [P, 3, KD * DE])
        phase_bc(c, d, raw)
        c.reuse_sems()
        experts = Experts(c, d, raw)
        counts, routed = sbuf(nc, ctx, "expert_counts", [P, NE]), c.sem("routed")
        ptab = sbuf(nc, ctx, "block_place", [P, BLOCKS], I32)
        btab = sbuf(nc, ctx, "block_expert", [P, BLOCKS + 1], I32)
        ids = sbuf(nc, ctx, "row_ids", [P, PLACES, 2], I32)
        phase_o(c, d, counts, routed, experts)
        experts.place_parts(sbuf(nc, ctx, "expert_h", [P, 3, KD * DE], F32R),
                            sbuf(nc, ctx, "expert_l", [P, 3, KD * DE], F32R))
        phase_r(c, d, counts, routed, btab, ptab, ids, experts)
        phase_e(c, d, btab, ptab, ids, experts)


def kernel(**inputs):
    import numpy as _np
    import concourse.bacc as _bacc
    from concourse.bass_utils import run_bass_kernel_spmd as _run

    arrays = {name: _np.asarray(a) for name, a in inputs.items()}
    arrays["x"], arrays["mem"] = arrays["x"][0], arrays["mem"][0]
    arrays["positions"] = arrays["positions"][0].reshape(NT, P).T
    arrays.update(constants())
    arrays = {name + "_dram": _np.ascontiguousarray(a) for name, a in arrays.items()}
    nc = _bacc.Bacc("TRN2", target_bir_lowering=False, num_devices=1)
    args = {name[:-5]: nc.dram_tensor(name, a.shape, mybir.dt.from_np(a.dtype), kind="ExternalInput").ap()
            for name, a in arrays.items()}
    args["out"] = nc.dram_tensor("out_dram", (SEQ, D), F32, kind="ExternalOutput").ap()
    for name, (shape, dt) in SCRATCH.items():
        args[name] = nc.dram_tensor(name + "_dram", shape, dt, kind="Internal").ap()
    build(nc, args)
    return _run(nc, [arrays], core_ids=[0]).results[0]["out_dram"][None]
```
